# Optimizing a Trainium2 kernel written in Bass

```python
import math
import jax, jax.numpy as jnp
from jax import lax
import numpy as np

D_MODEL = 1024
BATCH = 1
SEQ = 2048
DEPTH = 1

CHUNK = 64
RMS_EPS = 1e-6
S5_WIDTH = D_MODEL // 2
S5_GROUP = 16
S5_GROUPS = S5_WIDTH // S5_GROUP
S5_STATE = 64
S5_DT_MIN = 1e-3
S5_DT_MAX = 1e-1
LRU_WIDTH = D_MODEL
LRU_HEADS = 16
LRU_HEAD_DIM = LRU_WIDTH // LRU_HEADS
CONV_WIDTH = 4
LRU_C = 8.0
LRU_A_MIN = 0.9
LRU_A_MAX = 0.999
IN_WIDTH = S5_WIDTH + 2 * LRU_WIDTH + 2 * D_MODEL
N_GROUPS = 4
EXPERTS_PER_GROUP = 8
N_EXPERTS = N_GROUPS * EXPERTS_PER_GROUP
TOP_K = 2
D_EXPERT = D_MODEL // 2
MOE_BLOCK = 128

kernel_name = "hybrid_s5_rglru_hmoe_block"

def rms_norm(x, g):
    xf = x.astype(jnp.float32)
    y = xf * lax.rsqrt(jnp.mean(xf * xf, axis=-1, keepdims=True) + RMS_EPS)
    return (y * g.astype(jnp.float32)).astype(x.dtype)

def _linear_combine(left, right):
    a_l, b_l = left
    a_r, b_r = right
    return a_r * a_l, a_r * b_l + b_r

def s5_mixer(u, lam_re, lam_im, log_dt, b_re, b_im, c_re, c_im, d_skip):
    bsz, seq, _ = u.shape
    uf = u.astype(jnp.float32).reshape(bsz, seq, S5_GROUPS, S5_GROUP)
    lam = lax.complex(lam_re.astype(jnp.float32), lam_im.astype(jnp.float32))
    dt = jnp.exp(log_dt.astype(jnp.float32))[:, None]
    lam_bar = jnp.exp(lam * dt)
    bmat = lax.complex(b_re.astype(jnp.float32), b_im.astype(jnp.float32))
    b_bar = ((lam_bar - 1.0) / lam)[..., None] * bmat
    bu = jnp.einsum('gpc,blgc->blgp', b_bar, uf.astype(jnp.complex64))
    a = jnp.broadcast_to(lam_bar, (1, seq, S5_GROUPS, S5_STATE))
    _, s = lax.associative_scan(_linear_combine, (a, bu), axis=1)
    cmat = lax.complex(c_re.astype(jnp.float32), c_im.astype(jnp.float32))
    y = jnp.real(jnp.einsum('gcp,blgp->blgc', cmat, s))
    y = y + d_skip.astype(jnp.float32).reshape(S5_GROUPS, S5_GROUP) * uf
    return y.reshape(bsz, seq, S5_WIDTH)

def rglru_mixer(x, conv_w, conv_b, w_r, b_r, w_i, b_i, lam):
    bsz, seq, width = x.shape
    xp = jnp.pad(x, ((0, 0), (CONV_WIDTH - 1, 0), (0, 0)))
    xc = conv_b + sum(xp[:, k:k + seq] * conv_w[k] for k in range(CONV_WIDTH))
    xh = xc.reshape(bsz, seq, LRU_HEADS, LRU_HEAD_DIM)
    r = jax.nn.sigmoid(jnp.einsum('blhi,hij->blhj', xh, w_r).reshape(bsz, seq, width) + b_r)
    i = jax.nn.sigmoid(jnp.einsum('blhi,hij->blhj', xh, w_i).reshape(bsz, seq, width) + b_i)
    log_a = -LRU_C * r.astype(jnp.float32) * jax.nn.softplus(-lam.astype(jnp.float32))
    a = jnp.exp(log_a)
    mult = jnp.sqrt(-jnp.expm1(2.0 * log_a))
    bx = mult * (i * xc).astype(jnp.float32)
    _, h = lax.associative_scan(_linear_combine, (a, bx), axis=1)
    return h.astype(x.dtype)

def hierarchical_moe(h, w_rg, b_rg, w_re, b_re, w_gate, w_up, w_down):
    bsz, seq, d = h.shape
    n_tok = bsz * seq
    hf = h.reshape(n_tok, d)
    g_prob = jax.nn.softmax((hf @ w_rg).astype(jnp.float32) + b_rg.astype(jnp.float32), axis=-1)
    g_idx = jnp.argmax(g_prob, axis=-1).astype(jnp.int32)
    p_g = jnp.max(g_prob, axis=-1, keepdims=True)
    e_logits = ((hf @ w_re).astype(jnp.float32) + b_re.astype(jnp.float32)).reshape(n_tok, N_GROUPS, EXPERTS_PER_GROUP)
    e_logits = jnp.take_along_axis(e_logits, g_idx[:, None, None], axis=1)[:, 0]
    e_prob = jax.nn.softmax(e_logits, axis=-1)
    top_p, top_i = lax.top_k(e_prob, TOP_K)
    gate = p_g * (top_p / jnp.sum(top_p, axis=-1, keepdims=True))
    expert_id = g_idx[:, None] * EXPERTS_PER_GROUP + top_i.astype(jnp.int32)

    n_assign = n_tok * TOP_K
    flat_e = expert_id.reshape(n_assign)
    flat_tok = jnp.repeat(jnp.arange(n_tok, dtype=jnp.int32), TOP_K)
    flat_w = gate.reshape(n_assign)
    order = jnp.argsort(flat_e)
    sorted_e = flat_e[order]
    counts = jnp.bincount(flat_e, length=N_EXPERTS)
    starts = jnp.cumsum(counts) - counts
    padded = ((counts + MOE_BLOCK - 1) // MOE_BLOCK) * MOE_BLOCK
    pad_ends = jnp.cumsum(padded)
    pad_starts = pad_ends - padded
    dest = pad_starts[sorted_e] + (jnp.arange(n_assign, dtype=jnp.int32) - starts[sorted_e])
    n_blocks = -(-n_assign // MOE_BLOCK) + N_EXPERTS
    slot_tok = jnp.full((n_blocks * MOE_BLOCK,), n_tok, jnp.int32).at[dest].set(flat_tok[order])
    slot_w = jnp.zeros((n_blocks * MOE_BLOCK,), jnp.float32).at[dest].set(flat_w[order])
    block_e = jnp.minimum(jnp.searchsorted(pad_ends, jnp.arange(n_blocks, dtype=jnp.int32) * MOE_BLOCK, side='right'), N_EXPERTS - 1)
    h_pad = jnp.concatenate([hf, jnp.zeros((1, d), hf.dtype)], axis=0)

    def expert_block(args):
        tok, wt, e = args
        xb = h_pad[tok]
        y = (jax.nn.silu(xb @ w_gate[e]) * (xb @ w_up[e])) @ w_down[e]
        return y * wt[:, None].astype(y.dtype)

    y = lax.map(expert_block, (slot_tok.reshape(n_blocks, MOE_BLOCK), slot_w.reshape(n_blocks, MOE_BLOCK), block_e))
    out = jnp.zeros((n_tok + 1, d), h.dtype).at[slot_tok].add(y.reshape(-1, d).astype(h.dtype))[:n_tok]
    return out.reshape(bsz, seq, d)

def setup_inputs(seed: int = 0) -> dict:
    key = jax.random.key(seed)
    ks = jax.random.split(key, 32)
    f32 = jnp.float32
    nrm = lambda k, shape, scale: jax.random.normal(k, shape, f32) * scale
    x = jax.random.normal(ks[0], (BATCH, SEQ, D_MODEL), f32)
    norm_mix = 1.0 + nrm(ks[1], (DEPTH, D_MODEL), 0.02)
    w_in = nrm(ks[2], (DEPTH, D_MODEL, IN_WIDTH), D_MODEL ** -0.5)
    s5_lam_re = -0.5 + nrm(ks[3], (DEPTH, S5_GROUPS, S5_STATE), 0.01)
    s5_lam_im = math.pi * jnp.arange(S5_STATE, dtype=f32) + nrm(ks[4], (DEPTH, S5_GROUPS, S5_STATE), 0.01)
    s5_log_dt = jax.random.uniform(ks[5], (DEPTH, S5_GROUPS), f32, math.log(S5_DT_MIN), math.log(S5_DT_MAX))
    s5_b_re = nrm(ks[6], (DEPTH, S5_GROUPS, S5_STATE, S5_GROUP), (2.0 * S5_GROUP) ** -0.5)
    s5_b_im = nrm(ks[7], (DEPTH, S5_GROUPS, S5_STATE, S5_GROUP), (2.0 * S5_GROUP) ** -0.5)
    s5_c_re = nrm(ks[8], (DEPTH, S5_GROUPS, S5_GROUP, S5_STATE), (2.0 * S5_STATE) ** -0.5)
    s5_c_im = nrm(ks[9], (DEPTH, S5_GROUPS, S5_GROUP, S5_STATE), (2.0 * S5_STATE) ** -0.5)
    s5_d = nrm(ks[10], (DEPTH, S5_WIDTH), 1.0)
    w_s5_out = nrm(ks[11], (DEPTH, S5_WIDTH, 2 * D_MODEL), S5_WIDTH ** -0.5)
    conv_w = nrm(ks[12], (DEPTH, CONV_WIDTH, LRU_WIDTH), CONV_WIDTH ** -0.5)
    conv_b = nrm(ks[13], (DEPTH, LRU_WIDTH), 0.01)
    lru_w_r = nrm(ks[14], (DEPTH, LRU_HEADS, LRU_HEAD_DIM, LRU_HEAD_DIM), LRU_HEAD_DIM ** -0.5)
    lru_b_r = nrm(ks[15], (DEPTH, LRU_WIDTH), 0.01)
    lru_w_i = nrm(ks[16], (DEPTH, LRU_HEADS, LRU_HEAD_DIM, LRU_HEAD_DIM), LRU_HEAD_DIM ** -0.5)
    lru_b_i = nrm(ks[17], (DEPTH, LRU_WIDTH), 0.01)
    a_c = jax.random.uniform(ks[18], (DEPTH, LRU_WIDTH), f32, LRU_A_MIN, LRU_A_MAX)
    a0 = a_c ** (1.0 / LRU_C)
    lru_lambda = jnp.log(a0) - jnp.log1p(-a0)
    w_lru_out = nrm(ks[19], (DEPTH, LRU_WIDTH, D_MODEL), LRU_WIDTH ** -0.5)
    w_o = nrm(ks[20], (DEPTH, D_MODEL, D_MODEL), D_MODEL ** -0.5)
    norm_ffn = 1.0 + nrm(ks[21], (DEPTH, D_MODEL), 0.02)
    router_group_w = nrm(ks[22], (DEPTH, D_MODEL, N_GROUPS), D_MODEL ** -0.5)
    router_group_b = nrm(ks[23], (DEPTH, N_GROUPS), 0.01)
    router_expert_w = nrm(ks[24], (DEPTH, D_MODEL, N_EXPERTS), D_MODEL ** -0.5)
    router_expert_b = nrm(ks[25], (DEPTH, N_EXPERTS), 0.01)
    expert_w_gate = nrm(ks[26], (DEPTH, N_EXPERTS, D_MODEL, D_EXPERT), D_MODEL ** -0.5)
    expert_w_up = nrm(ks[27], (DEPTH, N_EXPERTS, D_MODEL, D_EXPERT), D_MODEL ** -0.5)
    expert_w_down = nrm(ks[28], (DEPTH, N_EXPERTS, D_EXPERT, D_MODEL), D_EXPERT ** -0.5)
    norm_final = 1.0 + nrm(ks[29], (D_MODEL,), 0.02)
    return {"x": x, "norm_mix": norm_mix, "w_in": w_in,
            "s5_lam_re": s5_lam_re, "s5_lam_im": s5_lam_im, "s5_log_dt": s5_log_dt,
            "s5_b_re": s5_b_re, "s5_b_im": s5_b_im, "s5_c_re": s5_c_re, "s5_c_im": s5_c_im,
            "s5_d": s5_d, "w_s5_out": w_s5_out,
            "conv_w": conv_w, "conv_b": conv_b, "lru_w_r": lru_w_r, "lru_b_r": lru_b_r,
            "lru_w_i": lru_w_i, "lru_b_i": lru_b_i, "lru_lambda": lru_lambda, "w_lru_out": w_lru_out,
            "w_o": w_o, "norm_ffn": norm_ffn,
            "router_group_w": router_group_w, "router_group_b": router_group_b,
            "router_expert_w": router_expert_w, "router_expert_b": router_expert_b,
            "expert_w_gate": expert_w_gate, "expert_w_up": expert_w_up, "expert_w_down": expert_w_down,
            "norm_final": norm_final}

def reference(x, norm_mix, w_in, s5_lam_re, s5_lam_im, s5_log_dt, s5_b_re, s5_b_im, s5_c_re, s5_c_im,
              s5_d, w_s5_out, conv_w, conv_b, lru_w_r, lru_b_r, lru_w_i, lru_b_i, lru_lambda, w_lru_out,
              w_o, norm_ffn, router_group_w, router_group_b, router_expert_w, router_expert_b,
              expert_w_gate, expert_w_up, expert_w_down, norm_final):
    d = D_MODEL
    for l in range(DEPTH):
        h = rms_norm(x, norm_mix[l])
        proj = h @ w_in[l]
        o1 = S5_WIDTH
        o2 = o1 + LRU_WIDTH
        o3 = o2 + LRU_WIDTH
        o4 = o3 + d
        u_s5 = proj[..., :o1]
        x_lru = proj[..., o1:o2]
        g_lru = proj[..., o2:o3]
        gate_a = jax.nn.sigmoid(proj[..., o3:o4])
        gate_b = jax.nn.sigmoid(proj[..., o4:])
        y_s5 = s5_mixer(u_s5, s5_lam_re[l], s5_lam_im[l], s5_log_dt[l], s5_b_re[l], s5_b_im[l],
                        s5_c_re[l], s5_c_im[l], s5_d[l]).astype(x.dtype)
        z = jax.nn.gelu(y_s5) @ w_s5_out[l]
        y_a = z[..., :d] * jax.nn.sigmoid(z[..., d:])
        y_lru = rglru_mixer(x_lru, conv_w[l], conv_b[l], lru_w_r[l], lru_b_r[l], lru_w_i[l], lru_b_i[l],
                            lru_lambda[l]) * jax.nn.gelu(g_lru)
        y_b = y_lru @ w_lru_out[l]
        x = x + (gate_a * y_a + gate_b * y_b) @ w_o[l]
        x = x + hierarchical_moe(rms_norm(x, norm_ffn[l]), router_group_w[l], router_group_b[l],
                                 router_expert_w[l], router_expert_b[l], expert_w_gate[l],
                                 expert_w_up[l], expert_w_down[l])
    return rms_norm(x, norm_final)


_drawn_inputs = setup_inputs


def setup_inputs(seed=0):
    import zlib

    import numpy as np

    out = dict(_drawn_inputs(seed))
    spreads = {}
    factors = {'norm_mix': 2.812,
     's5_lam_re': 64.0,
     's5_b_re': 2.801,
     's5_c_re': 2.711,
     's5_c_im': 2.762,
     'lru_b_r': 29.325,
     'lru_b_i': 27.47,
     'router_group_b': 28.656,
     'router_expert_b': 20.654,
     'norm_final': 8.617,
     's5_b_im': 3.736,
     'norm_ffn': 5.025}
    for name, (base, spread) in spreads.items():
        noise = np.random.default_rng([zlib.crc32(name.encode()), seed]).standard_normal(out[name].shape)
        drawn = base * np.exp(spread * noise) if base else spread * noise
        out[name] = __import__('jax').numpy.asarray(drawn.astype(out[name].dtype))
    for name, factor in factors.items():
        out[name] = (out[name] * factor).astype(out[name].dtype)
    return out
```

```python
import math
from contextlib import ExitStack

import concourse.bass as bass
from concourse import mybir

F32 = mybir.dt.float32
F32R = mybir.dt.float32r
I32 = mybir.dt.int32
U32 = mybir.dt.uint32
ALU = mybir.AluOpType
ACT = mybir.ActivationFunctionType
AX = mybir.AxisListType

P = 128
D_MODEL = 1024
SEQ = 2048
KT = D_MODEL // P
TOK_TILES = SEQ // P
RMS_EPS = 1e-6
S5_WIDTH = D_MODEL // 2
S5_GROUP = 16
S5_GROUPS = S5_WIDTH // S5_GROUP
S5_STATE = 64
PAIRS = S5_GROUPS // 2
STEP = P // S5_GROUP
CHUNKS = SEQ // STEP
CTS = CHUNKS // P
CBS = S5_WIDTH // P
CB_PAIRS = PAIRS // CBS
CB_GROUPS = S5_GROUPS // CBS
LRU_WIDTH = D_MODEL
LRU_HEAD_DIM = 64
LRU_BLOCKS = LRU_WIDTH // P
CONV_WIDTH = 4
LRU_C = 8.0
N_GROUPS = 4
EXPERTS_PER_GROUP = 8
N_EXPERTS = N_GROUPS * EXPERTS_PER_GROUP
D_EXPERT = D_MODEL // 2
QUARTER = 512
QUARTERS = SEQ // QUARTER
O_LRU = S5_WIDTH
O_GATE = O_LRU + LRU_WIDTH
O_GA = O_GATE + LRU_WIDTH
O_GB = O_GA + D_MODEL
MAX_TILES = 2 * SEQ // P + N_EXPERTS
W_SLOTS = 3

PACK_W = 0
PACK_C = PACK_W + CB_PAIRS * 2 * P
PACK_T = PACK_C + CB_PAIRS * 2 * 2 * P
PACK_TAB = PACK_T + CB_GROUPS * P
PACK_DECAY = PACK_TAB + 2 * CB_PAIRS * CHUNKS
PACK = PACK_DECAY + CB_PAIRS


class Chain:

    def __init__(self, eng, sem, base=0):
        self.eng, self.sem, self.base, self.n = eng, sem, base, 0

    def __call__(self, ins):
        self.n += 1
        ins.then_inc(self.sem, 1)
        self.eng.wait_ge(self.sem, self.base + self.n)


def matmul3(nc, out, l_hi, l_lo, r_hi, r_lo, start, stop):
    nc.tensor.matmul(out, l_hi, r_hi, start=start, stop=False)
    nc.tensor.matmul(out, l_hi, r_lo, start=False, stop=False)
    return nc.tensor.matmul(out, l_lo, r_hi, start=False, stop=stop)


def columns(v, count):
    return v.rearrange("(c p) -> p c", p=P)


def s5_constants(nc, d, ident):
    with ExitStack() as cx:
        sb = lambda n, s, t=F32: cx.enter_context(nc.sbuf_tensor("c0_" + n, s, t))
        sem = lambda n: cx.enter_context(nc.semaphore("c0_" + n))
        lam = sb("lam", [P, 2, PAIRS])
        ldt = sb("ldt", [P, PAIRS])
        decay = sb("decay", [P, PAIRS])
        braw = sb("braw", [P, 2, PAIRS, S5_GROUP])
        craw = sb("craw", [P, 2, CBS, 2, S5_STATE])
        cl = sb("cl", [P, 2, PAIRS, S5_GROUP])
        sc = sb("sc", [P, 16, PAIRS])
        bb = sb("bb", [P, 2, PAIRS, S5_GROUP])
        pf = sb("pf", [P, 2, STEP + 1, PAIRS])
        pr = sb("pr", [P, 2, STEP, PAIRS])
        v = sb("v", [P, 2, PAIRS, STEP, S5_GROUP])
        t1 = sb("t1", [P, PAIRS * STEP * S5_GROUP + PAIRS * S5_GROUP])
        t2 = sb("t2", [P, PAIRS * STEP * S5_GROUP + PAIRS * S5_GROUP])
        crx = sb("crx", [P, PAIRS, 2, 2, STEP + 1, S5_GROUP])
        w = sb("w", [P, PAIRS, 2, P])
        kt = sb("kt", [S5_GROUP, S5_GROUPS, STEP, S5_GROUP])
        tt = sb("tt", [P, S5_GROUPS, P])
        tab = sb("tab", [P, 2, PAIRS, CHUNKS])
        dcol = sb("dcol", [S5_GROUP, S5_GROUPS])
        dd = sb("dd", [S5_GROUP, S5_GROUPS, S5_GROUP])
        ps_c = cx.enter_context(nc.psum_tensor("c0_ps_c", [P, 2, 512], F32))
        ps_w = cx.enter_context(nc.psum_tensor("c0_ps_w", [P, 2, 512], F32))
        ps_k = cx.enter_context(nc.psum_tensor("c0_ps_k", [S5_GROUP, 2, 512], F32))
        loaded, exps, sins, ident_ready = sem("loaded"), sem("exps"), sem("sins"), sem("ident_ready")
        zeroed, args_ready, chain = sem("zeroed"), sem("args_ready"), sem("chain")
        c_turned, c_lanes, v_ready, w_turned, w_ready = (sem(n) for n in
            ("c_turned", "c_lanes", "v_ready", "w_turned", "w_ready"))
        k_rhs, k_made, k_ready, k_placed, stored, packed = (sem(n) for n in
            ("k_rhs", "k_made", "k_ready", "k_placed", "stored", "packed"))
        INPUTS = 16 * 11
        (DT, ZR, ZI, ER, CO, SI, RA, RB, MR, MI, WR, WI, X1, X2, X3, X4) = range(16)

        with nc.Block() as block:

            @block.sync
            def _(sp):
                with nc.allow_non_contiguous_dma(reason="small parameters, one word a lane"):
                    for j, name in enumerate(("s5_lam_re", "s5_lam_im")):
                        sp.dma_start(lam[:, j, :], d[name][0].rearrange("(q r) p -> (r p) q", r=2)).then_inc(loaded, 16)
                    for r in range(2):
                        sp.dma_start(ldt[64 * r:64 * r + 64, :],
                                     d["s5_log_dt"][0].rearrange("(q r) -> r q", r=2)[r:r + 1, :].to_broadcast([64, PAIRS])
                                     ).then_inc(loaded, 16)
                    for j, name in enumerate(("s5_b_re", "s5_b_im")):
                        sp.dma_start(braw[:, j, :, :], d[name][0].rearrange("(q r) p c -> (r p) q c", r=2)).then_inc(loaded, 16)
                    for j, name in enumerate(("s5_c_re", "s5_c_im")):
                        for dup in range(2):
                            sp.dma_start(craw[:, j, :, dup, :],
                                         d[name][0].rearrange("(b g) c p -> (g c) b p", b=CBS)).then_inc(loaded, 16)
                    sp.dma_start(dcol[:, :], d["s5_d"][0].rearrange("(g c) -> c g", c=S5_GROUP)).then_inc(loaded, 16)
                sp.wait_ge(k_ready, 1)
                sp.wait_ge(zeroed, 2)
                for s in range(STEP):
                    sp.dma_start(tt[s * S5_GROUP:(s + 1) * S5_GROUP, :, s * S5_GROUP:],
                                 kt[:, :, 0:STEP - s, :].rearrange("p g t c -> p g (t c)")).then_inc(k_placed, 16)
                sp.wait_ge(w_ready, 8)
                sp.wait_ge(k_placed, 16 * STEP)
                sp.wait_ge(packed, 1)
                for b in range(CBS):
                    dst = d["s5_pack"][b]
                    q = slice(b * CB_PAIRS, (b + 1) * CB_PAIRS)
                    sp.dma_start(dst[:, PACK_W:PACK_C], w[:, q, :, :].rearrange("p q j m -> p (q j m)")).then_inc(stored, 16)
                    sp.dma_start(dst[:, PACK_C:PACK_T].rearrange("p (k m) -> p k m", m=P),
                                 crx[:, q, :, :, 1:, :].rearrange("p q j r t c -> p (q j r) (t c)")).then_inc(stored, 16)
                    sp.dma_start(dst[:, PACK_T:PACK_TAB],
                                 tt[:, b * CB_GROUPS:(b + 1) * CB_GROUPS, :].rearrange("p g m -> p (g m)")).then_inc(stored, 16)
                    sp.dma_start(dst[:, PACK_TAB:PACK_DECAY].rearrange("p (j m) -> p j m", j=2),
                                 tab[:, :, q, :].rearrange("p j q m -> p j (q m)")).then_inc(stored, 16)
                    sp.dma_start(dst[:, PACK_DECAY:PACK], decay[:, q]).then_inc(stored, 16)
                sp.wait_ge(stored, 16 * 5 * CBS)

            @block.gpsimd
            def _(pool):
                nc.gpsimd.memset(ident[:, :], 0.0).then_inc(zeroed, 1)
                pool.wait_ge(zeroed, 1)
                nc.gpsimd.affine_select(out=ident[:, :], in_=ident[:, :], compare_op=ALU.not_equal, fill=1.0,
                                        base=0, pattern=[[-1, P]], channel_multiplier=1).then_inc(ident_ready, 1)
                nc.gpsimd.memset(tt[:, :, :], 0.0).then_inc(zeroed, 1)
                nc.gpsimd.memset(crx[:, :, :, :, :, :], 0.0).then_inc(zeroed, 1)

            @block.scalar
            def _(act):
                act.wait_ge(loaded, INPUTS - 32)
                act.wait_ge(loaded, INPUTS)
                nc.scalar.activation(sc[:, DT, :], ldt[:, :], ACT.Exp).then_inc(exps, 1)
                act.wait_ge(args_ready, 1)
                nc.scalar.activation(sc[:, ER, :], sc[:, ZR, :], ACT.Exp).then_inc(exps, 1)
                nc.scalar.activation(decay[:, :], sc[:, ZR, :], ACT.Exp, scale=float(STEP)).then_inc(exps, 1)
                nc.scalar.activation(sc[:, SI, :], sc[:, RA, :], ACT.Sin).then_inc(sins, 1)
                nc.scalar.activation(sc[:, CO, :], sc[:, RB, :], ACT.Sin).then_inc(sins, 1)
                act.wait_ge(c_turned, 1)
                for b in range(CBS):
                    for j in range(2):
                        src = ps_c[:, j, b * P:(b + 1) * P].rearrange("p (q r c) -> p q r c", r=2, c=S5_GROUP)
                        for r in range(2):
                            rows = slice(64 * r, 64 * r + 64)
                            nc.scalar.copy(cl[rows, j, b * CB_PAIRS:(b + 1) * CB_PAIRS, :], src[rows, :, r, :]).then_inc(c_lanes, 1)

            @block.tensor
            def _(pe):
                pe.wait_ge(ident_ready, 1)
                pe.wait_ge(loaded, INPUTS)
                for j in range(2):
                    for b in range(CBS):
                        last = nc.tensor.transpose(ps_c[:, j, b * P:(b + 1) * P],
                                                   craw[:, j, b, :, :].rearrange("p r s -> p (r s)"), ident[:, :])
                last.then_inc(c_turned, 1)
                pe.wait_ge(v_ready, 1)
                for i in range(PAIRS // 2):
                    if i >= 2:
                        pe.wait_ge(w_ready, i - 1)
                    for q in (2 * i, 2 * i + 1):
                        for j in range(2):
                            last = nc.tensor.transpose(ps_w[:, i % 2, ((q % 2) * 2 + j) * P:((q % 2) * 2 + j + 1) * P],
                                                       v[:, j, q, :, :].rearrange("p t c -> p (t c)"), ident[:, :])
                    last.then_inc(w_turned, 1)
                pe.wait_ge(k_rhs, 1)
                for i in range(PAIRS // 2):
                    if i >= 2:
                        pe.wait_ge(k_made, i - 1)
                    for q in (2 * i, 2 * i + 1):
                        for j in range(2):
                            last = nc.tensor.matmul(ps_k[:, i % 2, (q % 2) * 256:(q % 2) * 256 + 256], bb[:, j, q, :],
                                                    crx[:, q, j, :, 0:STEP, :],
                                                    start=(j == 0), stop=(j == 1))
                    last.then_inc(w_turned, 1)

            @block.vector
            def _(dve):
                step = Chain(dve, chain)
                tt_ = nc.vector.tensor_tensor
                ts_ = nc.vector.tensor_scalar

                def cmul(o_re, o_im, a_re, a_im, b_re, b_im, x, y):
                    step(tt_(x, a_re, b_re, ALU.mult))
                    step(tt_(y, a_im, b_im, ALU.mult))
                    step(tt_(o_re, x, y, ALU.subtract))
                    step(tt_(x, a_re, b_im, ALU.mult))
                    step(tt_(y, a_im, b_re, ALU.mult))
                    step(tt_(o_im, x, y, ALU.add))

                s = lambda i: sc[:, i, :]
                dve.wait_ge(loaded, INPUTS)
                dve.wait_ge(exps, 1)
                step(tt_(s(ZR), lam[:, 0, :], s(DT), ALU.mult))
                step(tt_(s(ZI), lam[:, 1, :], s(DT), ALU.mult))
                magic, inv = 1.5 * 2.0 ** 23, 1.0 / (2 * math.pi)
                c1, c2 = 6.28125, 0.0019350051879882812
                c3 = 2 * math.pi - c1 - c2
                for out, turn in ((RA, 0.0), (RB, 0.25)):
                    step(ts_(s(X1), s(ZI), inv, turn, ALU.mult, ALU.add))
                    step(ts_(s(X2), s(X1), magic, None, ALU.add))
                    step(ts_(s(X1), s(X2), magic, None, ALU.subtract))
                    for n, part in enumerate((c1, c2, c3)):
                        step(nc.vector.scalar_tensor_tensor(s(X2), s(X1), -part, s(ZI) if n == 0 else s(X2), ALU.mult, ALU.add))
                    step(ts_(s(X2), s(X2), turn * 2 * math.pi, 3.1415925, ALU.add, ALU.min))
                    step(ts_(s(out), s(X2), -3.1415925, None, ALU.max))
                nc.vector.tensor_copy(s(X3), s(ZI)).then_inc(args_ready, 1)
                dve.wait_ge(exps, 3)
                dve.wait_ge(sins, 2)
                step(nc.vector.memset(pf[:, 0, 0, :], 1.0))
                step(nc.vector.memset(pf[:, 1, 0, :], 0.0))
                step(tt_(pf[:, 0, 1, :], s(ER), s(CO), ALU.mult))
                step(tt_(pf[:, 1, 1, :], s(ER), s(SI), ALU.mult))
                for n in range(2, STEP + 1):
                    h, k = n // 2, n - n // 2
                    cmul(pf[:, 0, n, :], pf[:, 1, n, :], pf[:, 0, h, :], pf[:, 1, h, :], pf[:, 0, k, :], pf[:, 1, k, :], s(X1), s(X2))
                for n in range(STEP):
                    step(nc.vector.tensor_copy(pr[:, :, n, :], pf[:, :, STEP - 1 - n, :]))
                step(tt_(s(X1), lam[:, 0, :], lam[:, 0, :], ALU.mult))
                step(tt_(s(X2), lam[:, 1, :], lam[:, 1, :], ALU.mult))
                step(tt_(s(X3), s(X1), s(X2), ALU.add))
                step(nc.vector.reciprocal(s(X4), s(X3)))
                step(tt_(s(MR), lam[:, 0, :], s(X4), ALU.mult))
                step(tt_(s(X3), lam[:, 1, :], s(X4), ALU.mult))
                step(ts_(s(MI), s(X3), -1.0, None, ALU.mult))
                step(ts_(s(X4), pf[:, 0, 1, :], -1.0, None, ALU.add))
                cmul(s(WR), s(WI), s(X4), pf[:, 1, 1, :], s(MR), s(MI), s(X1), s(X2))
                wide = lambda a, shape: a.unsqueeze(len(shape) - 1).to_broadcast(shape)
                small = [P, PAIRS, S5_GROUP]
                x3 = t1[:, 0:PAIRS * S5_GROUP].rearrange("p (q c) -> p q c", q=PAIRS)
                y3 = t2[:, 0:PAIRS * S5_GROUP].rearrange("p (q c) -> p q c", q=PAIRS)
                cmul(bb[:, 0], bb[:, 1], wide(s(WR), small), wide(s(WI), small), braw[:, 0], braw[:, 1], x3, y3)
                big = [P, STEP, PAIRS, S5_GROUP]
                vt = lambda j: v[:, j].rearrange("p q t c -> p t q c")
                bw = lambda j: bb[:, j].unsqueeze(1).to_broadcast(big)
                x4 = t1[:, 0:PAIRS * P].rearrange("p (t q c) -> p t q c", t=STEP, q=PAIRS)
                y4 = t2[:, 0:PAIRS * P].rearrange("p (t q c) -> p t q c", t=STEP, q=PAIRS)
                cmul(vt(0), vt(1), wide(pr[:, 0], big), wide(pr[:, 1], big), bw(0), bw(1), x4, y4)
                nc.vector.tensor_copy(s(X1), s(X2)).then_inc(v_ready, 1)
                dve.wait_ge(c_lanes, 4 * CBS)
                dve.wait_ge(zeroed, 3)
                for r in range(2):
                    rows = slice(64 * r, 64 * r + 64)
                    shp = [64, STEP + 1, PAIRS, S5_GROUP]
                    x5 = t1[rows, :].rearrange("p (t q c) -> p t q c", t=STEP + 1, q=PAIRS)
                    y5 = t2[rows, :].rearrange("p (t q c) -> p t q c", t=STEP + 1, q=PAIRS)
                    o = lambda j: crx[rows, :, j, r].rearrange("p q t c -> p t q c")
                    pw = lambda j: pf[rows, j].unsqueeze(3).to_broadcast(shp)
                    cc = lambda j: cl[rows, j].unsqueeze(1).to_broadcast(shp)
                    step(tt_(x5, pw(0), cc(0), ALU.mult))
                    step(tt_(y5, pw(1), cc(1), ALU.mult))
                    step(tt_(o(0), x5, y5, ALU.subtract))
                    step(tt_(x5, pw(0), cc(1), ALU.mult))
                    step(tt_(y5, pw(1), cc(0), ALU.mult))
                    step(tt_(x5, x5, y5, ALU.add))
                    step(ts_(o(1), x5, -1.0, None, ALU.mult))
                nc.vector.tensor_copy(s(X1), s(X2)).then_inc(k_rhs, 1)
                for i in range(PAIRS // 2):
                    dve.wait_ge(w_turned, i + 1)
                    nc.vector.tensor_copy(w[:, 2 * i:2 * i + 2, :, :].rearrange("p q j m -> p (q j m)"), ps_w[:, i % 2, :]).then_inc(w_ready, 1)
                for i in range(PAIRS // 2):
                    dve.wait_ge(w_turned, PAIRS // 2 + i + 1)
                    nc.vector.tensor_copy(kt[:, 4 * i:4 * i + 4, :, :].rearrange("p g t c -> p (g t c)"),
                                          ps_k[:, i % 2, :]).then_inc(k_made, 1)
                dve.wait_ge(k_made, PAIRS // 2)
                dshape = [S5_GROUP, S5_GROUPS, S5_GROUP]
                step(tt_(dd[:, :, :], dcol[:, :].unsqueeze(2).to_broadcast(dshape),
                         ident[0:S5_GROUP, 0:S5_GROUP].unsqueeze(1).to_broadcast(dshape), ALU.mult))
                tt_(kt[:, :, 0, :], kt[:, :, 0, :], dd[:, :, :], ALU.add).then_inc(k_ready, 1)
                cmul(s(MR), s(MI), s(CO), s(SI), s(CO), s(SI), s(X1), s(X2))
                cmul(s(WR), s(WI), s(MR), s(MI), s(MR), s(MI), s(X1), s(X2))
                cmul(s(MR), s(MI), s(WR), s(WI), s(WR), s(WI), s(X1), s(X2))
                step(nc.vector.memset(tab[:, 0, :, 0:1], 1.0))
                step(nc.vector.memset(tab[:, 1, :, 0:1], 0.0))
                m = 1
                while m < CHUNKS:
                    shp = [P, PAIRS, m]
                    x6 = t1[:, 0:PAIRS * m].rearrange("p (q m) -> p q m", m=m)
                    y6 = t2[:, 0:PAIRS * m].rearrange("p (q m) -> p q m", m=m)
                    cmul(tab[:, 0, :, m:2 * m], tab[:, 1, :, m:2 * m], tab[:, 0, :, 0:m], tab[:, 1, :, 0:m],
                         wide(s(MR), shp), wide(s(MI), shp), x6, y6)
                    if 2 * m < CHUNKS:
                        cmul(s(WR), s(WI), s(MR), s(MI), s(MR), s(MI), s(X1), s(X2))
                        step(nc.vector.tensor_copy(s(MR), s(WR)))
                        step(nc.vector.tensor_copy(s(MI), s(WI)))
                    m *= 2
                nc.vector.tensor_copy(s(X1), s(X2)).then_inc(packed, 1)


def norm_and_turn(nc, d, ident, h_hi, h_lo):
    with ExitStack() as cx:
        sb = lambda n, s, t=F32: cx.enter_context(nc.sbuf_tensor("n1_" + n, s, t))
        sem = lambda n: cx.enter_context(nc.semaphore("n1_" + n))
        xin = sb("xin", [P, 2, D_MODEL])
        xn = sb("xn", [P, 2, D_MODEL])
        hs = sb("hs", [P, 2, KT, P])
        sq = sb("sq", [P, 2, D_MODEL])
        ss = sb("ss", [P, 2])
        ms = sb("ms", [P, 2])
        rs = sb("rs", [P, 2])
        gain = sb("gain", [P, KT])
        half = sb("half", [P, 2])
        pst = cx.enter_context(nc.psum_tensor("n1_pst", [P, 2, KT, P], F32))
        gain_in, squared, mean, rstd, normed, turned, gained, high, split = (sem(n) for n in
            ("gain_in", "squared", "mean", "rstd", "normed", "turned", "gained", "high", "split"))
        x_in = [sem("x_in0"), sem("x_in1")]
        last = TOK_TILES - 1
        with nc.Block() as block:

            @block.sync
            def _(sp):
                with nc.allow_non_contiguous_dma(reason="one gain a partition"):
                    sp.dma_start(gain[:, :], columns(d["norm_mix"][0], KT)).then_inc(gain_in, 16)
                with sp.Fori(0, TOK_TILES // 2) as i:
                    for b in range(2):
                        sp.wait_ge(normed, 2 * i + b + 1)
                        sp.dma_start(xin[:, b, :], d["x"][0, bass.ds((2 * i + b) * P, P), :]).then_inc(x_in[b], 16)

            @block.scalar
            def _(act):
                act.sem_inc(high, 2)

                def square(t, b, turn):
                    act.wait_ge(x_in[b], 16 * (turn + 1))
                    act.wait_ge(rstd, t + 1)
                    nc.scalar.activation(sq[:, b, :], xin[:, b, :], ACT.Square, accum_out=ss[:, b:b + 1]).then_inc(squared, 1)

                def take_high(t, b):
                    act.wait_ge(gained, t + 3)
                    nc.scalar.copy(h_hi[:, :, bass.ds(t * P, P)], hs[:, b, :, :]).then_inc(high, 1)

                square(0, 0, 0)
                with act.Fori(0, TOK_TILES // 2 - 1) as i:
                    for b in range(2):
                        square(2 * i + b + 1, 1 - b, i + b)
                        take_high(2 * i + b, b)
                square(last, 1, TOK_TILES // 2 - 1)
                take_high(last - 1, 0)
                take_high(last, 1)

            @block.gpsimd
            def _(pool):
                pool.sem_inc(rstd, 2)
                nc.gpsimd.memset(half[:, 0:1], -0.5).then_inc(mean, 1)
                nc.gpsimd.memset(half[:, 1:2], RMS_EPS * D_MODEL).then_inc(mean, 1)
                pool.wait_ge(mean, 2)
                with pool.Fori(0, TOK_TILES // 2) as i:
                    for b in range(2):
                        t = 2 * i + b
                        pool.wait_ge(squared, t + 1)
                        nc.gpsimd.tensor_tensor(ms[:, b:b + 1], ss[:, b:b + 1], half[:, 1:2], ALU.add).then_inc(mean, 1)
                        pool.wait_ge(mean, t + 3)
                        pool.wait_ge(normed, t + 1)
                        nc.gpsimd.tensor_tensor(rs[:, b:b + 1], ms[:, b:b + 1], half[:, 0:1], ALU.pow).then_inc(rstd, 1)

            @block.tensor
            def _(pe):
                pe.sem_inc(turned, 2)
                with pe.Fori(0, TOK_TILES // 2) as i:
                    for b in range(2):
                        t = 2 * i + b
                        pe.wait_ge(normed, t + 3)
                        pe.wait_ge(gained, t + 1)
                        for k in range(KT):
                            done = nc.tensor.transpose(pst[:, b, k, :], xn[:, b, k * P:(k + 1) * P], ident[:, :])
                        done.then_inc(turned, 1)

            @block.vector
            def _(dve):
                dve.sem_inc(normed, 2)
                dve.sem_inc(gained, 2)
                dve.wait_ge(gain_in, 16)

                def norm(t, b):
                    dve.wait_ge(rstd, t + 3)
                    dve.wait_ge(turned, t + 1)
                    nc.vector.tensor_scalar(xn[:, b, :], xin[:, b, :], rs[:, b:b + 1], math.sqrt(D_MODEL), ALU.mult, ALU.mult).then_inc(normed, 1)

                def gain_and_split(t, b):
                    dve.wait_ge(turned, t + 3)
                    dve.wait_ge(high, t + 1)
                    nc.vector.tensor_tensor(hs[:, b, :, :], pst[:, b, :, :],
                                            gain[:, :].unsqueeze(2).to_broadcast([P, KT, P]), ALU.mult).then_inc(gained, 1)
                    dve.wait_ge(high, t + 3)
                    nc.vector.tensor_tensor(h_lo[:, :, bass.ds(t * P, P)], hs[:, b, :, :],
                                            h_hi[:, :, bass.ds(t * P, P)].bitcast(F32), ALU.subtract).then_inc(split, 1)

                norm(0, 0)
                with dve.Fori(0, TOK_TILES // 2 - 1) as i:
                    for b in range(2):
                        norm(2 * i + b + 1, 1 - b)
                        gain_and_split(2 * i + b, b)
                norm(last, 1)
                gain_and_split(last - 1, 0)
                gain_and_split(last, 1)


def s5_inputs(nc, d, h_hi, h_lo):
    with ExitStack() as cx:
        sb = lambda n, s, t=F32: cx.enter_context(nc.sbuf_tensor("u2_" + n, s, t))
        sem = lambda n: cx.enter_context(nc.semaphore("u2_" + n))
        raw = sb("raw", [P, 2, S5_WIDTH])
        w_hi = sb("w_hi", [P, KT, S5_WIDTH], F32R)
        w_lo = sb("w_lo", [P, KT, S5_WIDTH], F32R)
        u = sb("u", [P, CTS, S5_GROUPS, STEP, S5_GROUP])
        ps = cx.enter_context(nc.psum_tensor("u2_ps", [P, 4, S5_WIDTH], F32))
        w_split, made, taken, stored, high, h_sent = (sem(n) for n in ("w_split", "made", "taken", "stored", "high", "h_sent"))
        w_in = [sem("w_in0"), sem("w_in1")]
        hv = [h[:, :, :].rearrange("p k (a m t) -> p k a t m", a=CTS, t=STEP) for h in (h_hi, h_lo)]
        with nc.Block() as block:

            @block.sync
            def _(sp):
                for k in range(KT):
                    if k >= 2:
                        sp.wait_ge(w_split, k - 1)
                    sp.dma_start(raw[:, k % 2, :], d["w_in"][0, k * P:(k + 1) * P, 0:S5_WIDTH]).then_inc(w_in[k % 2], 16)
                for a, h in ((0, h_hi), (1, h_lo)):
                    for k in range(KT):
                        sp.dma_start(d["h_t"][a, k * P:(k + 1) * P, :], h[:, k, :].bitcast(F32)).then_inc(h_sent, 16)
                for a in range(CTS):
                    sp.wait_ge(taken, STEP * (a + 1))
                    for b in range(CBS):
                        sp.dma_start(d["u"][b, :, a, :], u[:, a, b * CB_GROUPS:(b + 1) * CB_GROUPS, :, :].rearrange("p g t c -> p (g t c)")
                                     ).then_inc(stored, 16)
                sp.wait_ge(stored, 16 * CTS * CBS)
                sp.wait_ge(h_sent, 16 * 2 * KT)

            @block.vector
            def _(dve):
                for k in range(KT):
                    dve.wait_ge(w_in[k % 2], 16 * (k // 2 + 1))
                    nc.vector.tensor_copy(w_hi[:, k, :], raw[:, k % 2, :]).then_inc(high, 1)
                    dve.wait_ge(high, k + 1)
                    nc.vector.tensor_tensor(w_lo[:, k, :], raw[:, k % 2, :], w_hi[:, k, :].bitcast(F32), ALU.subtract).then_inc(w_split, 1)

            @block.tensor
            def _(pe):
                n = 0
                for a in range(CTS):
                    for t in range(STEP):
                        if n >= 4:
                            pe.wait_ge(taken, n - 3)
                        for k in range(KT):
                            if n == 0:
                                pe.wait_ge(w_split, k + 1)
                            last = matmul3(nc, ps[:, n % 4, :], hv[0][:, k, a, t, :], hv[1][:, k, a, t, :],
                                           w_hi[:, k, :], w_lo[:, k, :], k == 0, k == KT - 1)
                        last.then_inc(made, 1)
                        n += 1

            @block.scalar
            def _(act):
                for n in range(CTS * STEP):
                    act.wait_ge(made, n + 1)
                    nc.scalar.copy(u[:, n // STEP, :, n % STEP, :], ps[:, n % 4, :].rearrange("p (g c) -> p g c", c=S5_GROUP)).then_inc(taken, 1)


def s5_scan(nc, d, ident):
    with ExitStack() as cx:
        sb = lambda n, s, t=F32: cx.enter_context(nc.sbuf_tensor("s3_" + n, s, t))
        sem = lambda n: cx.enter_context(nc.semaphore("s3_" + n))
        pack = sb("pack", [P, PACK])
        uy = sb("uy", [P, CTS, CB_GROUPS * P])
        ut = sb("ut", [P, CB_GROUPS, CHUNKS])
        state = sb("state", [P, 2, CB_PAIRS, CHUNKS])
        scanned = sb("scanned", [P, 2, CB_PAIRS, CHUNKS])
        t1 = sb("t1", [P, CB_PAIRS, CHUNKS])
        t2 = sb("t2", [P, CB_PAIRS, CHUNKS])
        out_hi = sb("out_hi", [P, P, STEP], F32R)
        out_lo = sb("out_lo", [P, P, STEP], F32R)
        ps_t = cx.enter_context(nc.psum_tensor("s3_ps_t", [P, 2, 4, P], F32))
        ps_x = cx.enter_context(nc.psum_tensor("s3_ps_x", [P, CB_PAIRS, 2, CHUNKS], F32))
        ps_y = cx.enter_context(nc.psum_tensor("s3_ps_y", [P, 2, 512], F32))
        (loaded, turned, ut_ready, x_made, dve_steps, y_made, y_ready, high, low, sent) = (sem(n) for n in
            ("loaded", "turned", "ut_ready", "x_made", "dve_steps", "y_made", "y_ready", "high", "low", "sent"))
        w = pack[:, PACK_W:PACK_C].rearrange("p (q j m) -> p q j m", q=CB_PAIRS, j=2)
        cm = pack[:, PACK_C:PACK_T].rearrange("p (q j m) -> p q j m", q=CB_PAIRS, j=2)
        tm = pack[:, PACK_T:PACK_TAB].rearrange("p (g m) -> p g m", g=CB_GROUPS)
        tab = pack[:, PACK_TAB:PACK_DECAY].rearrange("p (j q m) -> p j q m", j=2, q=CB_PAIRS)
        decay = pack[:, PACK_DECAY:PACK]
        DVE_STEPS = 6 + 2 * CB_PAIRS + 6
        with nc.Block() as block:

            @block.sync
            def _(sp):
                sp.sem_inc(sent, 32)
                with sp.Fori(0, CBS) as i:
                    sp.wait_ge(low, 4 * i + 4)
                    sp.dma_start(pack[:, :], d["s5_pack"][bass.ds(i, 1), :, :].rearrange("a p n -> (a p) n")).then_inc(loaded, 16)
                    sp.dma_start(uy[:, :, :], d["u"][bass.ds(i, 1), :, :, :].rearrange("a p t n -> (a p) t n")).then_inc(loaded, 16)
                    for a in range(CTS):
                        sp.wait_ge(low, 4 * i + 2 * a + 6)
                        for j, o in enumerate((out_hi, out_lo)):
                            sp.dma_start(d["ys_t"][j, bass.ds(i * P, P), a * P * STEP:(a + 1) * P * STEP],
                                         o[:, :, :].rearrange("p m t -> p (m t)").bitcast(F32)).then_inc(sent, 16)
                sp.wait_ge(sent, 32 + 64 * CBS)

            @block.tensor
            def _(pe):
                with pe.Fori(0, CBS) as i:
                    pe.wait_ge(loaded, 32 * (i + 1))
                    for j in range(4):
                        if j >= 2:
                            pe.wait_ge(ut_ready, 4 * i + j - 1)
                        for g in range(2):
                            for a in range(CTS):
                                last = nc.tensor.transpose(ps_t[:, j % 2, 2 * g + a, :],
                                                           uy[:, a, (2 * j + g) * P:(2 * j + g + 1) * P], ident[:, :])
                        last.then_inc(turned, 1)
                    for q in range(CB_PAIRS):
                        pe.wait_ge(ut_ready, 4 * i + q + 1)
                        for j in range(2):
                            for r in range(2):
                                last = nc.tensor.matmul(ps_x[64 * r:64 * r + 64, q, j, :], w[:, q, j, 64 * r:64 * r + 64],
                                                        ut[:, 2 * q + r, :], start=True, stop=True)
                    last.then_inc(x_made, 1)
                    pe.wait_ge(dve_steps, DVE_STEPS * (i + 1) + 2)
                    for a in range(CTS):
                        for h in range(2):
                            n = 2 * a + h
                            if n >= 2:
                                pe.wait_ge(y_ready, 4 * i + n - 1)
                            for q in (2 * h, 2 * h + 1):
                                o = ps_y[:, h, (q % 2) * 256:(q % 2) * 256 + 256]
                                for j in range(2):
                                    nc.tensor.matmul(o, state[:, j, q, a * P:(a + 1) * P], cm[:, q, j, :], start=(j == 0), stop=False)
                                for r in range(2):
                                    last = nc.tensor.matmul(o[:, r * P:(r + 1) * P], ut[:, 2 * q + r, a * P:(a + 1) * P],
                                                            tm[:, 2 * q + r, :], start=False, stop=(r == 1))
                            last.then_inc(y_made, 1)
                    for a in range(CTS):
                        pe.wait_ge(y_ready, 4 * i + 2 * a + 2)
                        for h in range(2):
                            n = 2 * a + h
                            if n >= 2:
                                pe.wait_ge(low, 4 * i + n + 3)
                            for t in range(4):
                                last = nc.tensor.transpose(ps_t[:, n % 2, t, :],
                                                           uy[:, a, (4 * h + t) * P:(4 * h + t + 1) * P],
                                                           ident[:, :])
                            last.then_inc(turned, 1)

            @block.scalar
            def _(act):
                with act.Fori(0, CBS) as i:
                    for j in range(4):
                        act.wait_ge(turned, 8 * i + j + 1)
                        nc.scalar.copy(ut[:, 2 * j:2 * j + 2, :], ps_t[:, j % 2, :, :].rearrange("p (g a) m -> p g (a m)", g=2)).then_inc(ut_ready, 1)
                    for a in range(CTS):
                        for h in range(2):
                            act.wait_ge(y_made, 4 * i + 2 * a + h + 1)
                            nc.scalar.activation(uy[:, a, :].rearrange("p (t g c) -> p g t c", t=STEP, g=CB_GROUPS)[:, 4 * h:4 * h + 4],
                                                 ps_y[:, h, :].rearrange("p (g t c) -> p g t c", g=4, t=STEP), ACT.Gelu_apprx_tanh).then_inc(y_ready, 1)
                    for a in range(CTS):
                        for h in range(2):
                            n = 2 * a + h
                            act.wait_ge(turned, 8 * i + 4 + n + 1)
                            if h == 0:
                                act.wait_ge(sent, 64 * i + 32 * a + 32)
                            nc.scalar.copy(out_hi[:, :, 4 * h:4 * h + 4].rearrange("p m t -> p t m"), ps_t[:, n % 2, :, :]).then_inc(high, 1)

            @block.vector
            def _(dve):
                tt_ = nc.vector.tensor_tensor
                dve.sem_inc(low, 4)
                first = Chain(dve, dve_steps)
                for j in range(2):
                    first(nc.vector.memset(scanned[:, j, :, 0:1], 0.0))
                with dve.Fori(0, CBS) as i:
                    step = Chain(dve, dve_steps, base=DVE_STEPS * i + 2)
                    dve.wait_ge(loaded, 32 * (i + 1))
                    dve.wait_ge(x_made, i + 1)
                    n1 = CHUNKS - 1
                    re, im = (ps_x[:, :, j, 0:n1] for j in range(2))
                    co, si = (tab[:, j, :, 1:CHUNKS] for j in range(2))
                    a, b = t1[:, :, 0:n1], t2[:, :, 0:n1]
                    step(tt_(a, co, re, ALU.mult))
                    step(tt_(b, si, im, ALU.mult))
                    step(tt_(state[:, 0, :, 1:], a, b, ALU.add))
                    step(tt_(a, co, im, ALU.mult))
                    step(tt_(b, si, re, ALU.mult))
                    step(tt_(state[:, 1, :, 1:], a, b, ALU.subtract))
                    for j in range(2):
                        for q in range(CB_PAIRS):
                            step(nc.vector.tensor_tensor_scan(scanned[:, j, q, 1:], decay[:, q:q + 1].to_broadcast([P, n1]),
                                                              state[:, j, q, 1:], 0.0, ALU.mult, ALU.add))
                    re, im = (scanned[:, j, :, :] for j in range(2))
                    co, si = (tab[:, j, :, :] for j in range(2))
                    a, b = t1[:, :, :], t2[:, :, :]
                    step(tt_(a, co, re, ALU.mult))
                    step(tt_(b, si, im, ALU.mult))
                    step(tt_(state[:, 0], a, b, ALU.subtract))
                    step(tt_(a, co, im, ALU.mult))
                    step(tt_(b, si, re, ALU.mult))
                    step(tt_(state[:, 1], a, b, ALU.add))
                    for n in range(4):
                        dve.wait_ge(high, 4 * i + n + 1)
                        h = n % 2
                        tt_(out_lo[:, :, 4 * h:4 * h + 4].rearrange("p m t -> p t m"), ps_t[:, n % 2, :, :],
                            out_hi[:, :, 4 * h:4 * h + 4].rearrange("p m t -> p t m").bitcast(F32), ALU.subtract).then_inc(low, 1)


def lru_units(eng, head, tail):
    per, turns = 2 * QUARTERS, LRU_BLOCKS // 2
    head(0, 0)
    with eng.Fori(0, turns - 1) as i:
        for u in range(per):
            head(*((i, u + 1) if u + 1 < per else (i + 1, 0)))
            tail(i, u)
    for u in range(per):
        if u + 1 < per:
            head(turns - 1, u + 1)
        tail(turns - 1, u)


def rg_lru(nc, d, h_hi, h_lo):
    with ExitStack() as cx:
        sb = lambda n, s, t=F32: cx.enter_context(nc.sbuf_tensor("r4_" + n, s, t))
        sem = lambda n: cx.enter_context(nc.semaphore("r4_" + n))
        Q = QUARTER
        HALO = CONV_WIDTH - 1
        raw = sb("raw", [P, 2, KT, P])
        w_hi = sb("w_hi", [P, 2, 2, KT, P], F32R)
        w_lo = sb("w_lo", [P, 2, 2, KT, P], F32R)
        graw = sb("graw", [P, 2, P])
        g_hi = sb("g_hi", [P, 2, 2, P], F32R)
        g_lo = sb("g_lo", [P, 2, 2, P], F32R)
        NPAR = CONV_WIDTH + 4
        C_BIAS, C_BR, C_BI, C_LAM = range(CONV_WIDTH, NPAR)
        par = sb("par", [P, NPAR, LRU_BLOCKS])
        pslot = sb("pslot", [P, 2, NPAR])
        pt = sb("pt", [P, 5, LRU_BLOCKS])
        xl = sb("xl", [P, 2, HALO + Q])
        xc = sb("xc", [P, 2, Q])
        xc_hi = sb("xc_hi", [P, Q], F32R)
        xc_lo = sb("xc_lo", [P, Q], F32R)
        rg = sb("rg", [P, Q])
        ig = sb("ig", [P, Q])
        th = sb("th", [P, Q])
        rc = sb("rc", [P, Q])
        root = sb("root", [P, Q])
        hh = sb("hh", [P, 2, Q])
        gy = sb("gy", [P, Q])
        y_hi = sb("y_hi", [P, Q], F32R)
        y_lo = sb("y_lo", [P, Q], F32R)
        psum = lambda n: cx.enter_context(nc.psum_tensor("r4_" + n, [P, 2, Q], F32))
        ps_x, ps_g, ps_r, ps_i = psum("ps_x"), psum("ps_g"), psum("ps_r"), psum("ps_i")
        (par_in, raw_in, w_split, w_steps, lam_steps, lam_exp, xl_made, gl_made, ri_made, xl_taken, sig_done, tanh_done,
         root_done, gelu_done, conv_done, xc_split, head_steps, tail_steps, bx_done, y_split, m2_done, y_sent, zeroed, scanned) = (sem(n) for n in (
            "par_in", "raw_in", "w_split", "w_steps", "lam_steps", "lam_exp", "xl_made", "gl_made", "ri_made", "xl_taken", "sig_done",
            "tanh_done", "root_done", "gelu_done", "conv_done", "xc_split", "head_steps", "tail_steps", "bx_done", "y_split", "m2_done", "y_sent", "zeroed", "scanned"))
        LOADS = 16 * 6
        W_STEPS = 7
        HEAD_STEPS = 5
        TAIL_STEPS = 6
        PARAMS = ("conv_b", "lru_b_r", "lru_b_i", "lru_lambda")
        unit = lambda i, u: 2 * QUARTERS * i + u
        block_of = lambda i, u: 2 * i + u // QUARTERS

        with nc.Block() as block:

            @block.sync
            def _(sp):
                with nc.allow_non_contiguous_dma(reason="one parameter a partition"):
                    for k in range(CONV_WIDTH):
                        sp.dma_start(par[:, k, :], columns(d["conv_w"][0, k], LRU_BLOCKS)).then_inc(par_in, 16)
                    for k, name in enumerate(PARAMS):
                        sp.dma_start(par[:, CONV_WIDTH + k, :], columns(d[name][0], LRU_BLOCKS)).then_inc(par_in, 16)
                sp.sem_inc(y_sent, 32)
                sp.wait_ge(zeroed, 1)

                def load(c):
                    sp.wait_ge(w_split, 4 * c + 4)
                    for j, o in enumerate((O_LRU, O_GATE)):
                        sp.dma_start(raw[:, j, :, :], d["w_in"][0, :, bass.ds(c * P + o, P)].rearrange("(k p) n -> p k n", p=P)).then_inc(raw_in, 16)
                    for j, name in enumerate(("lru_w_r", "lru_w_i")):
                        for r in range(2):
                            rows = slice(64 * r, 64 * r + 64)
                            sp.dma_start(graw[rows, j, rows], d[name][0, bass.ds(2 * c + r, 1), :, :].rearrange("a i j -> (a i) j")).then_inc(raw_in, 16)

                def store(i, u):
                    n = unit(i, u)
                    sp.wait_ge(y_split, n + 2)
                    for j, y in enumerate((y_hi, y_lo)):
                        sp.dma_start(d["yl_t"][j, bass.ds(block_of(i, u) * P, P), (u % QUARTERS) * Q:(u % QUARTERS + 1) * Q],
                                     y[:, :].bitcast(F32)).then_inc(y_sent, 16)

                load(0)
                load(1)
                with sp.Fori(0, LRU_BLOCKS // 2 - 1) as i:
                    for u in range(2 * QUARTERS):
                        if u % QUARTERS == QUARTERS - 1:
                            load(2 * i + u // QUARTERS + 2)
                        store(i, u)
                for u in range(2 * QUARTERS):
                    store(LRU_BLOCKS // 2 - 1, u)
                sp.wait_ge(y_sent, 32 * (1 + QUARTERS * LRU_BLOCKS))

            @block.tensor
            def _(pe):
                pe.sem_inc(ri_made, 1)

                def head(i, u):
                    n, c, p, b = unit(i, u), block_of(i, u), u % 2, u // QUARTERS
                    if u % QUARTERS == 0:
                        pe.wait_ge(w_split, 4 * c + 8)
                    toks = slice((u % QUARTERS) * Q, (u % QUARTERS + 1) * Q)
                    for j, (ps, free, made) in enumerate(((ps_x, xl_taken, xl_made), (ps_g, gelu_done, gl_made))):
                        pe.wait_ge(free, n + 1)
                        for k in range(KT):
                            last = matmul3(nc, ps[:, p, :], w_hi[:, b, j, k, :], w_lo[:, b, j, k, :],
                                           h_hi[:, k, toks], h_lo[:, k, toks], k == 0, k == KT - 1)
                        last.then_inc(made, 1)

                def tail(i, u):
                    n, p, b = unit(i, u), u % 2, u // QUARTERS
                    pe.wait_ge(xc_split, n + 1)
                    pe.wait_ge(sig_done, n + 1)
                    for j, ps in enumerate((ps_r, ps_i)):
                        last = matmul3(nc, ps[:, p, :], g_hi[:, b, j, :], g_lo[:, b, j, :], xc_hi[:, :], xc_lo[:, :], True, True)
                    last.then_inc(ri_made, 1)

                lru_units(pe, head, tail)

            @block.scalar
            def _(act):
                act.sem_inc(xl_taken, 2)
                act.sem_inc(gelu_done, 2)
                act.sem_inc(sig_done, 2)
                act.wait_ge(lam_steps, 1)
                nc.scalar.activation(pt[:, 1, :], pt[:, 0, :], ACT.Exp, scale=-1.0).then_inc(lam_exp, 1)

                def head(i, u):
                    n, p = unit(i, u), u % 2
                    act.wait_ge(xl_made, n + 1)
                    act.wait_ge(conv_done, n + 3)
                    nc.scalar.copy(xl[:, p, HALO:], ps_x[:, p, :]).then_inc(xl_taken, 1)

                def tail(i, u):
                    n, p, b = unit(i, u), u % 2, u // QUARTERS
                    act.wait_ge(ri_made, n + 2)
                    act.wait_ge(bx_done, n + 1)
                    nc.scalar.activation(rg[:, :], ps_r[:, p, :], ACT.Sigmoid, bias=pslot[:, b, C_BR:C_BR + 1]).then_inc(tanh_done, 1)
                    nc.scalar.activation(ig[:, :], ps_i[:, p, :], ACT.Sigmoid, bias=pslot[:, b, C_BI:C_BI + 1]).then_inc(sig_done, 1)
                    act.wait_ge(tanh_done, 2 * n + 1)
                    nc.scalar.activation(th[:, :], rg[:, :], ACT.Tanh, scale=pslot[:, b, C_LAM:C_LAM + 1]).then_inc(tanh_done, 1)
                    act.wait_ge(tanh_done, 2 * n + 2)
                    act.wait_ge(scanned, n + 1)
                    nc.scalar.activation(root[:, :], th[:, :], ACT.Sqrt, scale=-1.0).then_inc(root_done, 1)
                    act.wait_ge(y_split, n + 1)
                    nc.scalar.activation(gy[:, :], ps_g[:, p, :], ACT.Gelu_apprx_tanh).then_inc(gelu_done, 1)

                lru_units(act, head, tail)

            @block.gpsimd
            def _(pool):
                nc.gpsimd.memset(graw[:, :, :], 0.0).then_inc(zeroed, 1)

                def head(i, u):
                    pass

                def tail(i, u):
                    n, p = unit(i, u), u % 2
                    pool.wait_ge(conv_done, n + 4)
                    pool.wait_ge(sig_done, n + 3)
                    nc.gpsimd.tensor_tensor(ig[:, :], ig[:, :], xc[:, p, :], ALU.mult).then_inc(m2_done, 1)

                lru_units(pool, head, tail)

            @block.vector
            def _(dve):
                ts_, tt_, stt_ = nc.vector.tensor_scalar, nc.vector.tensor_tensor, nc.vector.scalar_tensor_tensor
                dve.sem_inc(w_split, 4)
                dve.sem_inc(conv_done, 3)
                dve.sem_inc(bx_done, 1)
                dve.sem_inc(scanned, 1)
                dve.sem_inc(y_split, 1)
                dve.wait_ge(par_in, 16 * NPAR)
                lam = par[:, C_LAM, :]
                step = Chain(dve, lam_steps)
                step(stt_(pt[:, 0, :], lam, -1.0, lam, ALU.mult, ALU.max))
                dve.wait_ge(lam_exp, 1)
                step(ts_(pt[:, 2, :], pt[:, 1, :], 2.0, None, ALU.add))
                step(nc.vector.reciprocal(pt[:, 3, :], pt[:, 2, :]))
                step(tt_(pt[:, 1, :], pt[:, 1, :], pt[:, 3, :], ALU.mult))
                step(tt_(pt[:, 2, :], pt[:, 1, :], pt[:, 1, :], ALU.mult))
                step(ts_(pt[:, 3, :], pt[:, 2, :], 1.0 / 15, 1.0 / 13, ALU.mult, ALU.add))
                for m in (11, 9, 7, 5, 3, 1):
                    step(tt_(pt[:, 4, :], pt[:, 3, :], pt[:, 2, :], ALU.mult))
                    step(ts_(pt[:, 3, :], pt[:, 4, :], 1.0 / m, None, ALU.add))
                step(tt_(pt[:, 4, :], pt[:, 3, :], pt[:, 1, :], ALU.mult))
                step(ts_(pt[:, 3, :], lam, -1.0, 0.0, ALU.mult, ALU.max))
                step(stt_(pt[:, 2, :], pt[:, 4, :], 2.0, pt[:, 3, :], ALU.mult, ALU.add))
                step(ts_(lam, pt[:, 2, :], -LRU_C / 2, None, ALU.mult))

                def split_weights(c, b, part):
                    if part == 0:
                        dve.wait_ge(raw_in, LOADS * (c + 1))
                    step = Chain(dve, w_steps, W_STEPS * c + part)
                    ks = slice(2 * part, 2 * part + 2)
                    step(nc.vector.tensor_copy(w_hi[:, b, :, ks, :], raw[:, :, ks, :]))
                    if part == QUARTERS - 1:
                        step(nc.vector.tensor_copy(g_hi[:, b, :, :], graw[:, :, :]))
                        step(tt_(g_lo[:, b, :, :], graw[:, :, :], g_hi[:, b, :, :].bitcast(F32), ALU.subtract))
                        step(nc.vector.tensor_copy(pslot[:, b, :].unsqueeze(2), par[:, :, bass.ds(c, 1)]))
                    tt_(w_lo[:, b, :, ks, :], raw[:, :, ks, :], w_hi[:, b, :, ks, :].bitcast(F32), ALU.subtract).then_inc(w_split, 1)

                for part in range(QUARTERS):
                    split_weights(0, 0, part)
                dve.wait_ge(w_split, 8)

                def head(i, u):
                    n, c, p, b, t = unit(i, u), block_of(i, u), u % 2, u // QUARTERS, u % QUARTERS
                    step = Chain(dve, head_steps, HEAD_STEPS * n)
                    tap = lambda k: pslot[:, b, k:k + 1]
                    dve.wait_ge(xl_taken, n + 3)
                    if t == 0:
                        step(nc.vector.memset(xl[:, p, 0:HALO], 0.0))
                    else:
                        step(nc.vector.tensor_copy(xl[:, p, 0:HALO], xl[:, 1 - p, Q:Q + HALO]))
                    step(ts_(xc[:, p, :], xl[:, p, 0:Q], tap(0), tap(C_BIAS), ALU.mult, ALU.add))
                    for k in (1, 2):
                        step(stt_(xc[:, p, :], xl[:, p, k:k + Q], tap(k), xc[:, p, :], ALU.mult, ALU.add))
                    stt_(xc[:, p, :], xl[:, p, HALO:], tap(HALO), xc[:, p, :], ALU.mult, ALU.add).then_inc(conv_done, 1)
                    dve.wait_ge(conv_done, n + 4)
                    dve.wait_ge(ri_made, n + 1)
                    step(nc.vector.tensor_copy(xc_hi[:, :], xc[:, p, :]))
                    tt_(xc_lo[:, :], xc[:, p, :], xc_hi[:, :].bitcast(F32), ALU.subtract).then_inc(xc_split, 1)
                    if not (isinstance(c, int) and c == LRU_BLOCKS - 1):
                        split_weights(c + 1, 1 - b, t)

                def tail(i, u):
                    n, p, t = unit(i, u), u % 2, u % QUARTERS
                    step = Chain(dve, tail_steps, TAIL_STEPS * n)
                    dve.wait_ge(tanh_done, 2 * n + 2)
                    step(ts_(rc[:, :], th[:, :], -1.0, 1.0, ALU.mult, ALU.add))
                    step(nc.vector.reciprocal(rc[:, :], rc[:, :]))
                    dve.wait_ge(root_done, n + 1)
                    step(tt_(root[:, :], rc[:, :], root[:, :], ALU.mult))
                    step(ts_(rc[:, :], rc[:, :], 2.0, -1.0, ALU.mult, ALU.add))
                    dve.wait_ge(m2_done, n + 1)
                    stt_(root[:, :], root[:, :], 2.0, ig[:, :], ALU.mult, ALU.mult).then_inc(bx_done, 1)
                    dve.wait_ge(bx_done, n + 2)
                    nc.vector.tensor_tensor_scan(hh[:, p, :], rc[:, :], root[:, :], 0.0 if t == 0 else hh[:, 1 - p, Q - 1:Q],
                                                 ALU.mult, ALU.add).then_inc(scanned, 1)
                    dve.wait_ge(scanned, n + 2)
                    dve.wait_ge(gelu_done, n + 3)
                    step(tt_(gy[:, :], gy[:, :], hh[:, p, :], ALU.mult))
                    dve.wait_ge(y_sent, 32 * n + 32)
                    step(nc.vector.tensor_copy(y_hi[:, :], gy[:, :]))
                    tt_(y_lo[:, :], gy[:, :], y_hi[:, :].bitcast(F32), ALU.subtract).then_inc(y_split, 1)

                lru_units(dve, head, tail)


def mix_branches(nc, d):
    DB = D_MODEL // P
    KS = S5_WIDTH // P
    Q = QUARTER
    UNITS = QUARTERS * DB
    with ExitStack() as cx:
        sb = lambda n, s, t=F32: cx.enter_context(nc.sbuf_tensor("m5_" + n, s, t))
        sem = lambda n: cx.enter_context(nc.semaphore("m5_" + n))
        h = sb("h", [P, 2, 2, KT, Q], F32R)
        ys = sb("ys", [P, 2, KS, Q], F32R)
        yl = sb("yl", [P, 2, KT, Q], F32R)
        raw = sb("raw", [P, 2, KT, P])
        w_hi = sb("w_hi", [P, 2, 4, KT, P], F32R)
        w_lo = sb("w_lo", [P, 2, 4, KT, P], F32R)
        ga = sb("ga", [P, Q])
        gb = sb("gb", [P, Q])
        gz = sb("gz", [P, Q])
        m_hi = sb("m_hi", [P, Q], F32R)
        m_lo = sb("m_lo", [P, Q], F32R)
        ps = {n: cx.enter_context(nc.psum_tensor("m5_ps_" + n, [P, Q], F32)) for n in ("ga", "gb", "z1", "z2", "yb")}
        (h_in0, h_in1, ys_in, yl_in, w_split, high, made_ga, made_gb, made_z, made_yb, sig, steps, mixed, sent) = (sem(n) for n in (
            "h_in0", "h_in1", "ys_in", "yl_in", "w_split", "high", "made_ga", "made_gb", "made_z", "made_yb", "sig", "steps", "mixed", "sent"))
        raw_in = [sem("raw_in0"), sem("raw_in1")]
        order = sem("order")
        h_in = [h_in0, h_in1]
        PIECES = 4
        GA, GB, Z, YB = range(PIECES)
        STEPS = 5

        def units(eng, body, enter=lambda tq: None):
            for tq in range(QUARTERS):
                enter(tq)
                with eng.Fori(0, DB // 2) as i:
                    for b in range(2):
                        body(DB * tq + 2 * i + b, tq, 2 * i + b, b)

        with nc.Block() as block:

            @block.sync
            def _(sp):
                def piece(n, blk, p, turn):
                    sp.wait_ge(w_split, PIECES * n + p + 1)
                    sp.sem_inc(order, 1)
                    cols = lambda o: bass.ds(blk * P + o, P)
                    if p == Z:
                        for j in range(2):
                            sp.dma_start(raw[:, p % 2, j * KS:(j + 1) * KS, :],
                                         d["w_s5_out"][0, :, cols(j * D_MODEL)].rearrange("(k p) n -> p k n", p=P)).then_inc(raw_in[p % 2], 16)
                    else:
                        src = d["w_lru_out"][0, :, cols(0)] if p == YB else d["w_in"][0, :, cols(O_GA if p == GA else O_GB)]
                        sp.dma_start(raw[:, p % 2, :, :], src.rearrange("(k p) n -> p k n", p=P)).then_inc(raw_in[p % 2], 16)

                def body(n, tq, blk, b):
                    for p in range(PIECES):
                        piece(n, blk, p, n)

                units(sp, body)

            @block.gpsimd
            def _(pool):
                def take(dst, src, sem_):
                    pool.dma_start(dst.bitcast(F32), src.rearrange("(k p) t -> p k t", p=P)).then_inc(sem_, 16)

                for tq in range(QUARTERS):
                    toks = slice(tq * Q, (tq + 1) * Q)
                    if tq == 0:
                        for a in range(2):
                            take(h[:, 0, a], d["h_t"][a, :, toks], h_in[0])
                    if tq >= 1:
                        pool.wait_ge(made_z, DB * tq)
                    for a in range(2):
                        take(ys[:, a], d["ys_t"][a, :, toks], ys_in)
                    if tq >= 1:
                        pool.wait_ge(made_yb, DB * tq)
                    for a in range(2):
                        take(yl[:, a], d["yl_t"][a, :, toks], yl_in)
                    if tq + 1 < QUARTERS:
                        toks = slice((tq + 1) * Q, (tq + 2) * Q)
                        for a in range(2):
                            take(h[:, (tq + 1) % 2, a], d["h_t"][a, :, toks], h_in[(tq + 1) % 2])

            @block.tensor
            def _(pe):
                def group(out, b, p, k0, count, act):
                    for k in range(count):
                        last = matmul3(nc, out[:, :], w_hi[:, b, p, k0 + k, :], w_lo[:, b, p, k0 + k, :],
                                       act[:, 0, k, :], act[:, 1, k, :], k == 0, k == count - 1)
                    return last

                def enter(tq):
                    pe.wait_ge(h_in[tq % 2], 32 * (tq // 2 + 1))

                def body(n, tq, blk, b):
                    pe.wait_ge(w_split, PIECES * (n + 1) + 2)
                    pe.wait_ge(sig, 3 * n + 3)
                    group(ps["ga"], b, GA, 0, KT, h[:, tq % 2]).then_inc(made_ga, 1)
                    group(ps["gb"], b, GB, 0, KT, h[:, tq % 2]).then_inc(made_gb, 1)
                    pe.wait_ge(ys_in, 32 * (tq + 1))
                    pe.wait_ge(mixed, n + 1)
                    group(ps["z2"], b, Z, KS, KS, ys)
                    group(ps["z1"], b, Z, 0, KS, ys).then_inc(made_z, 1)
                    pe.wait_ge(yl_in, 32 * (tq + 1))
                    group(ps["yb"], b, YB, 0, KT, yl).then_inc(made_yb, 1)

                units(pe, body, enter)

            @block.scalar
            def _(act):
                act.sem_inc(sig, 3)

                def body(n, tq, blk, b):
                    act.wait_ge(made_ga, n + 1)
                    act.wait_ge(mixed, n + 1)
                    nc.scalar.activation(ga[:, :], ps["ga"][:, :], ACT.Sigmoid).then_inc(sig, 1)
                    act.wait_ge(made_gb, n + 1)
                    nc.scalar.activation(gb[:, :], ps["gb"][:, :], ACT.Sigmoid).then_inc(sig, 1)
                    act.wait_ge(made_z, n + 1)
                    nc.scalar.activation(gz[:, :], ps["z2"][:, :], ACT.Sigmoid).then_inc(sig, 1)
                    act.wait_ge(mixed, n + 2)
                    for a, m in enumerate((m_hi, m_lo)):
                        act.dma_start(d["mix_t"][a, bass.ds(blk * P, P), tq * Q:(tq + 1) * Q], m[:, :].bitcast(F32)).then_inc(sent, 16)

                units(act, body)
                act.wait_ge(sent, 32 * UNITS + 32)

            @block.vector
            def _(dve):
                tt_ = nc.vector.tensor_tensor
                dve.sem_inc(mixed, 1)
                dve.sem_inc(w_split, 2)
                dve.sem_inc(sent, 32)

                def split(n, b, turn):
                    for p in range(PIECES):
                        dve.wait_ge(raw_in[p % 2], (48 * turn + (16, 16, 48, 32)[p]) if p % 2 == 0 else 32 * turn + (0, 16, 0, 32)[p])
                        nc.vector.tensor_copy(w_hi[:, b, p], raw[:, p % 2]).then_inc(high, 1)
                        dve.wait_ge(high, PIECES * n + p + 1)
                        tt_(w_lo[:, b, p], raw[:, p % 2], w_hi[:, b, p].bitcast(F32), ALU.subtract).then_inc(w_split, 1)

                def mix(n):
                    step = Chain(dve, steps, STEPS * n)
                    dve.wait_ge(sig, 3 * n + 6)
                    step(tt_(gz[:, :], gz[:, :], ps["z1"][:, :], ALU.mult))
                    step(tt_(ga[:, :], ga[:, :], gz[:, :], ALU.mult))
                    dve.wait_ge(made_yb, n + 1)
                    step(tt_(gb[:, :], gb[:, :], ps["yb"][:, :], ALU.mult))
                    step(tt_(ga[:, :], ga[:, :], gb[:, :], ALU.add))
                    dve.wait_ge(sent, 32 * n + 32)
                    step(nc.vector.tensor_copy(m_hi[:, :], ga[:, :]))
                    tt_(m_lo[:, :], ga[:, :], m_hi[:, :].bitcast(F32), ALU.subtract).then_inc(mixed, 1)

                split(0, 0, 0)
                with dve.Fori(0, UNITS // 2 - 1) as i:
                    for b in range(2):
                        split(2 * i + b + 1, 1 - b, 2 * i + b + 1)
                        mix(2 * i + b)
                split(UNITS - 1, 1, UNITS - 1)
                mix(UNITS - 2)
                mix(UNITS - 1)


def project_and_route(nc, d, keep):
    with ExitStack() as cx:
        sb = lambda n, s, t=F32: cx.enter_context(nc.sbuf_tensor("p6_" + n, s, t))
        sem = lambda n: cx.enter_context(nc.semaphore("p6_" + n))
        NR = N_GROUPS + N_EXPERTS
        ident = keep["ident"]
        raw = sb("raw", [P, 2, D_MODEL])
        w_hi = sb("w_hi", [P, KT, D_MODEL], F32R)
        w_lo = sb("w_lo", [P, KT, D_MODEL], F32R)
        mix = sb("mix", [P, 2, 2, KT, P], F32R)
        xt = sb("xt", [P, 2, D_MODEL])
        h2 = sb("h2", [P, 2, D_MODEL])
        sq = sb("sq", [P, 2, D_MODEL])
        gain = sb("gain", [P, D_MODEL])
        ht = sb("ht", [P, KT, P])
        wr = sb("wr", [P, KT, NR])
        br = sb("br", [P, NR])
        sst = sb("sst", [P, 2, 3])
        cst = sb("cst", [P, 2])
        g8 = sb("g8", [P, 8])
        el = sb("el", [P, N_EXPERTS])
        e8 = sb("e8", [P, 8])
        top = sb("top", [P, 8])
        idx = sb("idx", [P, 8], U32)
        gsel = sb("gsel", [P, 8])
        s1 = sb("s1", [P, 8])
        ex = sb("ex", [P, 8])
        iota = sb("iota", [P, N_EXPERTS])
        tri = sb("tri", [P, P])
        ones = sb("ones", [P, P])
        acc = keep["acc"]
        asum = sb("asum", [P, N_EXPERTS])
        ranked = sb("ranked", [P, 2, N_EXPERTS])
        ps_o = cx.enter_context(nc.psum_tensor("p6_ps_o", [P, 2, D_MODEL], F32))
        ps_t = cx.enter_context(nc.psum_tensor("p6_ps_t", [P, KT, P], F32))
        ps_l = cx.enter_context(nc.psum_tensor("p6_ps_l", [P, 512], F32))
        ps_k = cx.enter_context(nc.psum_tensor("p6_ps_k", [P, 512], F32))
        (w_split, high, small_in, consts, made, x2_done, squared, mean, rstd, normed, turned, ht_done, logits, steps,
         picked, exped, ranked_mm) = (sem(n) for n in (
            "w_split", "high", "small_in", "consts", "made", "x2_done", "squared", "mean", "rstd", "normed", "turned", "ht_done",
            "logits", "steps", "picked", "exped", "ranked_mm"))
        x2_sent = [sem("x2_sent0"), sem("x2_sent1")]
        h2_sent = [sem("h2_sent0"), sem("h2_sent1")]
        w_in = [sem("w_in0"), sem("w_in1")]
        order = keep["order"]
        t_in = [sem("t_in0"), sem("t_in1")]
        STEPS = 26
        last_tile = TOK_TILES - 1

        def tiles(eng, head, tail):
            head(0, 0, 0)
            with eng.Fori(0, TOK_TILES // 2 - 1) as i:
                for b in range(2):
                    head(2 * i + b + 1, 1 - b, i + b)
                    tail(2 * i + b, b, i)
            head(last_tile, 1, TOK_TILES // 2 - 1)
            tail(last_tile - 1, 0, TOK_TILES // 2 - 1)
            tail(last_tile, 1, TOK_TILES // 2 - 1)

        with nc.Block() as block:

            @block.sync
            def _(sp):
                for k in range(KT):
                    if k >= 2:
                        sp.wait_ge(w_split, k - 1)
                    sp.dma_start(raw[:, k % 2, :], d["w_o"][0, k * P:(k + 1) * P, :]).then_inc(w_in[k % 2], 16)
                sp.dma_start(gain[:, :], d["norm_ffn"][0:1, :].to_broadcast([P, D_MODEL])).then_inc(small_in, 16)
                with nc.allow_non_contiguous_dma(reason="the router's narrow weights"):
                    sp.dma_start(wr[:, :, 0:N_GROUPS], d["router_group_w"][0].rearrange("(k p) n -> p k n", p=P)).then_inc(small_in, 16)
                    sp.dma_start(wr[:, :, N_GROUPS:], d["router_expert_w"][0].rearrange("(k p) n -> p k n", p=P)).then_inc(small_in, 16)
                sp.dma_start(br[:, 0:N_GROUPS], d["router_group_b"][0:1, :].to_broadcast([P, N_GROUPS])).then_inc(small_in, 16)
                sp.dma_start(br[:, N_GROUPS:], d["router_expert_b"][0:1, :].to_broadcast([P, N_EXPERTS])).then_inc(small_in, 16)
                with sp.Fori(0, TOK_TILES // 2) as i:
                    for b in range(2):
                        t = 2 * i + b
                        sp.wait_ge(normed, t + 1)
                        sp.sem_inc(order, 1)
                        sp.wait_ge(x2_sent[b], 16 * i + 16)
                        for a in range(2):
                            sp.dma_start(mix[:, b, a].bitcast(F32), d["mix_t"][a, :, bass.ds(t * P, P)].rearrange("(k p) t -> p k t", p=P)).then_inc(t_in[b], 16)
                        sp.dma_start(xt[:, b, :], d["x"][0, bass.ds(t * P, P), :]).then_inc(t_in[b], 16)

            @block.tensor
            def _(pe):
                pe.sem_inc(turned, 1)
                pe.wait_ge(small_in, 16 * 5)
                pe.wait_ge(consts, 7)

                def head(t, b, turn):
                    pe.wait_ge(t_in[b], 48 * (turn + 1))
                    pe.wait_ge(x2_done, t + 1)
                    for half in range(2):
                        for k in range(KT):
                            if isinstance(t, int) and t == 0 and half == 0:
                                pe.wait_ge(w_split, k + 1)
                            cols = slice(half * 512, half * 512 + 512)
                            last = matmul3(nc, ps_o[:, b, cols], mix[:, b, 0, k, :], mix[:, b, 1, k, :], w_hi[:, k, cols], w_lo[:, k, cols],
                                           k == 0, k == KT - 1)
                    last.then_inc(made, 1)

                def tail(t, b, turn):
                    pe.wait_ge(normed, t + 3)
                    pe.wait_ge(ht_done, t + 1)
                    for k in range(KT):
                        last = nc.tensor.transpose(ps_t[:, k, :], h2[:, b, k * P:(k + 1) * P], ident[:, :])
                    last.then_inc(turned, 1)
                    pe.wait_ge(ht_done, t + 2)
                    for k in range(KT):
                        last = nc.tensor.matmul(ps_l[:, 0:NR], ht[:, k, :], wr[:, k, :], start=(k == 0), stop=(k == KT - 1))
                    last.then_inc(logits, 1)
                    pe.wait_ge(picked, t + 1)
                    nc.tensor.matmul(ps_k[:, 0:N_EXPERTS], tri[:, :], asum[:, :], start=True, stop=False)
                    nc.tensor.matmul(ps_k[:, 0:N_EXPERTS], ones[:, :], acc[:, :], start=False, stop=True).then_inc(ranked_mm, 1)

                tiles(pe, head, tail)

            @block.scalar
            def _(act):
                for s in x2_sent + h2_sent:
                    act.sem_inc(s, 16)
                act.sem_inc(ht_done, 1)
                act.wait_ge(small_in, 16 * 5)

                def head(t, b, turn):
                    act.wait_ge(x2_done, t + 3)
                    act.dma_start(d["x2"][bass.ds(t * P, P), :], xt[:, b, :]).then_inc(x2_sent[b], 16)
                    act.wait_ge(rstd, t + 1)
                    nc.scalar.activation(sq[:, b, :], xt[:, b, :], ACT.Square, accum_out=sst[:, b, 0:1]).then_inc(squared, 1)

                def tail(t, b, turn):
                    act.wait_ge(normed, t + 3)
                    act.dma_start(d["h2"][bass.ds(t * P, P), :], h2[:, b, :]).then_inc(h2_sent[b], 16)
                    act.wait_ge(turned, t + 2)
                    act.wait_ge(steps, STEPS * t + 1)
                    nc.scalar.copy(ht[:, :, :], ps_t[:, :, :]).then_inc(ht_done, 1)
                    act.wait_ge(steps, STEPS * t + 5)
                    nc.scalar.activation(s1[:, 0:N_GROUPS], g8[:, 0:N_GROUPS], ACT.Exp, bias=ex[:, 0:1], accum_out=ex[:, 1:2]).then_inc(exped, 1)
                    act.wait_ge(steps, STEPS * t + 15)
                    nc.scalar.activation(ex[:, 3:4], ex[:, 2:3], ACT.Exp).then_inc(exped, 1)

                tiles(act, head, tail)
                for s in x2_sent + h2_sent:
                    act.wait_ge(s, 16 * (TOK_TILES // 2 + 1))

            @block.gpsimd
            def _(pool):
                pool.sem_inc(rstd, 2)
                nc.gpsimd.memset(cst[:, 0:1], -0.5).then_inc(consts, 1)
                nc.gpsimd.memset(cst[:, 1:2], RMS_EPS * D_MODEL).then_inc(consts, 1)
                nc.gpsimd.iota(iota[:, :], pattern=[[1, N_EXPERTS]], base=0, channel_multiplier=0,
                               allow_small_or_imprecise_dtypes=True).then_inc(consts, 1)
                nc.gpsimd.memset(ones[:, :], 1.0).then_inc(consts, 1)
                nc.gpsimd.memset(g8[:, :], -3.0e38).then_inc(consts, 1)
                nc.gpsimd.memset(acc[:, :], 0.0).then_inc(consts, 1)
                pool.wait_ge(consts, 6)
                nc.gpsimd.affine_select(out=tri[:, :], in_=ones[:, :], compare_op=ALU.is_gt, fill=0.0,
                                        base=0, pattern=[[1, P]], channel_multiplier=-1).then_inc(consts, 1)

                def head(t, b, turn):
                    pool.wait_ge(squared, t + 1)
                    nc.gpsimd.tensor_tensor(sst[:, b, 1:2], sst[:, b, 0:1], cst[:, 1:2], ALU.add).then_inc(mean, 1)
                    pool.wait_ge(mean, t + 1)
                    pool.wait_ge(normed, t + 1)
                    nc.gpsimd.tensor_tensor(sst[:, b, 2:3], sst[:, b, 1:2], cst[:, 0:1], ALU.pow).then_inc(rstd, 1)

                tiles(pool, head, lambda t, b, turn: None)

            @block.vector
            def _(dve):
                ts_, tt_, stt_ = nc.vector.tensor_scalar, nc.vector.tensor_tensor, nc.vector.scalar_tensor_tensor
                dve.sem_inc(x2_done, 2)
                dve.sem_inc(normed, 2)
                for k in range(KT):
                    dve.wait_ge(w_in[k % 2], 16 * (k // 2 + 1))
                    nc.vector.tensor_copy(w_hi[:, k, :], raw[:, k % 2, :]).then_inc(high, 1)
                    dve.wait_ge(high, k + 1)
                    tt_(w_lo[:, k, :], raw[:, k % 2, :], w_hi[:, k, :].bitcast(F32), ALU.subtract).then_inc(w_split, 1)
                dve.wait_ge(small_in, 16 * 5)
                dve.wait_ge(consts, 7)
                nc.vector.tensor_scalar(gain[:, :], gain[:, :], math.sqrt(D_MODEL), None, ALU.mult).then_inc(steps, 1)
                dve.wait_ge(steps, 1)

                def head(t, b, turn):
                    dve.wait_ge(made, t + 1)
                    tt_(xt[:, b, :], ps_o[:, b, :], xt[:, b, :], ALU.add).then_inc(x2_done, 1)

                def tail(t, b, turn):
                    dve.wait_ge(rstd, t + 3)
                    dve.wait_ge(turned, t + 1)
                    dve.wait_ge(h2_sent[b], 16 * turn + 16)
                    stt_(h2[:, b, :], xt[:, b, :], sst[:, b, 2:3], gain[:, :], ALU.mult, ALU.mult).then_inc(normed, 1)
                    step = Chain(dve, steps, STEPS * t + 1)
                    dve.wait_ge(logits, t + 1)
                    step(tt_(g8[:, 0:N_GROUPS], ps_l[:, 0:N_GROUPS], br[:, 0:N_GROUPS], ALU.add))
                    step(tt_(el[:, :], ps_l[:, N_GROUPS:NR], br[:, N_GROUPS:], ALU.add))
                    dve.sem_inc(order, 1)
                    step(nc.vector.max(top[:, :], g8[:, :]))
                    step(ts_(ex[:, 0:1], top[:, 0:1], -1.0, None, ALU.mult))
                    dve.sem_inc(order, 1)
                    step(nc.vector.max_index(idx[:, :], top[:, :], g8[:, :]))
                    step(nc.vector.tensor_copy(gsel[:, 0:1], idx[:, 0:1]))
                    step(ts_(gsel[:, 4:8], iota[:, 0:N_GROUPS], gsel[:, 0:1], None, ALU.is_equal))
                    step(ts_(e8[:, :], el[:, 0:8], gsel[:, 4:5], None, ALU.mult))
                    for g in range(1, N_GROUPS):
                        step(stt_(e8[:, :], el[:, 8 * g:8 * g + 8], gsel[:, 4 + g:5 + g], e8[:, :], ALU.mult, ALU.add))
                    dve.sem_inc(order, 1)
                    step(nc.vector.max(top[:, :], e8[:, :]))
                    dve.sem_inc(order, 1)
                    step(nc.vector.max_index(idx[:, :], top[:, :], e8[:, :]))
                    step(tt_(ex[:, 2:3], top[:, 1:2], top[:, 0:1], ALU.subtract))
                    step(nc.vector.tensor_copy(gsel[:, 1:3], idx[:, 0:2]))
                    step(stt_(gsel[:, 1:3], gsel[:, 0:1].to_broadcast([P, 2]), float(EXPERTS_PER_GROUP), gsel[:, 1:3], ALU.mult, ALU.add))
                    chosen = keep["chosen"]
                    for k in range(2):
                        step(ts_(chosen[:, bass.ds(t, 1), k, :].rearrange("p a e -> p (a e)"), iota[:, :], gsel[:, 1 + k:2 + k], None, ALU.is_equal))
                    both = [chosen[:, bass.ds(t, 1), k, :].rearrange("p a e -> p (a e)") for k in range(2)]
                    tt_(asum[:, :], both[0], both[1], ALU.add).then_inc(picked, 1)
                    dve.wait_ge(exped, 2 * t + 2)
                    step(ts_(ex[:, 4:5], ex[:, 3:4], 1.0, None, ALU.add))
                    step(tt_(ex[:, 4:5], ex[:, 4:5], ex[:, 1:2], ALU.mult))
                    step(nc.vector.reciprocal(ex[:, 5:6], ex[:, 4:5]))
                    step(tt_(ex[:, 6:7], ex[:, 5:6], ex[:, 3:4], ALU.mult))
                    dve.sem_inc(order, 1)
                    step(nc.vector.tensor_copy(keep["gates"][:, bass.ds(t, 1), :].rearrange("p a k -> p (a k)"), ex[:, 5:7]))
                    dve.wait_ge(ranked_mm, t + 1)
                    step(tt_(ranked[:, :, :], chosen[:, bass.ds(t, 1), :, :].rearrange("p a k e -> p (a k) e"),
                             ps_k[:, 0:N_EXPERTS].unsqueeze(1).to_broadcast([P, 2, N_EXPERTS]), ALU.mult))
                    dve.sem_inc(order, 1)
                    step(nc.vector.tensor_reduce(keep["rank"][:, bass.ds(t, 1), :].rearrange("p a k -> p (a k)"), ranked[:, :, :], AX.X, ALU.add))
                    step(tt_(acc[:, :], acc[:, :], asum[:, :], ALU.add))
                    assert step.n == STEPS, step.n

                tiles(dve, head, tail)


def place_tokens(nc, d, keep):
    with ExitStack() as cx:
        sb = lambda n, s, t=F32: cx.enter_context(nc.sbuf_tensor("q7_" + n, s, t))
        sem = lambda n: cx.enter_context(nc.semaphore("q7_" + n))
        E = N_EXPERTS
        SLOT_STEPS = SEQ // P + 7
        ones = sb("ones", [P, P])
        cnt = sb("cnt", [P, E])
        nt = sb("nt", [P, E])
        end = sb("end", [P, E])
        pad = sb("pad", [P, E])
        one = sb("one", [P, E])
        prod = sb("prod", [P, TOK_TILES * 2, E])
        slotf = sb("slotf", [P, TOK_TILES * 2])
        te = sb("te", [1, MAX_TILES, E - 1])
        turn = sb("turn", [1, E])
        tef = sb("tef", [1, MAX_TILES])
        tio = sb("tio", [1, MAX_TILES])
        tok = sb("tok", [P, TOK_TILES], I32)
        zero = sb("zero", [MAX_TILES, P], I32)
        ids = sb("ids", [MAX_TILES, P], I32)
        idf = sb("idf", [MAX_TILES, P])
        pairs = sb("pairs", [1, 4])
        ps_c = cx.enter_context(nc.psum_tensor("q7_ps_c", [P, 512], F32))
        ps_i = cx.enter_context(nc.psum_tensor("q7_ps_i", [P, 512], F32))
        consts, counted, steps, zero_sent, scattered, ids_in, idf_done, turned = (sem(n) for n in (
            "consts", "counted", "steps", "zero_sent", "scattered", "ids_in", "idf_done", "turned"))
        with nc.Block() as block:

            @block.gpsimd
            def _(pool):
                nc.gpsimd.memset(ones[:, :], 1.0).then_inc(consts, 1)
                nc.gpsimd.memset(one[:, :], 1.0).then_inc(consts, 1)
                nc.gpsimd.memset(zero[:, :], 0).then_inc(consts, 1)
                nc.gpsimd.iota(tio[:, :], pattern=[[1, MAX_TILES]], base=0, channel_multiplier=0,
                               allow_small_or_imprecise_dtypes=True).then_inc(consts, 1)
                nc.gpsimd.iota(tok[:, :], pattern=[[P, TOK_TILES]], base=0, channel_multiplier=1).then_inc(consts, 1)
                nc.gpsimd.memset(turn[:, :], 1.0).then_inc(consts, 1)
                pool.wait_ge(consts, 6)
                nc.gpsimd.memset(turn[:, W_SLOTS - 1::W_SLOTS], 1.0 - W_SLOTS).then_inc(consts, 1)
                pool.wait_ge(consts, 7)
                pool.wait_ge(zero_sent, 16)
                pool.wait_ge(steps, SLOT_STEPS)
                for t in range(TOK_TILES):
                    for k in range(2):
                        nc.gpsimd.indirect_dma_start(out=d["slot_tok"], out_offset=bass.IndirectOffsetOnAxis(ap=keep["slot"][:, t, k:k + 1], axis=0),
                                                     in_=tok[:, t:t + 1], in_offset=None).then_inc(scattered, 16)

            @block.sync
            def _(sp):
                sp.wait_ge(consts, 7)
                sp.dma_start(d["slot_tok"].rearrange("(t p) o -> t (p o)", p=P), zero[:, :]).then_inc(zero_sent, 16)
                sp.wait_ge(scattered, 16 * 2 * TOK_TILES)
                sp.dma_start(ids[:, :], d["slot_tok"].rearrange("(t p) o -> t (p o)", p=P)).then_inc(ids_in, 16)

            @block.tensor
            def _(pe):
                pe.wait_ge(consts, 7)
                nc.tensor.matmul(ps_c[:, 0:E], ones[:, :], keep["acc"][:, :], start=True, stop=True).then_inc(counted, 1)
                pe.wait_ge(idf_done, 2)
                nc.tensor.transpose(ps_i[:, 0:MAX_TILES], idf[:, :], keep["ident"][0:MAX_TILES, 0:MAX_TILES]).then_inc(turned, 1)

            @block.vector
            def _(dve):
                ts_, tt_, stt_ = nc.vector.tensor_scalar, nc.vector.tensor_tensor, nc.vector.scalar_tensor_tensor
                step = Chain(dve, steps)
                nc.vector.memset(keep["ids"][:, MAX_TILES:], 0).then_inc(idf_done, 1)
                dve.wait_ge(counted, 1)
                dve.wait_ge(consts, 7)
                step(nc.vector.tensor_copy(cnt[:, :], ps_c[:, 0:E]))
                step(ts_(nt[:, :], cnt[:, :], float(P), 1.0, ALU.is_gt, ALU.add))
                for m in range(2, SEQ // P):
                    step(stt_(nt[:, :], cnt[:, :], float(m * P), nt[:, :], ALU.is_gt, ALU.add))
                step(nc.vector.tensor_tensor_scan(end[:, :], one[:, :], nt[:, :], 0.0, ALU.mult, ALU.add))
                step(tt_(pad[:, :], end[:, :], nt[:, :], ALU.subtract))
                step(ts_(pad[:, :], pad[:, :], float(P), None, ALU.mult))
                chosen = keep["chosen"][:, :, :, :].rearrange("p t k e -> p (t k) e")
                step(tt_(prod[:, :, :], chosen, pad[:, :].unsqueeze(1).to_broadcast([P, 2 * TOK_TILES, E]), ALU.mult))
                step(nc.vector.tensor_reduce(slotf[:, :], prod[:, :, :], AX.X, ALU.add))
                step(tt_(slotf[:, :], slotf[:, :], keep["rank"][:, :, :].rearrange("p t k -> p (t k)"), ALU.add))
                step(nc.vector.tensor_copy(keep["slot"][:, :, :].rearrange("p t k -> p (t k)"), slotf[:, :]))
                assert step.n == SLOT_STEPS
                shp = [1, MAX_TILES, E - 1]
                step(tt_(te[:, :, :], end[0:1, 0:E - 1].unsqueeze(1).to_broadcast(shp), tio[:, :].unsqueeze(2).to_broadcast(shp), ALU.is_le))
                step(nc.vector.tensor_reduce(tef[:, :], te[:, :, :], AX.X, ALU.add))
                step(nc.vector.tensor_copy(keep["tile_expert"][:, 0, :], tef[:, :]))
                step(tt_(te[:, :, :], te[:, :, :], turn[:, 0:E - 1].unsqueeze(1).to_broadcast(shp), ALU.mult))
                step(nc.vector.tensor_reduce(tef[:, :], te[:, :, :], AX.X, ALU.add))
                step(nc.vector.tensor_copy(keep["tile_expert"][:, 1, :], tef[:, :]))
                step(nc.vector.tensor_copy(keep["tile_end"][:, 0:E], end[0:1, :]))
                step(ts_(pairs[:, 0:1], end[0:1, E - 1:E], 0.5, 0.25, ALU.mult, ALU.add))
                step(ts_(pairs[:, 1:2], pairs[:, 0:1], 2.0 ** 23, None, ALU.add))
                step(ts_(pairs[:, 2:3], pairs[:, 1:2], 2.0 ** 23, None, ALU.subtract))
                step(ts_(pairs[:, 3:4], pairs[:, 2:3], -1.0, MAX_TILES / 2 + 1.0, ALU.mult, ALU.add))
                step(nc.vector.tensor_copy(keep["tile_end"][:, E:E + 2], pairs[:, 2:4]))
                dve.wait_ge(ids_in, 16)
                nc.vector.tensor_copy(idf[:, :], ids[:, :]).then_inc(idf_done, 1)
                dve.wait_ge(turned, 1)
                nc.vector.tensor_copy(keep["ids"][:, 0:MAX_TILES], ps_i[:, 0:MAX_TILES]).then_inc(idf_done, 1)


def run_experts(nc, d, keep):
    with ExitStack() as cx:
        sb = lambda n, s, t=F32: cx.enter_context(nc.sbuf_tensor("e8_" + n, s, t))
        sem = lambda n: cx.enter_context(nc.semaphore("e8_" + n))
        ident, ids, order = keep["ident"], keep["ids"], keep["order"]
        FK = D_EXPERT // P
        GATE, UP, DOWN = 0, KT * D_EXPERT, 2 * KT * D_EXPERT
        W = DOWN + FK * D_MODEL
        w = sb("w", [P, W_SLOTS * W])
        idc = sb("idc", [P, 2], U32)
        zero = sb("zero", [P, D_MODEL])
        xg = sb("xg", [P, 2, D_MODEL])
        xt = sb("xt", [P, 2, KT, P])
        s = sb("s", [P, D_EXPERT])
        a = sb("a", [P, D_EXPERT])
        at = sb("at", [P, FK, P])
        y = sb("y", [P, 2, D_MODEL])
        ps_t = cx.enter_context(nc.psum_tensor("e8_ps_t", [P, KT, P], F32))
        ps_g = cx.enter_context(nc.psum_tensor("e8_ps_g", [P, D_EXPERT], F32))
        ps_u = cx.enter_context(nc.psum_tensor("e8_ps_u", [P, D_EXPERT], F32))
        ps_a = cx.enter_context(nc.psum_tensor("e8_ps_a", [P, FK, P], F32))
        ps_y = cx.enter_context(nc.psum_tensor("e8_ps_y", [P, D_MODEL], F32))
        (weights_ready, idc_done, turned, xt_ready, g_made, u_made, a_done, a_turned, at_ready, y_made, y_out, silu_done) = (
            sem(n) for n in ("weights_ready", "idc_done", "turned", "xt_ready", "g_made", "u_made", "a_done", "a_turned",
                             "at_ready", "y_made", "y_out", "silu_done"))
        zeroed, filled = sem("zeroed"), sem("filled")
        w_in = [sem(f"w_in{i}") for i in range(W_SLOTS)]
        x_in = [sem("x_in0"), sem("x_in1")]
        y_sent = [sem("y_sent0"), sem("y_sent1")]
        pairs = lambda eng: eng.value_load(keep["tile_end"][0:1, N_EXPERTS:N_EXPERTS + 1], min_val=1, max_val=MAX_TILES // 2)

        with nc.Block() as block:

            @block.sync
            def _(sp):
                def issue(e, j, first):
                    if not first:
                        end = sp.value_load(keep["tile_end"][0:1, bass.ds(e - W_SLOTS, 1)], min_val=1, max_val=MAX_TILES)
                        sp.wait_ge(y_made, end)
                    at_ = lambda off, n: w[:, j * W + off:j * W + off + n]
                    for name, off, k in (("expert_w_gate", GATE, KT), ("expert_w_up", UP, KT), ("expert_w_down", DOWN, FK)):
                        n = KT * D_EXPERT
                        sp.dma_start(at_(off, n).rearrange("p (k n) -> p k n", k=k),
                                     d[name][0, bass.ds(e, 1), :, :].rearrange("a (k p) n -> p (a k) n", p=P)).then_inc(w_in[j], 16)

                def confirm(j, turn):
                    sp.wait_ge(w_in[j], 48 * (turn + 1))
                    sp.sem_inc(weights_ready, 1)

                for e in range(W_SLOTS):
                    issue(e, e, True)
                used = pairs(sp)
                sp.wait_ge(zeroed, 1)
                with sp.Fori(used, MAX_TILES // 2 + 1) as i:
                    sp.dma_start(d["y_slots"][bass.ds(2 * i * P, 2 * P), :].rearrange("(a p) d -> p a d", p=P),
                                 zero[:, :].unsqueeze(1).to_broadcast([P, 2, D_MODEL])).then_inc(filled, 16)
                confirm(0, 0)
                confirm(1, 0)
                rounds = N_EXPERTS // W_SLOTS
                with sp.Fori(1, rounds) as i:
                    for j in range(W_SLOTS):
                        issue(W_SLOTS * i + j, j, False)
                        confirm((j + W_SLOTS - 1) % W_SLOTS, i - 1 if j == 0 else i)
                for e in range(rounds * W_SLOTS, N_EXPERTS):
                    issue(e, e % W_SLOTS, False)
                    confirm((e - 1) % W_SLOTS, (e - 1) // W_SLOTS)
                confirm((N_EXPERTS - 1) % W_SLOTS, (N_EXPERTS - 1) // W_SLOTS)
                unused = sp.value_load(keep["tile_end"][0:1, N_EXPERTS + 1:N_EXPERTS + 2], min_val=1, max_val=MAX_TILES // 2)
                sp.wait_ge(filled, 16 * unused)
                sp.sem_inc(order, 1)

            @block.gpsimd
            def _(pool):
                def gather(t, b, turn):
                    pool.wait_ge(turned, t + 1)
                    pool.sem_inc(order, 1)
                    nc.gpsimd.tensor_copy(idc[:, b:b + 1], ids[:, bass.ds(t, 1)]).then_inc(idc_done, 1)
                    pool.wait_ge(idc_done, t + 1)
                    pool.sem_inc(order, 1)
                    nc.gpsimd.indirect_dma_start(out=xg[:, b, :], out_offset=None, in_=d["h2"],
                                                 in_offset=bass.IndirectOffsetOnAxis(ap=idc[:, b:b + 1], axis=0)).then_inc(x_in[b], 16)

                nc.gpsimd.memset(zero[:, :], 0.0).then_inc(zeroed, 1)
                gather(0, 0, 0)
                with pool.Fori(0, pairs(pool)) as i:
                    gather(2 * i + 1, 1, i)
                    gather(2 * i + 2, 0, i + 1)

            @block.tensor
            def _(pe):
                pe.sem_inc(turned, 2)

                def turn_x(t, b, turn):
                    pe.wait_ge(x_in[b], 16 * turn + 16)
                    pe.wait_ge(xt_ready, t + 1)
                    for k in range(KT):
                        last = nc.tensor.transpose(ps_t[:, k, :], xg[:, b, k * P:(k + 1) * P], ident[:, :])
                    last.then_inc(turned, 1)

                def rhs(slot, off):
                    return w[:, bass.ds(slot * W + off, 512)]

                def tile(t, b):
                    expert = pe.value_load(keep["tile_expert"][0:1, 0, bass.ds(t, 1)], min_val=0, max_val=N_EXPERTS - 1)
                    slot = pe.value_load(keep["tile_expert"][0:1, 1, bass.ds(t, 1)], min_val=0, max_val=W_SLOTS - 1)
                    pe.wait_ge(weights_ready, expert + 1)
                    pe.wait_ge(xt_ready, t + 2)
                    pe.wait_ge(a_done, t + 1)
                    for ps, off, made in ((ps_g, GATE, g_made), (ps_u, UP, u_made)):
                        for k in range(KT):
                            last = nc.tensor.matmul(ps[:, :], xt[:, b, k, :], rhs(slot, off + k * D_EXPERT), start=(k == 0), stop=(k == KT - 1))
                        last.then_inc(made, 1)
                    turn_x(t + 1, 1 - b, turn_of(t, b))
                    pe.wait_ge(a_done, t + 2)
                    for k in range(FK):
                        last = nc.tensor.transpose(ps_a[:, k, :], a[:, k * P:(k + 1) * P], ident[:, :])
                    last.then_inc(a_turned, 1)
                    pe.wait_ge(at_ready, t + 1)
                    pe.wait_ge(y_out, t + 1)
                    for half in range(2):
                        for k in range(FK):
                            last = nc.tensor.matmul(ps_y[:, half * 512:half * 512 + 512], at[:, k, :], rhs(slot, DOWN + k * D_MODEL + half * 512),
                                                    start=(k == 0), stop=(k == FK - 1))
                    last.then_inc(y_made, 1)

                turn_x(0, 0, 0)
                with pe.Fori(0, pairs(pe)) as i:
                    turn_of = lambda t, b: i + b
                    for b in range(2):
                        tile(2 * i + b, b)

            @block.scalar
            def _(act):
                act.sem_inc(xt_ready, 1)
                for q in y_sent:
                    act.sem_inc(q, 16)

                def take_x(t, b):
                    act.wait_ge(turned, t + 3)
                    nc.scalar.copy(xt[:, b, :, :], ps_t[:, :, :]).then_inc(xt_ready, 1)

                count = pairs(act)
                take_x(0, 0)
                with act.Fori(0, count) as i:
                    for b in range(2):
                        t = 2 * i + b
                        act.wait_ge(g_made, t + 1)
                        act.wait_ge(a_done, t + 1)
                        nc.scalar.activation(s[:, :], ps_g[:, :], ACT.Silu).then_inc(silu_done, 1)
                        act.wait_ge(a_turned, t + 1)
                        nc.scalar.copy(at[:, :, :], ps_a[:, :, :]).then_inc(at_ready, 1)
                        take_x(t + 1, 1 - b)
                        act.wait_ge(y_out, t + 2)
                        act.dma_start(d["y_slots"][bass.ds(t * P, P), :], y[:, b, :]).then_inc(y_sent[b], 16)
                for q in y_sent:
                    act.wait_ge(q, 16 * count + 16)
                    act.sem_inc(order, 1)

            @block.vector
            def _(dve):
                dve.sem_inc(a_done, 1)
                dve.sem_inc(y_out, 1)
                with dve.Fori(0, pairs(dve)) as i:
                    for b in range(2):
                        t = 2 * i + b
                        dve.wait_ge(silu_done, t + 1)
                        dve.wait_ge(u_made, t + 1)
                        nc.vector.tensor_tensor(a[:, :], s[:, :], ps_u[:, :], ALU.mult).then_inc(a_done, 1)
                        dve.wait_ge(y_made, t + 1)
                        dve.wait_ge(y_sent[b], 16 * i + 16)
                        nc.vector.tensor_copy(y[:, b, :], ps_y[:, :]).then_inc(y_out, 1)


def combine_and_norm(nc, d, keep):
    with ExitStack() as cx:
        sb = lambda n, s, t=F32: cx.enter_context(nc.sbuf_tensor("f9_" + n, s, t))
        sem = lambda n: cx.enter_context(nc.semaphore("f9_" + n))
        xt = sb("xt", [P, 2, D_MODEL])
        yg = sb("yg", [P, 2, 2, D_MODEL])
        o = sb("o", [P, 2, D_MODEL])
        sq = sb("sq", [P, 2, D_MODEL])
        gain = sb("gain", [P, D_MODEL])
        slc = sb("slc", [P, 2, 2], U32)
        gc = sb("gc", [P, 2, 2])
        sst = sb("sst", [P, 2, 3])
        cst = sb("cst", [P, 2])
        small_in, pool_steps, steps, combined, squared, mean, rstd, done = (sem(n) for n in (
            "small_in", "pool_steps", "steps", "combined", "squared", "mean", "rstd", "done"))
        x_in = [sem("x_in0"), sem("x_in1")]
        y_in = [sem("y_in0"), sem("y_in1")]
        sent = [sem("sent0"), sem("sent1")]
        last_tile = TOK_TILES - 1
        turns = TOK_TILES // 2
        order = keep["order"]
        STEPS = 2
        with nc.Block() as block:

            @block.sync
            def _(sp):
                sp.dma_start(gain[:, :], d["norm_final"].unsqueeze(0).to_broadcast([P, D_MODEL])).then_inc(small_in, 16)
                with sp.Fori(0, turns) as i:
                    for b in range(2):
                        t = 2 * i + b
                        sp.wait_ge(done, t + 1)
                        sp.dma_start(xt[:, b, :], d["x2"][bass.ds(t * P, P), :]).then_inc(x_in[b], 16)

            @block.gpsimd
            def _(pool):
                pool.sem_inc(rstd, 2)
                nc.gpsimd.memset(cst[:, 0:1], -0.5).then_inc(pool_steps, 1)
                nc.gpsimd.memset(cst[:, 1:2], RMS_EPS * D_MODEL).then_inc(pool_steps, 1)

                def gather(t, b, turn):
                    pool.wait_ge(combined, t + 1)
                    pool.sem_inc(order, 1)
                    nc.gpsimd.tensor_copy(slc[:, b, :], keep["slot"][:, bass.ds(t, 1), :].rearrange("p a k -> p (a k)")).then_inc(pool_steps, 1)
                    pool.wait_ge(pool_steps, t + 3)
                    pool.sem_inc(order, 1)
                    for k in range(2):
                        nc.gpsimd.indirect_dma_start(out=yg[:, b, k, :], out_offset=None, in_=d["y_slots"],
                                                     in_offset=bass.IndirectOffsetOnAxis(ap=slc[:, b, k:k + 1], axis=0)).then_inc(y_in[b], 16)

                def scale(t, b):
                    pool.wait_ge(squared, t + 1)
                    nc.gpsimd.tensor_tensor(sst[:, b, 1:2], sst[:, b, 0:1], cst[:, 1:2], ALU.add).then_inc(mean, 1)
                    pool.wait_ge(mean, t + 1)
                    pool.wait_ge(done, t + 1)
                    nc.gpsimd.tensor_tensor(sst[:, b, 2:3], sst[:, b, 1:2], cst[:, 0:1], ALU.pow).then_inc(rstd, 1)

                gather(0, 0, 0)
                gather(1, 1, 0)
                with pool.Fori(0, turns - 1) as i:
                    for b in range(2):
                        scale(2 * i + b, b)
                        gather(2 * i + b + 2, b, i + 1)
                scale(last_tile - 1, 0)
                scale(last_tile, 1)

            @block.scalar
            def _(act):
                for q in sent:
                    act.sem_inc(q, 16)

                def square(t, b):
                    act.wait_ge(combined, t + 3)
                    act.wait_ge(rstd, t + 1)
                    nc.scalar.activation(sq[:, b, :], xt[:, b, :], ACT.Square, accum_out=sst[:, b, 0:1]).then_inc(squared, 1)

                def store(t, b):
                    act.wait_ge(done, t + 3)
                    act.dma_start(d["out"][0, bass.ds(t * P, P), :], o[:, b, :]).then_inc(sent[b], 16)

                square(0, 0)
                with act.Fori(0, turns - 1) as i:
                    for b in range(2):
                        square(2 * i + b + 1, 1 - b)
                        store(2 * i + b, b)
                square(last_tile, 1)
                store(last_tile - 1, 0)
                store(last_tile, 1)
                for q in sent:
                    act.wait_ge(q, 16 * (turns + 1))

            @block.vector
            def _(dve):
                stt_ = nc.vector.scalar_tensor_tensor
                dve.sem_inc(done, 2)
                dve.sem_inc(combined, 2)
                dve.wait_ge(small_in, 16)
                nc.vector.tensor_scalar(gain[:, :], gain[:, :], math.sqrt(D_MODEL), None, ALU.mult).then_inc(steps, 1)

                def head(t, b, turn):
                    step = Chain(dve, steps, STEPS * t + 1)
                    step(nc.vector.tensor_copy(gc[:, b, :], keep["gates"][:, bass.ds(t, 1), :].rearrange("p a k -> p (a k)")))
                    dve.wait_ge(x_in[b], 16 * turn + 16)
                    dve.wait_ge(y_in[b], 32 * turn + 32)
                    step(stt_(xt[:, b, :], yg[:, b, 0, :], gc[:, b, 0:1], xt[:, b, :], ALU.mult, ALU.add))
                    stt_(xt[:, b, :], yg[:, b, 1, :], gc[:, b, 1:2], xt[:, b, :], ALU.mult, ALU.add).then_inc(combined, 1)

                def tail(t, b, turn):
                    dve.wait_ge(rstd, t + 3)
                    dve.wait_ge(sent[b], 16 * turn + 16)
                    stt_(o[:, b, :], xt[:, b, :], sst[:, b, 2:3], gain[:, :], ALU.mult, ALU.mult).then_inc(done, 1)

                head(0, 0, 0)
                with dve.Fori(0, turns - 1) as i:
                    for b in range(2):
                        head(2 * i + b + 1, 1 - b, i + b)
                        tail(2 * i + b, b, i)
                head(last_tile, 1, turns - 1)
                tail(last_tile - 1, 0, turns - 1)
                tail(last_tile, 1, turns - 1)


def hybrid_block(nc, d):
    with ExitStack() as cx:
        sb = lambda n, s, t=F32: cx.enter_context(nc.sbuf_tensor(n, s, t))
        ident = sb("ident", [P, P])
        s5_constants(nc, d, ident)
        with ExitStack() as hold:
            h_hi = hold.enter_context(nc.sbuf_tensor("h_hi", [P, KT, SEQ], F32R))
            h_lo = hold.enter_context(nc.sbuf_tensor("h_lo", [P, KT, SEQ], F32R))
            norm_and_turn(nc, d, ident, h_hi, h_lo)
            s5_inputs(nc, d, h_hi, h_lo)
            s5_scan(nc, d, ident)
            rg_lru(nc, d, h_hi, h_lo)
        mix_branches(nc, d)
        keep = {
            "ident": ident,
            "order": cx.enter_context(nc.semaphore("order")),
            "acc": sb("acc", [P, N_EXPERTS]),
            "chosen": sb("chosen", [P, TOK_TILES, 2, N_EXPERTS]),
            "gates": sb("gates", [P, TOK_TILES, 2]),
            "rank": sb("rank", [P, TOK_TILES, 2]),
            "slot": sb("slot", [P, TOK_TILES, 2], U32),
            "ids": sb("ids", [P, MAX_TILES + 2], U32),
            "tile_expert": sb("tile_expert", [1, 2, MAX_TILES], I32),
            "tile_end": sb("tile_end", [1, N_EXPERTS + 2], I32),
        }
        project_and_route(nc, d, keep)
        place_tokens(nc, d, keep)
        run_experts(nc, d, keep)
        combine_and_norm(nc, d, keep)


SCRATCH = {
    "s5_pack": ((CBS, P, PACK), F32),
    "h_t": ((2, D_MODEL, SEQ), F32),
    "u": ((CBS, P, CTS, CB_GROUPS * P), F32),
    "ys_t": ((2, S5_WIDTH, SEQ), F32),
    "yl_t": ((2, LRU_WIDTH, SEQ), F32),
    "mix_t": ((2, D_MODEL, SEQ), F32),
    "x2": ((SEQ, D_MODEL), F32),
    "h2": ((SEQ, D_MODEL), F32),
    "slot_tok": ((MAX_TILES * P, 1), I32),
    "y_slots": (((MAX_TILES + 2) * P, D_MODEL), F32),
}


def kernel(**inputs):
    import numpy as _np
    import concourse.bacc as _bacc
    from concourse import mybir as _mybir
    from concourse.bass_utils import run_bass_kernel_spmd as _run

    nc = _bacc.Bacc("TRN2", target_bir_lowering=False, num_devices=1)
    arrays, d = {}, {}
    for name in inputs:
        a = _np.ascontiguousarray(inputs[name])
        arrays[f"in_{name}_dram"] = a
        d[name] = nc.dram_tensor(f"in_{name}_dram", a.shape, _mybir.dt.from_np(a.dtype), kind="ExternalInput").ap()
    for name, (shape, dt) in SCRATCH.items():
        d[name] = nc.dram_tensor(name, shape, dt).ap()
    d["out"] = nc.dram_tensor("out_0_dram", (1, SEQ, D_MODEL), F32, kind="ExternalOutput").ap()
    hybrid_block(nc, d)
    r = _run(nc, [arrays], core_ids=[0])
    return r.results[0]["out_0_dram"]
```

```python
import math
from contextlib import ExitStack

import concourse.bass as bass
from concourse import mybir

F32 = mybir.dt.float32
F32R = mybir.dt.float32r
I32 = mybir.dt.int32
U32 = mybir.dt.uint32
ALU = mybir.AluOpType
ACT = mybir.ActivationFunctionType
AX = mybir.AxisListType

P = 128
D_MODEL = 1024
SEQ = 2048
KT = D_MODEL // P
TOK_TILES = SEQ // P
RMS_EPS = 1e-6
S5_WIDTH = D_MODEL // 2
S5_GROUP = 16
S5_GROUPS = S5_WIDTH // S5_GROUP
S5_STATE = 64
PAIRS = S5_GROUPS // 2
STEP = P // S5_GROUP
CHUNKS = SEQ // STEP
CTS = CHUNKS // P
CBS = S5_WIDTH // P
CB_PAIRS = PAIRS // CBS
CB_GROUPS = S5_GROUPS // CBS
LRU_WIDTH = D_MODEL
LRU_HEAD_DIM = 64
LRU_BLOCKS = LRU_WIDTH // P
CONV_WIDTH = 4
LRU_C = 8.0
N_GROUPS = 4
EXPERTS_PER_GROUP = 8
N_EXPERTS = N_GROUPS * EXPERTS_PER_GROUP
D_EXPERT = D_MODEL // 2
QUARTER = 512
QUARTERS = SEQ // QUARTER
O_LRU = S5_WIDTH
O_GATE = O_LRU + LRU_WIDTH
O_GA = O_GATE + LRU_WIDTH
O_GB = O_GA + D_MODEL
MAX_TILES = 2 * SEQ // P + N_EXPERTS
W_SLOTS = 2

PACK_W = 0
PACK_C = PACK_W + CB_PAIRS * 2 * P
PACK_T = PACK_C + CB_PAIRS * 2 * 2 * P
PACK_TAB = PACK_T + CB_GROUPS * P
PACK_DECAY = PACK_TAB + 2 * CB_PAIRS * CHUNKS
PACK = PACK_DECAY + CB_PAIRS


class Chain:

    def __init__(self, eng, sem, base=0):
        self.eng, self.sem, self.base, self.n = eng, sem, base, 0

    def __call__(self, ins):
        self.n += 1
        ins.then_inc(self.sem, 1)
        self.eng.wait_ge(self.sem, self.base + self.n)


def matmul3(nc, out, l_hi, l_lo, r_hi, r_lo, start, stop):
    nc.tensor.matmul(out, l_hi, r_hi, start=start, stop=False)
    nc.tensor.matmul(out, l_hi, r_lo, start=False, stop=False)
    return nc.tensor.matmul(out, l_lo, r_hi, start=False, stop=stop)


def columns(v, count):
    return v.rearrange("(c p) -> p c", p=P)


def s5_constants(nc, d, ident):
    with ExitStack() as cx:
        sb = lambda n, s, t=F32: cx.enter_context(nc.sbuf_tensor("c0_" + n, s, t))
        sem = lambda n: cx.enter_context(nc.semaphore("c0_" + n))
        lam = sb("lam", [P, 2, PAIRS])
        ldt = sb("ldt", [P, PAIRS])
        decay = sb("decay", [P, PAIRS])
        braw = sb("braw", [P, 2, PAIRS, S5_GROUP])
        craw = sb("craw", [P, 2, CBS, 2, S5_STATE])
        cl = sb("cl", [P, 2, PAIRS, S5_GROUP])
        sc = sb("sc", [P, 16, PAIRS])
        bb = sb("bb", [P, 2, PAIRS, S5_GROUP])
        pf = sb("pf", [P, 2, STEP + 1, PAIRS])
        pr = sb("pr", [P, 2, STEP, PAIRS])
        v = sb("v", [P, 2, PAIRS, STEP, S5_GROUP])
        t1 = sb("t1", [P, PAIRS * STEP * S5_GROUP + PAIRS * S5_GROUP])
        t2 = sb("t2", [P, PAIRS * STEP * S5_GROUP + PAIRS * S5_GROUP])
        crx = sb("crx", [P, PAIRS, 2, 2, STEP + 1, S5_GROUP])
        w = sb("w", [P, PAIRS, 2, P])
        kt = sb("kt", [S5_GROUP, S5_GROUPS, STEP, S5_GROUP])
        tt = sb("tt", [P, S5_GROUPS, P])
        tab = sb("tab", [P, 2, PAIRS, CHUNKS])
        dcol = sb("dcol", [S5_GROUP, S5_GROUPS])
        dd = sb("dd", [S5_GROUP, S5_GROUPS, S5_GROUP])
        ps_c = cx.enter_context(nc.psum_tensor("c0_ps_c", [P, 2, 512], F32))
        ps_w = cx.enter_context(nc.psum_tensor("c0_ps_w", [P, 2, 512], F32))
        ps_k = cx.enter_context(nc.psum_tensor("c0_ps_k", [S5_GROUP, 2, 512], F32))
        loaded, exps, sins, ident_ready = sem("loaded"), sem("exps"), sem("sins"), sem("ident_ready")
        zeroed, args_ready, chain = sem("zeroed"), sem("args_ready"), sem("chain")
        c_turned, c_lanes, v_ready, w_turned, w_ready = (sem(n) for n in
            ("c_turned", "c_lanes", "v_ready", "w_turned", "w_ready"))
        k_rhs, k_made, k_ready, k_placed, stored, packed = (sem(n) for n in
            ("k_rhs", "k_made", "k_ready", "k_placed", "stored", "packed"))
        INPUTS = 16 * 11
        (DT, ZR, ZI, ER, CO, SI, RA, RB, MR, MI, WR, WI, X1, X2, X3, X4) = range(16)

        with nc.Block() as block:

            @block.sync
            def _(sp):
                with nc.allow_non_contiguous_dma(reason="small parameters, one word a lane"):
                    for j, name in enumerate(("s5_lam_re", "s5_lam_im")):
                        sp.dma_start(lam[:, j, :], d[name][0].rearrange("(q r) p -> (r p) q", r=2)).then_inc(loaded, 16)
                    for r in range(2):
                        sp.dma_start(ldt[64 * r:64 * r + 64, :],
                                     d["s5_log_dt"][0].rearrange("(q r) -> r q", r=2)[r:r + 1, :].to_broadcast([64, PAIRS])
                                     ).then_inc(loaded, 16)
                    for j, name in enumerate(("s5_b_re", "s5_b_im")):
                        sp.dma_start(braw[:, j, :, :], d[name][0].rearrange("(q r) p c -> (r p) q c", r=2)).then_inc(loaded, 16)
                    for j, name in enumerate(("s5_c_re", "s5_c_im")):
                        for dup in range(2):
                            sp.dma_start(craw[:, j, :, dup, :],
                                         d[name][0].rearrange("(b g) c p -> (g c) b p", b=CBS)).then_inc(loaded, 16)
                    sp.dma_start(dcol[:, :], d["s5_d"][0].rearrange("(g c) -> c g", c=S5_GROUP)).then_inc(loaded, 16)
                sp.wait_ge(k_ready, 1)
                sp.wait_ge(zeroed, 2)
                for s in range(STEP):
                    sp.dma_start(tt[s * S5_GROUP:(s + 1) * S5_GROUP, :, s * S5_GROUP:],
                                 kt[:, :, 0:STEP - s, :].rearrange("p g t c -> p g (t c)")).then_inc(k_placed, 16)
                sp.wait_ge(w_ready, 8)
                sp.wait_ge(k_placed, 16 * STEP)
                sp.wait_ge(packed, 1)
                for b in range(CBS):
                    dst = d["s5_pack"][b]
                    q = slice(b * CB_PAIRS, (b + 1) * CB_PAIRS)
                    sp.dma_start(dst[:, PACK_W:PACK_C], w[:, q, :, :].rearrange("p q j m -> p (q j m)")).then_inc(stored, 16)
                    sp.dma_start(dst[:, PACK_C:PACK_T].rearrange("p (k m) -> p k m", m=P),
                                 crx[:, q, :, :, 1:, :].rearrange("p q j r t c -> p (q j r) (t c)")).then_inc(stored, 16)
                    sp.dma_start(dst[:, PACK_T:PACK_TAB],
                                 tt[:, b * CB_GROUPS:(b + 1) * CB_GROUPS, :].rearrange("p g m -> p (g m)")).then_inc(stored, 16)
                    sp.dma_start(dst[:, PACK_TAB:PACK_DECAY].rearrange("p (j m) -> p j m", j=2),
                                 tab[:, :, q, :].rearrange("p j q m -> p j (q m)")).then_inc(stored, 16)
                    sp.dma_start(dst[:, PACK_DECAY:PACK], decay[:, q]).then_inc(stored, 16)
                sp.wait_ge(stored, 16 * 5 * CBS)

            @block.gpsimd
            def _(pool):
                nc.gpsimd.memset(ident[:, :], 0.0).then_inc(zeroed, 1)
                pool.wait_ge(zeroed, 1)
                nc.gpsimd.affine_select(out=ident[:, :], in_=ident[:, :], compare_op=ALU.not_equal, fill=1.0,
                                        base=0, pattern=[[-1, P]], channel_multiplier=1).then_inc(ident_ready, 1)
                nc.gpsimd.memset(tt[:, :, :], 0.0).then_inc(zeroed, 1)
                nc.gpsimd.memset(crx[:, :, :, :, :, :], 0.0).then_inc(zeroed, 1)

            @block.scalar
            def _(act):
                act.wait_ge(loaded, INPUTS - 32)
                act.wait_ge(loaded, INPUTS)
                nc.scalar.activation(sc[:, DT, :], ldt[:, :], ACT.Exp).then_inc(exps, 1)
                act.wait_ge(args_ready, 1)
                nc.scalar.activation(sc[:, ER, :], sc[:, ZR, :], ACT.Exp).then_inc(exps, 1)
                nc.scalar.activation(decay[:, :], sc[:, ZR, :], ACT.Exp, scale=float(STEP)).then_inc(exps, 1)
                nc.scalar.activation(sc[:, SI, :], sc[:, RA, :], ACT.Sin).then_inc(sins, 1)
                nc.scalar.activation(sc[:, CO, :], sc[:, RB, :], ACT.Sin).then_inc(sins, 1)
                act.wait_ge(c_turned, 1)
                for b in range(CBS):
                    for j in range(2):
                        src = ps_c[:, j, b * P:(b + 1) * P].rearrange("p (q r c) -> p q r c", r=2, c=S5_GROUP)
                        for r in range(2):
                            rows = slice(64 * r, 64 * r + 64)
                            nc.scalar.copy(cl[rows, j, b * CB_PAIRS:(b + 1) * CB_PAIRS, :], src[rows, :, r, :]).then_inc(c_lanes, 1)

            @block.tensor
            def _(pe):
                pe.wait_ge(ident_ready, 1)
                pe.wait_ge(loaded, INPUTS)
                for j in range(2):
                    for b in range(CBS):
                        last = nc.tensor.transpose(ps_c[:, j, b * P:(b + 1) * P],
                                                   craw[:, j, b, :, :].rearrange("p r s -> p (r s)"), ident[:, :])
                last.then_inc(c_turned, 1)
                pe.wait_ge(v_ready, 1)
                for i in range(PAIRS // 2):
                    if i >= 2:
                        pe.wait_ge(w_ready, i - 1)
                    for q in (2 * i, 2 * i + 1):
                        for j in range(2):
                            last = nc.tensor.transpose(ps_w[:, i % 2, ((q % 2) * 2 + j) * P:((q % 2) * 2 + j + 1) * P],
                                                       v[:, j, q, :, :].rearrange("p t c -> p (t c)"), ident[:, :])
                    last.then_inc(w_turned, 1)
                pe.wait_ge(k_rhs, 1)
                for i in range(PAIRS // 2):
                    if i >= 2:
                        pe.wait_ge(k_made, i - 1)
                    for q in (2 * i, 2 * i + 1):
                        for j in range(2):
                            last = nc.tensor.matmul(ps_k[:, i % 2, (q % 2) * 256:(q % 2) * 256 + 256], bb[:, j, q, :],
                                                    crx[:, q, j, :, 0:STEP, :],
                                                    start=(j == 0), stop=(j == 1))
                    last.then_inc(w_turned, 1)

            @block.vector
            def _(dve):
                step = Chain(dve, chain)
                tt_ = nc.vector.tensor_tensor
                ts_ = nc.vector.tensor_scalar

                def cmul(o_re, o_im, a_re, a_im, b_re, b_im, x, y):
                    step(tt_(x, a_re, b_re, ALU.mult))
                    step(tt_(y, a_im, b_im, ALU.mult))
                    step(tt_(o_re, x, y, ALU.subtract))
                    step(tt_(x, a_re, b_im, ALU.mult))
                    step(tt_(y, a_im, b_re, ALU.mult))
                    step(tt_(o_im, x, y, ALU.add))

                s = lambda i: sc[:, i, :]
                dve.wait_ge(loaded, INPUTS)
                dve.wait_ge(exps, 1)
                step(tt_(s(ZR), lam[:, 0, :], s(DT), ALU.mult))
                step(tt_(s(ZI), lam[:, 1, :], s(DT), ALU.mult))
                magic, inv = 1.5 * 2.0 ** 23, 1.0 / (2 * math.pi)
                c1, c2 = 6.28125, 0.0019350051879882812
                c3 = 2 * math.pi - c1 - c2
                for out, turn in ((RA, 0.0), (RB, 0.25)):
                    step(ts_(s(X1), s(ZI), inv, turn, ALU.mult, ALU.add))
                    step(ts_(s(X2), s(X1), magic, None, ALU.add))
                    step(ts_(s(X1), s(X2), magic, None, ALU.subtract))
                    for n, part in enumerate((c1, c2, c3)):
                        step(nc.vector.scalar_tensor_tensor(s(X2), s(X1), -part, s(ZI) if n == 0 else s(X2), ALU.mult, ALU.add))
                    step(ts_(s(X2), s(X2), turn * 2 * math.pi, 3.1415925, ALU.add, ALU.min))
                    step(ts_(s(out), s(X2), -3.1415925, None, ALU.max))
                nc.vector.tensor_copy(s(X3), s(ZI)).then_inc(args_ready, 1)
                dve.wait_ge(exps, 3)
                dve.wait_ge(sins, 2)
                step(nc.vector.memset(pf[:, 0, 0, :], 1.0))
                step(nc.vector.memset(pf[:, 1, 0, :], 0.0))
                step(tt_(pf[:, 0, 1, :], s(ER), s(CO), ALU.mult))
                step(tt_(pf[:, 1, 1, :], s(ER), s(SI), ALU.mult))
                for n in range(2, STEP + 1):
                    h, k = n // 2, n - n // 2
                    cmul(pf[:, 0, n, :], pf[:, 1, n, :], pf[:, 0, h, :], pf[:, 1, h, :], pf[:, 0, k, :], pf[:, 1, k, :], s(X1), s(X2))
                for n in range(STEP):
                    step(nc.vector.tensor_copy(pr[:, :, n, :], pf[:, :, STEP - 1 - n, :]))
                step(tt_(s(X1), lam[:, 0, :], lam[:, 0, :], ALU.mult))
                step(tt_(s(X2), lam[:, 1, :], lam[:, 1, :], ALU.mult))
                step(tt_(s(X3), s(X1), s(X2), ALU.add))
                step(nc.vector.reciprocal(s(X4), s(X3)))
                step(tt_(s(MR), lam[:, 0, :], s(X4), ALU.mult))
                step(tt_(s(X3), lam[:, 1, :], s(X4), ALU.mult))
                step(ts_(s(MI), s(X3), -1.0, None, ALU.mult))
                step(ts_(s(X4), pf[:, 0, 1, :], -1.0, None, ALU.add))
                cmul(s(WR), s(WI), s(X4), pf[:, 1, 1, :], s(MR), s(MI), s(X1), s(X2))
                wide = lambda a, shape: a.unsqueeze(len(shape) - 1).to_broadcast(shape)
                small = [P, PAIRS, S5_GROUP]
                x3 = t1[:, 0:PAIRS * S5_GROUP].rearrange("p (q c) -> p q c", q=PAIRS)
                y3 = t2[:, 0:PAIRS * S5_GROUP].rearrange("p (q c) -> p q c", q=PAIRS)
                cmul(bb[:, 0], bb[:, 1], wide(s(WR), small), wide(s(WI), small), braw[:, 0], braw[:, 1], x3, y3)
                big = [P, STEP, PAIRS, S5_GROUP]
                vt = lambda j: v[:, j].rearrange("p q t c -> p t q c")
                bw = lambda j: bb[:, j].unsqueeze(1).to_broadcast(big)
                x4 = t1[:, 0:PAIRS * P].rearrange("p (t q c) -> p t q c", t=STEP, q=PAIRS)
                y4 = t2[:, 0:PAIRS * P].rearrange("p (t q c) -> p t q c", t=STEP, q=PAIRS)
                cmul(vt(0), vt(1), wide(pr[:, 0], big), wide(pr[:, 1], big), bw(0), bw(1), x4, y4)
                nc.vector.tensor_copy(s(X1), s(X2)).then_inc(v_ready, 1)
                dve.wait_ge(c_lanes, 4 * CBS)
                dve.wait_ge(zeroed, 3)
                for r in range(2):
                    rows = slice(64 * r, 64 * r + 64)
                    shp = [64, STEP + 1, PAIRS, S5_GROUP]
                    x5 = t1[rows, :].rearrange("p (t q c) -> p t q c", t=STEP + 1, q=PAIRS)
                    y5 = t2[rows, :].rearrange("p (t q c) -> p t q c", t=STEP + 1, q=PAIRS)
                    o = lambda j: crx[rows, :, j, r].rearrange("p q t c -> p t q c")
                    pw = lambda j: pf[rows, j].unsqueeze(3).to_broadcast(shp)
                    cc = lambda j: cl[rows, j].unsqueeze(1).to_broadcast(shp)
                    step(tt_(x5, pw(0), cc(0), ALU.mult))
                    step(tt_(y5, pw(1), cc(1), ALU.mult))
                    step(tt_(o(0), x5, y5, ALU.subtract))
                    step(tt_(x5, pw(0), cc(1), ALU.mult))
                    step(tt_(y5, pw(1), cc(0), ALU.mult))
                    step(tt_(x5, x5, y5, ALU.add))
                    step(ts_(o(1), x5, -1.0, None, ALU.mult))
                nc.vector.tensor_copy(s(X1), s(X2)).then_inc(k_rhs, 1)
                for i in range(PAIRS // 2):
                    dve.wait_ge(w_turned, i + 1)
                    nc.vector.tensor_copy(w[:, 2 * i:2 * i + 2, :, :].rearrange("p q j m -> p (q j m)"), ps_w[:, i % 2, :]).then_inc(w_ready, 1)
                for i in range(PAIRS // 2):
                    dve.wait_ge(w_turned, PAIRS // 2 + i + 1)
                    nc.vector.tensor_copy(kt[:, 4 * i:4 * i + 4, :, :].rearrange("p g t c -> p (g t c)"),
                                          ps_k[:, i % 2, :]).then_inc(k_made, 1)
                dve.wait_ge(k_made, PAIRS // 2)
                dshape = [S5_GROUP, S5_GROUPS, S5_GROUP]
                step(tt_(dd[:, :, :], dcol[:, :].unsqueeze(2).to_broadcast(dshape),
                         ident[0:S5_GROUP, 0:S5_GROUP].unsqueeze(1).to_broadcast(dshape), ALU.mult))
                tt_(kt[:, :, 0, :], kt[:, :, 0, :], dd[:, :, :], ALU.add).then_inc(k_ready, 1)
                cmul(s(MR), s(MI), s(CO), s(SI), s(CO), s(SI), s(X1), s(X2))
                cmul(s(WR), s(WI), s(MR), s(MI), s(MR), s(MI), s(X1), s(X2))
                cmul(s(MR), s(MI), s(WR), s(WI), s(WR), s(WI), s(X1), s(X2))
                step(nc.vector.memset(tab[:, 0, :, 0:1], 1.0))
                step(nc.vector.memset(tab[:, 1, :, 0:1], 0.0))
                m = 1
                while m < CHUNKS:
                    shp = [P, PAIRS, m]
                    x6 = t1[:, 0:PAIRS * m].rearrange("p (q m) -> p q m", m=m)
                    y6 = t2[:, 0:PAIRS * m].rearrange("p (q m) -> p q m", m=m)
                    cmul(tab[:, 0, :, m:2 * m], tab[:, 1, :, m:2 * m], tab[:, 0, :, 0:m], tab[:, 1, :, 0:m],
                         wide(s(MR), shp), wide(s(MI), shp), x6, y6)
                    if 2 * m < CHUNKS:
                        cmul(s(WR), s(WI), s(MR), s(MI), s(MR), s(MI), s(X1), s(X2))
                        step(nc.vector.tensor_copy(s(MR), s(WR)))
                        step(nc.vector.tensor_copy(s(MI), s(WI)))
                    m *= 2
                nc.vector.tensor_copy(s(X1), s(X2)).then_inc(packed, 1)


def norm_and_turn(nc, d, ident, h_hi, h_lo):
    with ExitStack() as cx:
        sb = lambda n, s, t=F32: cx.enter_context(nc.sbuf_tensor("n1_" + n, s, t))
        sem = lambda n: cx.enter_context(nc.semaphore("n1_" + n))
        xin = sb("xin", [P, 2, D_MODEL])
        xn = sb("xn", [P, 2, D_MODEL])
        hs = sb("hs", [P, 2, KT, P])
        sq = sb("sq", [P, 2, D_MODEL])
        ss = sb("ss", [P, 2])
        ms = sb("ms", [P, 2])
        rs = sb("rs", [P, 2])
        gain = sb("gain", [P, KT])
        half = sb("half", [P, 2])
        pst = cx.enter_context(nc.psum_tensor("n1_pst", [P, 2, KT, P], F32))
        gain_in, squared, mean, rstd, normed, turned, gained, high, split = (sem(n) for n in
            ("gain_in", "squared", "mean", "rstd", "normed", "turned", "gained", "high", "split"))
        x_in = [sem("x_in0"), sem("x_in1")]
        last = TOK_TILES - 1
        with nc.Block() as block:

            @block.sync
            def _(sp):
                with nc.allow_non_contiguous_dma(reason="one gain a partition"):
                    sp.dma_start(gain[:, :], columns(d["norm_mix"][0], KT)).then_inc(gain_in, 16)
                with sp.Fori(0, TOK_TILES // 2) as i:
                    for b in range(2):
                        sp.wait_ge(normed, 2 * i + b + 1)
                        sp.dma_start(xin[:, b, :], d["x"][0, bass.ds((2 * i + b) * P, P), :]).then_inc(x_in[b], 16)

            @block.scalar
            def _(act):
                act.sem_inc(high, 2)

                def square(t, b, turn):
                    act.wait_ge(x_in[b], 16 * (turn + 1))
                    act.wait_ge(rstd, t + 1)
                    nc.scalar.activation(sq[:, b, :], xin[:, b, :], ACT.Square, accum_out=ss[:, b:b + 1]).then_inc(squared, 1)

                def take_high(t, b):
                    act.wait_ge(gained, t + 3)
                    nc.scalar.copy(h_hi[:, :, bass.ds(t * P, P)], hs[:, b, :, :]).then_inc(high, 1)

                square(0, 0, 0)
                with act.Fori(0, TOK_TILES // 2 - 1) as i:
                    for b in range(2):
                        square(2 * i + b + 1, 1 - b, i + b)
                        take_high(2 * i + b, b)
                square(last, 1, TOK_TILES // 2 - 1)
                take_high(last - 1, 0)
                take_high(last, 1)

            @block.gpsimd
            def _(pool):
                pool.sem_inc(rstd, 2)
                nc.gpsimd.memset(half[:, 0:1], -0.5).then_inc(mean, 1)
                nc.gpsimd.memset(half[:, 1:2], RMS_EPS * D_MODEL).then_inc(mean, 1)
                pool.wait_ge(mean, 2)
                with pool.Fori(0, TOK_TILES // 2) as i:
                    for b in range(2):
                        t = 2 * i + b
                        pool.wait_ge(squared, t + 1)
                        nc.gpsimd.tensor_tensor(ms[:, b:b + 1], ss[:, b:b + 1], half[:, 1:2], ALU.add).then_inc(mean, 1)
                        pool.wait_ge(mean, t + 3)
                        pool.wait_ge(normed, t + 1)
                        nc.gpsimd.tensor_tensor(rs[:, b:b + 1], ms[:, b:b + 1], half[:, 0:1], ALU.pow).then_inc(rstd, 1)

            @block.tensor
            def _(pe):
                pe.sem_inc(turned, 2)
                with pe.Fori(0, TOK_TILES // 2) as i:
                    for b in range(2):
                        t = 2 * i + b
                        pe.wait_ge(normed, t + 3)
                        pe.wait_ge(gained, t + 1)
                        for k in range(KT):
                            done = nc.tensor.transpose(pst[:, b, k, :], xn[:, b, k * P:(k + 1) * P], ident[:, :])
                        done.then_inc(turned, 1)

            @block.vector
            def _(dve):
                dve.sem_inc(normed, 2)
                dve.sem_inc(gained, 2)
                dve.wait_ge(gain_in, 16)

                def norm(t, b):
                    dve.wait_ge(rstd, t + 3)
                    dve.wait_ge(turned, t + 1)
                    nc.vector.tensor_scalar(xn[:, b, :], xin[:, b, :], rs[:, b:b + 1], math.sqrt(D_MODEL), ALU.mult, ALU.mult).then_inc(normed, 1)

                def gain_and_split(t, b):
                    dve.wait_ge(turned, t + 3)
                    dve.wait_ge(high, t + 1)
                    nc.vector.tensor_tensor(hs[:, b, :, :], pst[:, b, :, :],
                                            gain[:, :].unsqueeze(2).to_broadcast([P, KT, P]), ALU.mult).then_inc(gained, 1)
                    dve.wait_ge(high, t + 3)
                    nc.vector.tensor_tensor(h_lo[:, :, bass.ds(t * P, P)], hs[:, b, :, :],
                                            h_hi[:, :, bass.ds(t * P, P)].bitcast(F32), ALU.subtract).then_inc(split, 1)

                norm(0, 0)
                with dve.Fori(0, TOK_TILES // 2 - 1) as i:
                    for b in range(2):
                        norm(2 * i + b + 1, 1 - b)
                        gain_and_split(2 * i + b, b)
                norm(last, 1)
                gain_and_split(last - 1, 0)
                gain_and_split(last, 1)


def s5_inputs(nc, d, h_hi, h_lo):
    with ExitStack() as cx:
        sb = lambda n, s, t=F32: cx.enter_context(nc.sbuf_tensor("u2_" + n, s, t))
        sem = lambda n: cx.enter_context(nc.semaphore("u2_" + n))
        raw = sb("raw", [P, 2, S5_WIDTH])
        w_hi = sb("w_hi", [P, KT, S5_WIDTH], F32R)
        w_lo = sb("w_lo", [P, KT, S5_WIDTH], F32R)
        u = sb("u", [P, CTS, S5_GROUPS, STEP, S5_GROUP])
        ps = cx.enter_context(nc.psum_tensor("u2_ps", [P, 4, S5_WIDTH], F32))
        w_split, made, taken, stored, high, h_sent = (sem(n) for n in ("w_split", "made", "taken", "stored", "high", "h_sent"))
        w_in = [sem("w_in0"), sem("w_in1")]
        hv = [h[:, :, :].rearrange("p k (a m t) -> p k a t m", a=CTS, t=STEP) for h in (h_hi, h_lo)]
        with nc.Block() as block:

            @block.sync
            def _(sp):
                for k in range(KT):
                    if k >= 2:
                        sp.wait_ge(w_split, k - 1)
                    sp.dma_start(raw[:, k % 2, :], d["w_in"][0, k * P:(k + 1) * P, 0:S5_WIDTH]).then_inc(w_in[k % 2], 16)
                for a, h in ((0, h_hi), (1, h_lo)):
                    for k in range(KT):
                        sp.dma_start(d["h_t"][a, k * P:(k + 1) * P, :], h[:, k, :].bitcast(F32)).then_inc(h_sent, 16)
                for a in range(CTS):
                    sp.wait_ge(taken, STEP * (a + 1))
                    for b in range(CBS):
                        sp.dma_start(d["u"][b, :, a, :], u[:, a, b * CB_GROUPS:(b + 1) * CB_GROUPS, :, :].rearrange("p g t c -> p (g t c)")
                                     ).then_inc(stored, 16)
                sp.wait_ge(stored, 16 * CTS * CBS)
                sp.wait_ge(h_sent, 16 * 2 * KT)

            @block.vector
            def _(dve):
                for k in range(KT):
                    dve.wait_ge(w_in[k % 2], 16 * (k // 2 + 1))
                    nc.vector.tensor_copy(w_hi[:, k, :], raw[:, k % 2, :]).then_inc(high, 1)
                    dve.wait_ge(high, k + 1)
                    nc.vector.tensor_tensor(w_lo[:, k, :], raw[:, k % 2, :], w_hi[:, k, :].bitcast(F32), ALU.subtract).then_inc(w_split, 1)

            @block.tensor
            def _(pe):
                n = 0
                for a in range(CTS):
                    for t in range(STEP):
                        if n >= 4:
                            pe.wait_ge(taken, n - 3)
                        for k in range(KT):
                            if n == 0:
                                pe.wait_ge(w_split, k + 1)
                            last = matmul3(nc, ps[:, n % 4, :], hv[0][:, k, a, t, :], hv[1][:, k, a, t, :],
                                           w_hi[:, k, :], w_lo[:, k, :], k == 0, k == KT - 1)
                        last.then_inc(made, 1)
                        n += 1

            @block.scalar
            def _(act):
                for n in range(CTS * STEP):
                    act.wait_ge(made, n + 1)
                    nc.scalar.copy(u[:, n // STEP, :, n % STEP, :], ps[:, n % 4, :].rearrange("p (g c) -> p g c", c=S5_GROUP)).then_inc(taken, 1)


def s5_scan(nc, d, ident):
    with ExitStack() as cx:
        sb = lambda n, s, t=F32: cx.enter_context(nc.sbuf_tensor("s3_" + n, s, t))
        sem = lambda n: cx.enter_context(nc.semaphore("s3_" + n))
        pack = sb("pack", [P, PACK])
        uy = sb("uy", [P, CTS, CB_GROUPS * P])
        ut = sb("ut", [P, CB_GROUPS, CHUNKS])
        state = sb("state", [P, 2, CB_PAIRS, CHUNKS])
        scanned = sb("scanned", [P, 2, CB_PAIRS, CHUNKS])
        t1 = sb("t1", [P, CB_PAIRS, CHUNKS])
        t2 = sb("t2", [P, CB_PAIRS, CHUNKS])
        out_hi = sb("out_hi", [P, P, STEP], F32R)
        out_lo = sb("out_lo", [P, P, STEP], F32R)
        ps_t = cx.enter_context(nc.psum_tensor("s3_ps_t", [P, 2, 4, P], F32))
        ps_x = cx.enter_context(nc.psum_tensor("s3_ps_x", [P, CB_PAIRS, 2, CHUNKS], F32))
        ps_y = cx.enter_context(nc.psum_tensor("s3_ps_y", [P, 2, 512], F32))
        (loaded, turned, ut_ready, x_made, dve_steps, y_made, y_ready, high, low, sent) = (sem(n) for n in
            ("loaded", "turned", "ut_ready", "x_made", "dve_steps", "y_made", "y_ready", "high", "low", "sent"))
        w = pack[:, PACK_W:PACK_C].rearrange("p (q j m) -> p q j m", q=CB_PAIRS, j=2)
        cm = pack[:, PACK_C:PACK_T].rearrange("p (q j m) -> p q j m", q=CB_PAIRS, j=2)
        tm = pack[:, PACK_T:PACK_TAB].rearrange("p (g m) -> p g m", g=CB_GROUPS)
        tab = pack[:, PACK_TAB:PACK_DECAY].rearrange("p (j q m) -> p j q m", j=2, q=CB_PAIRS)
        decay = pack[:, PACK_DECAY:PACK]
        DVE_STEPS = 6 + 2 * CB_PAIRS + 6
        with nc.Block() as block:

            @block.sync
            def _(sp):
                sp.sem_inc(sent, 32)
                with sp.Fori(0, CBS) as i:
                    sp.wait_ge(low, 4 * i + 4)
                    sp.dma_start(pack[:, :], d["s5_pack"][bass.ds(i, 1), :, :].rearrange("a p n -> (a p) n")).then_inc(loaded, 16)
                    sp.dma_start(uy[:, :, :], d["u"][bass.ds(i, 1), :, :, :].rearrange("a p t n -> (a p) t n")).then_inc(loaded, 16)
                    for a in range(CTS):
                        sp.wait_ge(low, 4 * i + 2 * a + 6)
                        for j, o in enumerate((out_hi, out_lo)):
                            sp.dma_start(d["ys_t"][j, bass.ds(i * P, P), a * P * STEP:(a + 1) * P * STEP],
                                         o[:, :, :].rearrange("p m t -> p (m t)").bitcast(F32)).then_inc(sent, 16)
                sp.wait_ge(sent, 32 + 64 * CBS)

            @block.tensor
            def _(pe):
                with pe.Fori(0, CBS) as i:
                    pe.wait_ge(loaded, 32 * (i + 1))
                    for j in range(4):
                        if j >= 2:
                            pe.wait_ge(ut_ready, 4 * i + j - 1)
                        for g in range(2):
                            for a in range(CTS):
                                last = nc.tensor.transpose(ps_t[:, j % 2, 2 * g + a, :],
                                                           uy[:, a, (2 * j + g) * P:(2 * j + g + 1) * P], ident[:, :])
                        last.then_inc(turned, 1)
                    for q in range(CB_PAIRS):
                        pe.wait_ge(ut_ready, 4 * i + q + 1)
                        for j in range(2):
                            for r in range(2):
                                last = nc.tensor.matmul(ps_x[64 * r:64 * r + 64, q, j, :], w[:, q, j, 64 * r:64 * r + 64],
                                                        ut[:, 2 * q + r, :], start=True, stop=True)
                    last.then_inc(x_made, 1)
                    pe.wait_ge(dve_steps, DVE_STEPS * (i + 1) + 2)
                    for a in range(CTS):
                        for h in range(2):
                            n = 2 * a + h
                            if n >= 2:
                                pe.wait_ge(y_ready, 4 * i + n - 1)
                            for q in (2 * h, 2 * h + 1):
                                o = ps_y[:, h, (q % 2) * 256:(q % 2) * 256 + 256]
                                for j in range(2):
                                    nc.tensor.matmul(o, state[:, j, q, a * P:(a + 1) * P], cm[:, q, j, :], start=(j == 0), stop=False)
                                for r in range(2):
                                    last = nc.tensor.matmul(o[:, r * P:(r + 1) * P], ut[:, 2 * q + r, a * P:(a + 1) * P],
                                                            tm[:, 2 * q + r, :], start=False, stop=(r == 1))
                            last.then_inc(y_made, 1)
                    for a in range(CTS):
                        pe.wait_ge(y_ready, 4 * i + 2 * a + 2)
                        for h in range(2):
                            n = 2 * a + h
                            if n >= 2:
                                pe.wait_ge(low, 4 * i + n + 3)
                            for t in range(4):
                                last = nc.tensor.transpose(ps_t[:, n % 2, t, :],
                                                           uy[:, a, (4 * h + t) * P:(4 * h + t + 1) * P],
                                                           ident[:, :])
                            last.then_inc(turned, 1)

            @block.scalar
            def _(act):
                with act.Fori(0, CBS) as i:
                    for j in range(4):
                        act.wait_ge(turned, 8 * i + j + 1)
                        nc.scalar.copy(ut[:, 2 * j:2 * j + 2, :], ps_t[:, j % 2, :, :].rearrange("p (g a) m -> p g (a m)", g=2)).then_inc(ut_ready, 1)
                    for a in range(CTS):
                        for h in range(2):
                            act.wait_ge(y_made, 4 * i + 2 * a + h + 1)
                            nc.scalar.activation(uy[:, a, :].rearrange("p (t g c) -> p g t c", t=STEP, g=CB_GROUPS)[:, 4 * h:4 * h + 4],
                                                 ps_y[:, h, :].rearrange("p (g t c) -> p g t c", g=4, t=STEP), ACT.Gelu_apprx_tanh).then_inc(y_ready, 1)
                    for a in range(CTS):
                        for h in range(2):
                            n = 2 * a + h
                            act.wait_ge(turned, 8 * i + 4 + n + 1)
                            if h == 0:
                                act.wait_ge(sent, 64 * i + 32 * a + 32)
                            nc.scalar.copy(out_hi[:, :, 4 * h:4 * h + 4].rearrange("p m t -> p t m"), ps_t[:, n % 2, :, :]).then_inc(high, 1)

            @block.vector
            def _(dve):
                tt_ = nc.vector.tensor_tensor
                dve.sem_inc(low, 4)
                first = Chain(dve, dve_steps)
                for j in range(2):
                    first(nc.vector.memset(scanned[:, j, :, 0:1], 0.0))
                with dve.Fori(0, CBS) as i:
                    step = Chain(dve, dve_steps, base=DVE_STEPS * i + 2)
                    dve.wait_ge(loaded, 32 * (i + 1))
                    dve.wait_ge(x_made, i + 1)
                    n1 = CHUNKS - 1
                    re, im = (ps_x[:, :, j, 0:n1] for j in range(2))
                    co, si = (tab[:, j, :, 1:CHUNKS] for j in range(2))
                    a, b = t1[:, :, 0:n1], t2[:, :, 0:n1]
                    step(tt_(a, co, re, ALU.mult))
                    step(tt_(b, si, im, ALU.mult))
                    step(tt_(state[:, 0, :, 1:], a, b, ALU.add))
                    step(tt_(a, co, im, ALU.mult))
                    step(tt_(b, si, re, ALU.mult))
                    step(tt_(state[:, 1, :, 1:], a, b, ALU.subtract))
                    for j in range(2):
                        for q in range(CB_PAIRS):
                            step(nc.vector.tensor_tensor_scan(scanned[:, j, q, 1:], decay[:, q:q + 1].to_broadcast([P, n1]),
                                                              state[:, j, q, 1:], 0.0, ALU.mult, ALU.add))
                    re, im = (scanned[:, j, :, :] for j in range(2))
                    co, si = (tab[:, j, :, :] for j in range(2))
                    a, b = t1[:, :, :], t2[:, :, :]
                    step(tt_(a, co, re, ALU.mult))
                    step(tt_(b, si, im, ALU.mult))
                    step(tt_(state[:, 0], a, b, ALU.subtract))
                    step(tt_(a, co, im, ALU.mult))
                    step(tt_(b, si, re, ALU.mult))
                    step(tt_(state[:, 1], a, b, ALU.add))
                    for n in range(4):
                        dve.wait_ge(high, 4 * i + n + 1)
                        h = n % 2
                        tt_(out_lo[:, :, 4 * h:4 * h + 4].rearrange("p m t -> p t m"), ps_t[:, n % 2, :, :],
                            out_hi[:, :, 4 * h:4 * h + 4].rearrange("p m t -> p t m").bitcast(F32), ALU.subtract).then_inc(low, 1)


def lru_units(eng, head, tail):
    per, turns = 2 * QUARTERS, LRU_BLOCKS // 2
    head(0, 0)
    with eng.Fori(0, turns - 1) as i:
        for u in range(per):
            head(*((i, u + 1) if u + 1 < per else (i + 1, 0)))
            tail(i, u)
    for u in range(per):
        if u + 1 < per:
            head(turns - 1, u + 1)
        tail(turns - 1, u)


def rg_lru(nc, d, h_hi, h_lo):
    with ExitStack() as cx:
        sb = lambda n, s, t=F32: cx.enter_context(nc.sbuf_tensor("r4_" + n, s, t))
        sem = lambda n: cx.enter_context(nc.semaphore("r4_" + n))
        Q = QUARTER
        HALO = CONV_WIDTH - 1
        raw = sb("raw", [P, 2, KT, P])
        w_hi = sb("w_hi", [P, 2, 2, KT, P], F32R)
        w_lo = sb("w_lo", [P, 2, 2, KT, P], F32R)
        graw = sb("graw", [P, 2, P])
        g_hi = sb("g_hi", [P, 2, 2, P], F32R)
        g_lo = sb("g_lo", [P, 2, 2, P], F32R)
        NPAR = CONV_WIDTH + 5
        C_BIAS, C_BR, C_BI, C_LAM, C_LOG = range(CONV_WIDTH, NPAR)
        par = sb("par", [P, NPAR, LRU_BLOCKS])
        pslot = sb("pslot", [P, 2, NPAR])
        pt = sb("pt", [P, 5, LRU_BLOCKS])
        xl = sb("xl", [P, 2, HALO + Q])
        xc = sb("xc", [P, 2, Q])
        xc_hi = sb("xc_hi", [P, Q], F32R)
        xc_lo = sb("xc_lo", [P, Q], F32R)
        rg = sb("rg", [P, Q])
        ig = sb("ig", [P, Q])
        decay = sb("decay", [P, Q])
        root = sb("root", [P, Q])
        hh = sb("hh", [P, 2, Q])
        gy = sb("gy", [P, 2, Q])
        y_hi = sb("y_hi", [P, Q], F32R)
        y_lo = sb("y_lo", [P, Q], F32R)
        psum = lambda n: cx.enter_context(nc.psum_tensor("r4_" + n, [P, 2, Q], F32))
        ps_x, ps_g, ps_r, ps_i = psum("ps_x"), psum("ps_g"), psum("ps_r"), psum("ps_i")
        (par_in, raw_in, w_split, w_steps, lam_steps, lam_exp, xl_made, gl_made, ri_made, xl_taken, sig_done, tanh_done,
         root_done, gelu_done, conv_done, xc_split, head_steps, tail_steps, bx_done, y_split, m2_done, y_sent, zeroed, scanned) = (sem(n) for n in (
            "par_in", "raw_in", "w_split", "w_steps", "lam_steps", "lam_exp", "xl_made", "gl_made", "ri_made", "xl_taken", "sig_done",
            "tanh_done", "root_done", "gelu_done", "conv_done", "xc_split", "head_steps", "tail_steps", "bx_done", "y_split", "m2_done", "y_sent", "zeroed", "scanned"))
        LOADS = 16 * 6
        W_STEPS = 7
        HEAD_STEPS = 5
        TAIL_STEPS = 3
        PARAMS = ("conv_b", "lru_b_r", "lru_b_i", "lru_lambda")
        unit = lambda i, u: 2 * QUARTERS * i + u
        block_of = lambda i, u: 2 * i + u // QUARTERS

        with nc.Block() as block:

            @block.sync
            def _(sp):
                with nc.allow_non_contiguous_dma(reason="one parameter a partition"):
                    for k in range(CONV_WIDTH):
                        sp.dma_start(par[:, k, :], columns(d["conv_w"][0, k], LRU_BLOCKS)).then_inc(par_in, 16)
                    for k, name in enumerate(PARAMS):
                        sp.dma_start(par[:, CONV_WIDTH + k, :], columns(d[name][0], LRU_BLOCKS)).then_inc(par_in, 16)
                sp.sem_inc(y_sent, 32)
                sp.wait_ge(zeroed, 1)

                def load(c):
                    sp.wait_ge(w_split, 4 * c + 4)
                    for j, o in enumerate((O_LRU, O_GATE)):
                        sp.dma_start(raw[:, j, :, :], d["w_in"][0, :, bass.ds(c * P + o, P)].rearrange("(k p) n -> p k n", p=P)).then_inc(raw_in, 16)
                    for j, name in enumerate(("lru_w_r", "lru_w_i")):
                        for r in range(2):
                            rows = slice(64 * r, 64 * r + 64)
                            sp.dma_start(graw[rows, j, rows], d[name][0, bass.ds(2 * c + r, 1), :, :].rearrange("a i j -> (a i) j")).then_inc(raw_in, 16)

                def store(i, u):
                    n = unit(i, u)
                    sp.wait_ge(y_split, n + 3)
                    for j, y in enumerate((y_hi, y_lo)):
                        sp.dma_start(d["yl_t"][j, bass.ds(block_of(i, u) * P, P), (u % QUARTERS) * Q:(u % QUARTERS + 1) * Q],
                                     y[:, :].bitcast(F32)).then_inc(y_sent, 16)

                load(0)
                load(1)
                with sp.Fori(0, LRU_BLOCKS // 2 - 1) as i:
                    for u in range(2 * QUARTERS):
                        if u % QUARTERS == QUARTERS - 1:
                            load(2 * i + u // QUARTERS + 2)
                        store(i, u)
                for u in range(2 * QUARTERS):
                    store(LRU_BLOCKS // 2 - 1, u)
                sp.wait_ge(y_sent, 32 * (1 + QUARTERS * LRU_BLOCKS))

            @block.tensor
            def _(pe):
                pe.sem_inc(ri_made, 1)

                def head(i, u):
                    n, c, p, b = unit(i, u), block_of(i, u), u % 2, u // QUARTERS
                    if u % QUARTERS == 0:
                        pe.wait_ge(w_split, 4 * c + 8)
                    toks = slice((u % QUARTERS) * Q, (u % QUARTERS + 1) * Q)
                    for j, (ps, free, made) in enumerate(((ps_x, xl_taken, xl_made), (ps_g, gelu_done, gl_made))):
                        pe.wait_ge(free, n + 1)
                        for k in range(KT):
                            last = matmul3(nc, ps[:, p, :], w_hi[:, b, j, k, :], w_lo[:, b, j, k, :],
                                           h_hi[:, k, toks], h_lo[:, k, toks], k == 0, k == KT - 1)
                        last.then_inc(made, 1)

                def tail(i, u):
                    n, p, b = unit(i, u), u % 2, u // QUARTERS
                    pe.wait_ge(xc_split, n + 1)
                    pe.wait_ge(sig_done, n + 1)
                    for j, ps in enumerate((ps_r, ps_i)):
                        last = matmul3(nc, ps[:, p, :], g_hi[:, b, j, :], g_lo[:, b, j, :], xc_hi[:, :], xc_lo[:, :], True, True)
                    last.then_inc(ri_made, 1)

                lru_units(pe, head, tail)

            @block.scalar
            def _(act):
                act.sem_inc(xl_taken, 2)
                act.sem_inc(gelu_done, 2)
                act.sem_inc(sig_done, 2)
                act.wait_ge(lam_steps, 1)
                nc.scalar.activation(pt[:, 1, :], pt[:, 0, :], ACT.Exp, scale=-1.0).then_inc(lam_exp, 1)

                def head(i, u):
                    n, p = unit(i, u), u % 2
                    act.wait_ge(xl_made, n + 1)
                    act.wait_ge(conv_done, n + 3)
                    nc.scalar.copy(xl[:, p, HALO:], ps_x[:, p, :]).then_inc(xl_taken, 1)
                    act.wait_ge(gl_made, n + 1)
                    act.wait_ge(y_split, n + 1)
                    nc.scalar.activation(gy[:, p, :], ps_g[:, p, :], ACT.Gelu_apprx_tanh).then_inc(gelu_done, 1)

                def tail(i, u):
                    n, p, b = unit(i, u), u % 2, u // QUARTERS
                    act.wait_ge(ri_made, n + 2)
                    act.wait_ge(bx_done, n + 1)
                    nc.scalar.activation(rg[:, :], ps_r[:, p, :], ACT.Sigmoid, bias=pslot[:, b, C_BR:C_BR + 1]).then_inc(tanh_done, 1)
                    nc.scalar.activation(ig[:, :], ps_i[:, p, :], ACT.Sigmoid, bias=pslot[:, b, C_BI:C_BI + 1]).then_inc(sig_done, 1)
                    act.wait_ge(tanh_done, 2 * n + 1)
                    act.wait_ge(scanned, n + 1)
                    nc.scalar.activation(decay[:, :], rg[:, :], ACT.Exp, scale=pslot[:, b, C_LOG:C_LOG + 1]).then_inc(root_done, 1)
                    nc.scalar.activation(root[:, :], rg[:, :], ACT.Tanh, scale=pslot[:, b, C_LAM:C_LAM + 1]).then_inc(tanh_done, 1)
                    act.wait_ge(tanh_done, 2 * n + 2)
                    nc.scalar.activation(root[:, :], root[:, :], ACT.Sqrt, scale=-1.0).then_inc(root_done, 1)

                lru_units(act, head, tail)

            @block.gpsimd
            def _(pool):
                nc.gpsimd.memset(graw[:, :, :], 0.0).then_inc(zeroed, 1)

                def head(i, u):
                    pass

                def tail(i, u):
                    n, p = unit(i, u), u % 2
                    pool.wait_ge(conv_done, n + 4)
                    pool.wait_ge(sig_done, n + 3)
                    nc.gpsimd.tensor_tensor(ig[:, :], ig[:, :], xc[:, p, :], ALU.mult).then_inc(m2_done, 1)

                lru_units(pool, head, tail)

            @block.vector
            def _(dve):
                ts_, tt_, stt_ = nc.vector.tensor_scalar, nc.vector.tensor_tensor, nc.vector.scalar_tensor_tensor
                dve.sem_inc(w_split, 4)
                dve.sem_inc(conv_done, 3)
                dve.sem_inc(bx_done, 1)
                dve.sem_inc(scanned, 1)
                dve.sem_inc(y_split, 2)
                dve.wait_ge(par_in, 16 * (CONV_WIDTH + len(PARAMS)))
                lam = par[:, C_LAM, :]
                step = Chain(dve, lam_steps)
                step(stt_(pt[:, 0, :], lam, -1.0, lam, ALU.mult, ALU.max))
                dve.wait_ge(lam_exp, 1)
                step(ts_(pt[:, 2, :], pt[:, 1, :], 2.0, None, ALU.add))
                step(nc.vector.reciprocal(pt[:, 3, :], pt[:, 2, :]))
                step(tt_(pt[:, 1, :], pt[:, 1, :], pt[:, 3, :], ALU.mult))
                step(tt_(pt[:, 2, :], pt[:, 1, :], pt[:, 1, :], ALU.mult))
                step(ts_(pt[:, 3, :], pt[:, 2, :], 1.0 / 15, 1.0 / 13, ALU.mult, ALU.add))
                for m in (11, 9, 7, 5, 3, 1):
                    step(tt_(pt[:, 4, :], pt[:, 3, :], pt[:, 2, :], ALU.mult))
                    step(ts_(pt[:, 3, :], pt[:, 4, :], 1.0 / m, None, ALU.add))
                step(tt_(pt[:, 4, :], pt[:, 3, :], pt[:, 1, :], ALU.mult))
                step(ts_(pt[:, 3, :], lam, -1.0, 0.0, ALU.mult, ALU.max))
                step(stt_(pt[:, 2, :], pt[:, 4, :], 2.0, pt[:, 3, :], ALU.mult, ALU.add))
                step(ts_(par[:, C_LOG, :], pt[:, 2, :], -LRU_C, None, ALU.mult))
                step(ts_(lam, pt[:, 2, :], -LRU_C / 2, None, ALU.mult))

                def split_weights(c, b, part):
                    if part == 0:
                        dve.wait_ge(raw_in, LOADS * (c + 1))
                    step = Chain(dve, w_steps, W_STEPS * c + part)
                    ks = slice(2 * part, 2 * part + 2)
                    step(nc.vector.tensor_copy(w_hi[:, b, :, ks, :], raw[:, :, ks, :]))
                    if part == QUARTERS - 1:
                        step(nc.vector.tensor_copy(g_hi[:, b, :, :], graw[:, :, :]))
                        step(tt_(g_lo[:, b, :, :], graw[:, :, :], g_hi[:, b, :, :].bitcast(F32), ALU.subtract))
                        step(nc.vector.tensor_copy(pslot[:, b, :].unsqueeze(2), par[:, :, bass.ds(c, 1)]))
                    tt_(w_lo[:, b, :, ks, :], raw[:, :, ks, :], w_hi[:, b, :, ks, :].bitcast(F32), ALU.subtract).then_inc(w_split, 1)

                for part in range(QUARTERS):
                    split_weights(0, 0, part)
                dve.wait_ge(w_split, 8)

                def head(i, u):
                    n, c, p, b, t = unit(i, u), block_of(i, u), u % 2, u // QUARTERS, u % QUARTERS
                    step = Chain(dve, head_steps, HEAD_STEPS * n)
                    tap = lambda k: pslot[:, b, k:k + 1]
                    dve.wait_ge(xl_taken, n + 3)
                    if t == 0:
                        step(nc.vector.memset(xl[:, p, 0:HALO], 0.0))
                    else:
                        step(nc.vector.tensor_copy(xl[:, p, 0:HALO], xl[:, 1 - p, Q:Q + HALO]))
                    step(ts_(xc[:, p, :], xl[:, p, 0:Q], tap(0), tap(C_BIAS), ALU.mult, ALU.add))
                    for k in (1, 2):
                        step(stt_(xc[:, p, :], xl[:, p, k:k + Q], tap(k), xc[:, p, :], ALU.mult, ALU.add))
                    stt_(xc[:, p, :], xl[:, p, HALO:], tap(HALO), xc[:, p, :], ALU.mult, ALU.add).then_inc(conv_done, 1)
                    dve.wait_ge(conv_done, n + 4)
                    dve.wait_ge(ri_made, n + 1)
                    step(nc.vector.tensor_copy(xc_hi[:, :], xc[:, p, :]))
                    tt_(xc_lo[:, :], xc[:, p, :], xc_hi[:, :].bitcast(F32), ALU.subtract).then_inc(xc_split, 1)
                    if not (isinstance(c, int) and c == LRU_BLOCKS - 1):
                        split_weights(c + 1, 1 - b, t)

                def tail(i, u):
                    n, p, t = unit(i, u), u % 2, u % QUARTERS
                    step = Chain(dve, tail_steps, TAIL_STEPS * n)
                    dve.wait_ge(root_done, 2 * n + 2)
                    step(stt_(root[:, :], decay[:, :], 1.0, root[:, :], ALU.add, ALU.mult))
                    dve.wait_ge(m2_done, n + 1)
                    tt_(root[:, :], root[:, :], ig[:, :], ALU.mult).then_inc(bx_done, 1)
                    dve.wait_ge(bx_done, n + 2)
                    nc.vector.tensor_tensor_scan(hh[:, p, :], decay[:, :], root[:, :], 0.0 if t == 0 else hh[:, 1 - p, Q - 1:Q],
                                                 ALU.mult, ALU.add).then_inc(scanned, 1)
                    dve.wait_ge(scanned, n + 2)
                    dve.wait_ge(gelu_done, n + 3)
                    step(tt_(gy[:, p, :], gy[:, p, :], hh[:, p, :], ALU.mult))
                    dve.wait_ge(y_sent, 32 * n + 32)
                    step(nc.vector.tensor_copy(y_hi[:, :], gy[:, p, :]))
                    tt_(y_lo[:, :], gy[:, p, :], y_hi[:, :].bitcast(F32), ALU.subtract).then_inc(y_split, 1)

                lru_units(dve, head, tail)


def mix_branches(nc, d):
    DB = D_MODEL // P
    KS = S5_WIDTH // P
    Q = QUARTER
    UNITS = QUARTERS * DB
    with ExitStack() as cx:
        sb = lambda n, s, t=F32: cx.enter_context(nc.sbuf_tensor("m5_" + n, s, t))
        sem = lambda n: cx.enter_context(nc.semaphore("m5_" + n))
        h = sb("h", [P, 2, 2, KT, Q], F32R)
        ys = sb("ys", [P, 2, KS, Q], F32R)
        yl = sb("yl", [P, 2, KT, Q], F32R)
        raw = sb("raw", [P, 2, KT, P])
        w_hi = sb("w_hi", [P, 2, 4, KT, P], F32R)
        w_lo = sb("w_lo", [P, 2, 4, KT, P], F32R)
        ga = sb("ga", [P, Q])
        gb = sb("gb", [P, Q])
        gz = sb("gz", [P, Q])
        m_hi = sb("m_hi", [P, Q], F32R)
        m_lo = sb("m_lo", [P, Q], F32R)
        ps = {n: cx.enter_context(nc.psum_tensor("m5_ps_" + n, [P, Q], F32)) for n in ("ga", "gb", "z1", "z2", "yb")}
        (h_in0, h_in1, ys_in, yl_in, w_split, high, made_ga, made_gb, made_z, made_yb, sig, steps, mixed, sent) = (sem(n) for n in (
            "h_in0", "h_in1", "ys_in", "yl_in", "w_split", "high", "made_ga", "made_gb", "made_z", "made_yb", "sig", "steps", "mixed", "sent"))
        raw_in = [sem("raw_in0"), sem("raw_in1")]
        order = sem("order")
        h_in = [h_in0, h_in1]
        PIECES = 4
        GA, GB, Z, YB = range(PIECES)
        STEPS = 5

        def units(eng, body, enter=lambda tq: None):
            for tq in range(QUARTERS):
                enter(tq)
                with eng.Fori(0, DB // 2) as i:
                    for b in range(2):
                        body(DB * tq + 2 * i + b, tq, 2 * i + b, b)

        with nc.Block() as block:

            @block.sync
            def _(sp):
                def piece(n, blk, p, turn):
                    sp.wait_ge(w_split, PIECES * n + p + 1)
                    sp.sem_inc(order, 1)
                    cols = lambda o: bass.ds(blk * P + o, P)
                    if p == Z:
                        for j in range(2):
                            sp.dma_start(raw[:, p % 2, j * KS:(j + 1) * KS, :],
                                         d["w_s5_out"][0, :, cols(j * D_MODEL)].rearrange("(k p) n -> p k n", p=P)).then_inc(raw_in[p % 2], 16)
                    else:
                        src = d["w_lru_out"][0, :, cols(0)] if p == YB else d["w_in"][0, :, cols(O_GA if p == GA else O_GB)]
                        sp.dma_start(raw[:, p % 2, :, :], src.rearrange("(k p) n -> p k n", p=P)).then_inc(raw_in[p % 2], 16)

                def body(n, tq, blk, b):
                    for p in range(PIECES):
                        piece(n, blk, p, n)

                units(sp, body)

            @block.gpsimd
            def _(pool):
                def take(dst, src, sem_):
                    pool.dma_start(dst.bitcast(F32), src.rearrange("(k p) t -> p k t", p=P)).then_inc(sem_, 16)

                for tq in range(QUARTERS):
                    toks = slice(tq * Q, (tq + 1) * Q)
                    if tq == 0:
                        for a in range(2):
                            take(h[:, 0, a], d["h_t"][a, :, toks], h_in[0])
                    if tq >= 1:
                        pool.wait_ge(made_z, DB * tq)
                    for a in range(2):
                        take(ys[:, a], d["ys_t"][a, :, toks], ys_in)
                    if tq >= 1:
                        pool.wait_ge(made_yb, DB * tq)
                    for a in range(2):
                        take(yl[:, a], d["yl_t"][a, :, toks], yl_in)
                    if tq + 1 < QUARTERS:
                        toks = slice((tq + 1) * Q, (tq + 2) * Q)
                        for a in range(2):
                            take(h[:, (tq + 1) % 2, a], d["h_t"][a, :, toks], h_in[(tq + 1) % 2])

            @block.tensor
            def _(pe):
                def group(out, b, p, k0, count, act):
                    for k in range(count):
                        last = matmul3(nc, out[:, :], w_hi[:, b, p, k0 + k, :], w_lo[:, b, p, k0 + k, :],
                                       act[:, 0, k, :], act[:, 1, k, :], k == 0, k == count - 1)
                    return last

                def enter(tq):
                    pe.wait_ge(h_in[tq % 2], 32 * (tq // 2 + 1))

                def body(n, tq, blk, b):
                    pe.wait_ge(w_split, PIECES * (n + 1) + 2)
                    pe.wait_ge(sig, 3 * n + 3)
                    group(ps["ga"], b, GA, 0, KT, h[:, tq % 2]).then_inc(made_ga, 1)
                    group(ps["gb"], b, GB, 0, KT, h[:, tq % 2]).then_inc(made_gb, 1)
                    pe.wait_ge(ys_in, 32 * (tq + 1))
                    pe.wait_ge(mixed, n + 1)
                    group(ps["z2"], b, Z, KS, KS, ys)
                    group(ps["z1"], b, Z, 0, KS, ys).then_inc(made_z, 1)
                    pe.wait_ge(yl_in, 32 * (tq + 1))
                    group(ps["yb"], b, YB, 0, KT, yl).then_inc(made_yb, 1)

                units(pe, body, enter)

            @block.scalar
            def _(act):
                act.sem_inc(sig, 3)

                def body(n, tq, blk, b):
                    act.wait_ge(made_ga, n + 1)
                    act.wait_ge(mixed, n + 1)
                    nc.scalar.activation(ga[:, :], ps["ga"][:, :], ACT.Sigmoid).then_inc(sig, 1)
                    act.wait_ge(made_gb, n + 1)
                    nc.scalar.activation(gb[:, :], ps["gb"][:, :], ACT.Sigmoid).then_inc(sig, 1)
                    act.wait_ge(made_z, n + 1)
                    nc.scalar.activation(gz[:, :], ps["z2"][:, :], ACT.Sigmoid).then_inc(sig, 1)
                    act.wait_ge(mixed, n + 2)
                    for a, m in enumerate((m_hi, m_lo)):
                        act.dma_start(d["mix_t"][a, bass.ds(blk * P, P), tq * Q:(tq + 1) * Q], m[:, :].bitcast(F32)).then_inc(sent, 16)

                units(act, body)
                act.wait_ge(sent, 32 * UNITS + 32)

            @block.vector
            def _(dve):
                tt_ = nc.vector.tensor_tensor
                dve.sem_inc(mixed, 1)
                dve.sem_inc(w_split, 2)
                dve.sem_inc(sent, 32)

                def split(n, b, turn):
                    for p in range(PIECES):
                        dve.wait_ge(raw_in[p % 2], (48 * turn + (16, 16, 48, 32)[p]) if p % 2 == 0 else 32 * turn + (0, 16, 0, 32)[p])
                        nc.vector.tensor_copy(w_hi[:, b, p], raw[:, p % 2]).then_inc(high, 1)
                        dve.wait_ge(high, PIECES * n + p + 1)
                        tt_(w_lo[:, b, p], raw[:, p % 2], w_hi[:, b, p].bitcast(F32), ALU.subtract).then_inc(w_split, 1)

                def mix(n):
                    step = Chain(dve, steps, STEPS * n)
                    dve.wait_ge(sig, 3 * n + 6)
                    step(tt_(gz[:, :], gz[:, :], ps["z1"][:, :], ALU.mult))
                    step(tt_(ga[:, :], ga[:, :], gz[:, :], ALU.mult))
                    dve.wait_ge(made_yb, n + 1)
                    step(tt_(gb[:, :], gb[:, :], ps["yb"][:, :], ALU.mult))
                    step(tt_(ga[:, :], ga[:, :], gb[:, :], ALU.add))
                    dve.wait_ge(sent, 32 * n + 32)
                    step(nc.vector.tensor_copy(m_hi[:, :], ga[:, :]))
                    tt_(m_lo[:, :], ga[:, :], m_hi[:, :].bitcast(F32), ALU.subtract).then_inc(mixed, 1)

                split(0, 0, 0)
                with dve.Fori(0, UNITS // 2 - 1) as i:
                    for b in range(2):
                        split(2 * i + b + 1, 1 - b, 2 * i + b + 1)
                        mix(2 * i + b)
                split(UNITS - 1, 1, UNITS - 1)
                mix(UNITS - 2)
                mix(UNITS - 1)


def project_and_route(nc, d, keep):
    with ExitStack() as cx:
        sb = lambda n, s, t=F32: cx.enter_context(nc.sbuf_tensor("p6_" + n, s, t))
        sem = lambda n: cx.enter_context(nc.semaphore("p6_" + n))
        NR = N_GROUPS + N_EXPERTS
        ident = keep["ident"]
        raw = sb("raw", [P, 2, D_MODEL])
        w_hi = sb("w_hi", [P, KT, D_MODEL], F32R)
        w_lo = sb("w_lo", [P, KT, D_MODEL], F32R)
        mix = sb("mix", [P, 2, 2, KT, P], F32R)
        xt = sb("xt", [P, 2, D_MODEL])
        h2 = sb("h2", [P, 2, D_MODEL])
        sq = sb("sq", [P, 2, D_MODEL])
        gain = sb("gain", [P, D_MODEL])
        ht = sb("ht", [P, KT, P])
        wr = sb("wr", [P, KT, NR])
        br = sb("br", [P, NR])
        sst = sb("sst", [P, 2, 3])
        cst = sb("cst", [P, 2])
        ps_o = cx.enter_context(nc.psum_tensor("p6_ps_o", [P, 2, D_MODEL], F32))
        ps_t = cx.enter_context(nc.psum_tensor("p6_ps_t", [P, KT, P], F32))
        ps_l = cx.enter_context(nc.psum_tensor("p6_ps_l", [P, 512], F32))
        (w_split, high, small_in, pool_steps, made, x2_done, squared, rstd, normed, turned, ht_done, logits, taken) = (
            sem(n) for n in ("w_split", "high", "small_in", "pool_steps", "made", "x2_done", "squared", "rstd", "normed",
                             "turned", "ht_done", "logits", "taken"))
        x2_sent = [sem("x2_sent0"), sem("x2_sent1")]
        h2_sent = [sem("h2_sent0"), sem("h2_sent1")]
        w_in = [sem("w_in0"), sem("w_in1")]
        order = keep["order"]
        t_in = [sem("t_in0"), sem("t_in1")]
        last_tile = TOK_TILES - 1

        def tiles(eng, head, tail):
            head(0, 0, 0)
            with eng.Fori(0, TOK_TILES // 2 - 1) as i:
                for b in range(2):
                    head(2 * i + b + 1, 1 - b, i + b)
                    tail(2 * i + b, b, i)
            head(last_tile, 1, TOK_TILES // 2 - 1)
            tail(last_tile - 1, 0, TOK_TILES // 2 - 1)
            tail(last_tile, 1, TOK_TILES // 2 - 1)

        with nc.Block() as block:

            @block.sync
            def _(sp):
                for k in range(KT):
                    if k >= 2:
                        sp.wait_ge(w_split, k - 1)
                    sp.dma_start(raw[:, k % 2, :], d["w_o"][0, k * P:(k + 1) * P, :]).then_inc(w_in[k % 2], 16)
                sp.dma_start(gain[:, :], d["norm_ffn"][0:1, :].to_broadcast([P, D_MODEL])).then_inc(small_in, 16)
                with nc.allow_non_contiguous_dma(reason="the router's narrow weights"):
                    sp.dma_start(wr[:, :, 0:N_GROUPS], d["router_group_w"][0].rearrange("(k p) n -> p k n", p=P)).then_inc(small_in, 16)
                    sp.dma_start(wr[:, :, N_GROUPS:], d["router_expert_w"][0].rearrange("(k p) n -> p k n", p=P)).then_inc(small_in, 16)
                sp.dma_start(br[:, 0:N_GROUPS], d["router_group_b"][0:1, :].to_broadcast([P, N_GROUPS])).then_inc(small_in, 16)
                sp.dma_start(br[:, N_GROUPS:], d["router_expert_b"][0:1, :].to_broadcast([P, N_EXPERTS])).then_inc(small_in, 16)
                with sp.Fori(0, TOK_TILES // 2) as i:
                    for b in range(2):
                        t = 2 * i + b
                        sp.wait_ge(made, t + 1)
                        sp.sem_inc(order, 1)
                        for a in range(2):
                            sp.dma_start(mix[:, b, a].bitcast(F32), d["mix_t"][a, :, bass.ds(t * P, P)].rearrange("(k p) t -> p k t", p=P)).then_inc(t_in[b], 16)
                        sp.wait_ge(normed, t + 1)
                        sp.sem_inc(order, 1)
                        sp.wait_ge(x2_sent[b], 16 * i + 16)
                        sp.dma_start(xt[:, b, :], d["x"][0, bass.ds(t * P, P), :]).then_inc(t_in[b], 16)

            @block.tensor
            def _(pe):
                pe.sem_inc(made, 2)
                pe.sem_inc(turned, 1)
                pe.sem_inc(logits, 1)
                pe.wait_ge(small_in, 16 * 5)

                def head(t, b, turn):
                    pe.wait_ge(t_in[b], 48 * (turn + 1))
                    pe.wait_ge(x2_done, t + 1)
                    for half in range(2):
                        for k in range(KT):
                            if isinstance(t, int) and t == 0 and half == 0:
                                pe.wait_ge(w_split, k + 1)
                            cols = slice(half * 512, half * 512 + 512)
                            last = matmul3(nc, ps_o[:, b, cols], mix[:, b, 0, k, :], mix[:, b, 1, k, :], w_hi[:, k, cols], w_lo[:, k, cols],
                                           k == 0, k == KT - 1)
                    last.then_inc(made, 1)

                def turn_h(t, b):
                    pe.wait_ge(normed, t + 3)
                    pe.wait_ge(ht_done, t + 1)
                    for k in range(KT):
                        last = nc.tensor.transpose(ps_t[:, k, :], h2[:, b, k * P:(k + 1) * P], ident[:, :])
                    last.then_inc(turned, 1)

                def route(t):
                    pe.wait_ge(ht_done, t + 2)
                    pe.wait_ge(taken, t + 1)
                    for k in range(KT):
                        last = nc.tensor.matmul(ps_l[:, 0:NR], ht[:, k, :], wr[:, k, :], start=(k == 0), stop=(k == KT - 1))
                    last.then_inc(logits, 1)

                head(0, 0, 0)
                head(1, 1, 0)
                turn_h(0, 0)
                with pe.Fori(0, TOK_TILES // 2 - 1) as i:
                    for b in (1, 0):
                        t = 2 * i + 2 - b
                        head(t + 1, 1 - b, i + 1)
                        route(t - 1)
                        turn_h(t, b)
                route(last_tile - 1)
                turn_h(last_tile, 1)
                route(last_tile)

            @block.scalar
            def _(act):
                for s in x2_sent + h2_sent:
                    act.sem_inc(s, 16)
                act.sem_inc(ht_done, 1)
                act.wait_ge(small_in, 16 * 5)

                def head(t, b, turn):
                    act.wait_ge(x2_done, t + 3)
                    act.dma_start(d["x2"][bass.ds(t * P, P), :], xt[:, b, :]).then_inc(x2_sent[b], 16)
                    act.wait_ge(rstd, t + 1)
                    nc.scalar.activation(sq[:, b, :], xt[:, b, :], ACT.Square, accum_out=sst[:, b, 0:1]).then_inc(squared, 1)

                def tail(t, b, turn):
                    act.wait_ge(normed, t + 3)
                    act.dma_start(d["h2"][bass.ds(t * P, P), :], h2[:, b, :]).then_inc(h2_sent[b], 16)
                    act.wait_ge(turned, t + 2)
                    act.wait_ge(logits, t + 1)
                    nc.scalar.copy(ht[:, :, :], ps_t[:, :, :]).then_inc(ht_done, 1)

                tiles(act, head, tail)
                for s in x2_sent + h2_sent:
                    act.wait_ge(s, 16 * (TOK_TILES // 2 + 1))

            @block.gpsimd
            def _(pool):
                pool.sem_inc(rstd, 2)
                nc.gpsimd.memset(cst[:, 0:1], -0.5).then_inc(pool_steps, 1)
                nc.gpsimd.memset(cst[:, 1:2], RMS_EPS * D_MODEL).then_inc(pool_steps, 1)
                pool.wait_ge(pool_steps, 2)

                def head(t, b, turn):
                    pool.wait_ge(squared, t + 1)
                    nc.gpsimd.tensor_tensor(sst[:, b, 1:2], sst[:, b, 0:1], cst[:, 1:2], ALU.add).then_inc(pool_steps, 1)
                    pool.wait_ge(pool_steps, t + 3)
                    pool.wait_ge(normed, t + 1)
                    nc.gpsimd.tensor_tensor(sst[:, b, 2:3], sst[:, b, 1:2], cst[:, 0:1], ALU.pow).then_inc(rstd, 1)

                tiles(pool, head, lambda t, b, turn: None)

            @block.vector
            def _(dve):
                ts_, tt_, stt_ = nc.vector.tensor_scalar, nc.vector.tensor_tensor, nc.vector.scalar_tensor_tensor
                dve.sem_inc(x2_done, 2)
                dve.sem_inc(normed, 2)
                dve.sem_inc(taken, 1)
                for k in range(KT):
                    dve.wait_ge(w_in[k % 2], 16 * (k // 2 + 1))
                    nc.vector.tensor_copy(w_hi[:, k, :], raw[:, k % 2, :]).then_inc(high, 1)
                    dve.wait_ge(high, k + 1)
                    tt_(w_lo[:, k, :], raw[:, k % 2, :], w_hi[:, k, :].bitcast(F32), ALU.subtract).then_inc(w_split, 1)
                dve.wait_ge(small_in, 16 * 5)
                nc.vector.tensor_scalar(gain[:, :], gain[:, :], math.sqrt(D_MODEL), None, ALU.mult).then_inc(high, 1)
                dve.wait_ge(high, KT + 1)

                def head(t, b, turn):
                    dve.wait_ge(made, t + 3)
                    tt_(xt[:, b, :], ps_o[:, b, :], xt[:, b, :], ALU.add).then_inc(x2_done, 1)

                def tail(t, b, turn):
                    dve.wait_ge(rstd, t + 3)
                    dve.wait_ge(turned, t + 1)
                    dve.wait_ge(h2_sent[b], 16 * turn + 16)
                    stt_(h2[:, b, :], xt[:, b, :], sst[:, b, 2:3], gain[:, :], ALU.mult, ALU.mult).then_inc(normed, 1)

                def take(t):
                    dve.wait_ge(logits, t + 2)
                    tt_(keep["logits"][:, bass.ds(t, 1), :].rearrange("p a n -> p (a n)"), ps_l[:, 0:NR], br[:, :], ALU.add).then_inc(taken, 1)

                head(0, 0, 0)
                head(1, 1, 0)
                tail(0, 0, 0)
                with dve.Fori(0, TOK_TILES // 2 - 1) as i:
                    for b in (1, 0):
                        t = 2 * i + 2 - b
                        head(t + 1, 1 - b, i + 1)
                        tail(t, b, i + 1 - b)
                        take(t - 1)
                tail(last_tile, 1, TOK_TILES // 2 - 1)
                take(last_tile - 1)
                take(last_tile)


def place_tokens(nc, d, keep):
    with ExitStack() as cx:
        sb = lambda n, s, t=F32: cx.enter_context(nc.sbuf_tensor("q7_" + n, s, t))
        sem = lambda n: cx.enter_context(nc.semaphore("q7_" + n))
        E = N_EXPERTS
        G, J, T = N_GROUPS, EXPERTS_PER_GROUP, TOK_TILES
        ROUTE_STEPS = 25 + T
        SLOT_STEPS = ROUTE_STEPS + 2 + SEQ // P + 7
        top = sb("top", [P, T, 3])
        is_top = sb("is_top", [P, T, J])
        group = sb("group", [P, T, G])
        first = sb("first", [P, T, J])
        chosen = sb("chosen", [P, T, 2, E])
        second = sb("second", [P, T, J])
        order_key = sb("order_key", [P, T, J])
        key_top = sb("key_top", [P, T])
        own = sb("own", [P, T, G, J])
        el = sb("el", [P, T, J])
        low = sb("low", [P, T, G + 1])
        ex = sb("ex", [P, T, G + 1])
        ssum = sb("ssum", [P, T, 2])
        iota = sb("iota", [P, J])
        tri = sb("tri", [P, P])
        asum = sb("asum", [P, T, E])
        before = sb("before", [P, T + 1, E])
        rank = sb("rank", [P, T * 2])
        ones = sb("ones", [P, P])
        cnt = sb("cnt", [P, E])
        nt = sb("nt", [P, E])
        end = sb("end", [P, E])
        pad = sb("pad", [P, E])
        one = sb("one", [P, E])
        prod = sb("prod", [P, TOK_TILES * 2, E])
        slotf = sb("slotf", [P, TOK_TILES * 2])
        te = sb("te", [1, MAX_TILES, E - 1])
        turn = sb("turn", [1, E])
        tef = sb("tef", [1, MAX_TILES])
        tio = sb("tio", [1, MAX_TILES])
        tok = sb("tok", [P, TOK_TILES], I32)
        zero = sb("zero", [MAX_TILES, P], I32)
        ids = sb("ids", [MAX_TILES, P], I32)
        idf = sb("idf", [MAX_TILES, P])
        spare = sb("spare", [1, 1])
        ps_c = cx.enter_context(nc.psum_tensor("q7_ps_c", [P, 512], F32))
        ps_k = cx.enter_context(nc.psum_tensor("q7_ps_k", [P, T, E], F32))
        ps_i = cx.enter_context(nc.psum_tensor("q7_ps_i", [P, 512], F32))
        consts, exped, counted, steps, zero_sent, scattered, ids_in, idf_done, turned = (sem(n) for n in (
            "consts", "exped", "counted", "steps", "zero_sent", "scattered", "ids_in", "idf_done", "turned"))
        with nc.Block() as block:

            @block.gpsimd
            def _(pool):
                nc.gpsimd.memset(ones[:, :], 1.0).then_inc(consts, 1)
                nc.gpsimd.memset(one[:, :], 1.0).then_inc(consts, 1)
                nc.gpsimd.memset(zero[:, :], 0).then_inc(consts, 1)
                nc.gpsimd.iota(tio[:, :], pattern=[[1, MAX_TILES]], base=0, channel_multiplier=0,
                               allow_small_or_imprecise_dtypes=True).then_inc(consts, 1)
                nc.gpsimd.iota(tok[:, :], pattern=[[P, TOK_TILES]], base=0, channel_multiplier=1).then_inc(consts, 1)
                nc.gpsimd.memset(turn[:, :], 1.0).then_inc(consts, 1)
                nc.gpsimd.iota(iota[:, :], pattern=[[1, J]], base=0, channel_multiplier=0,
                               allow_small_or_imprecise_dtypes=True).then_inc(consts, 1)
                nc.gpsimd.memset(before[:, 0, :], 0.0).then_inc(consts, 1)
                pool.wait_ge(consts, 8)
                nc.gpsimd.memset(turn[:, W_SLOTS - 1::W_SLOTS], 1.0 - W_SLOTS).then_inc(consts, 1)
                nc.gpsimd.affine_select(out=tri[:, :], in_=ones[:, :], compare_op=ALU.is_gt, fill=0.0,
                                        base=0, pattern=[[1, P]], channel_multiplier=-1).then_inc(consts, 1)
                pool.wait_ge(consts, 10)
                pool.wait_ge(zero_sent, 16)
                pool.wait_ge(steps, SLOT_STEPS)
                for t in range(TOK_TILES):
                    for k in range(2):
                        nc.gpsimd.indirect_dma_start(out=d["slot_tok"], out_offset=bass.IndirectOffsetOnAxis(ap=keep["slot"][:, t, k:k + 1], axis=0),
                                                     in_=tok[:, t:t + 1], in_offset=None).then_inc(scattered, 16)

            @block.sync
            def _(sp):
                sp.wait_ge(consts, 10)
                sp.dma_start(d["slot_tok"].rearrange("(t p) o -> t (p o)", p=P), zero[:, :]).then_inc(zero_sent, 16)
                sp.wait_ge(scattered, 16 * 2 * TOK_TILES)
                sp.dma_start(ids[:, :], d["slot_tok"].rearrange("(t p) o -> t (p o)", p=P)).then_inc(ids_in, 16)

            @block.tensor
            def _(pe):
                pe.wait_ge(consts, 10)
                pe.wait_ge(steps, ROUTE_STEPS)
                nc.tensor.matmul(ps_c[:, 0:E], ones[:, :], before[:, T, :], start=True, stop=True).then_inc(counted, 1)
                nc.tensor.matmul(ps_k[:, :, :], tri[:, :], asum[:, :, :], start=True, stop=False)
                nc.tensor.matmul(ps_k[:, :, :], ones[:, :], before[:, 0:T, :], start=False, stop=True).then_inc(counted, 1)
                pe.wait_ge(idf_done, 3)
                nc.tensor.transpose(ps_i[:, 0:MAX_TILES], idf[:, :], keep["ident"][0:MAX_TILES, 0:MAX_TILES]).then_inc(turned, 1)

            @block.scalar
            def _(act):
                act.wait_ge(steps, 18)
                nc.scalar.activation(ex[:, :, :], low[:, :, :], ACT.Exp).then_inc(exped, 1)

            @block.vector
            def _(dve):
                ts_, tt_, stt_ = nc.vector.tensor_scalar, nc.vector.tensor_tensor, nc.vector.scalar_tensor_tensor
                step = Chain(dve, steps)
                logits = keep["logits"]
                across = lambda v, n: v.unsqueeze(2).to_broadcast([P, T, n])

                def largest(values, n, slot, one_hot):
                    step(nc.vector.tensor_reduce(top[:, :, slot], values, AX.X, ALU.max))
                    step(tt_(is_top[:, :, 0:n], values, across(top[:, :, slot], n), ALU.is_equal))
                    step(stt_(order_key[:, :, 0:n], is_top[:, :, 0:n], float(J), iota[:, 0:n].unsqueeze(1).to_broadcast([P, T, n]), ALU.mult, ALU.subtract))
                    step(nc.vector.tensor_reduce(key_top[:, :], order_key[:, :, 0:n], AX.X, ALU.max))
                    step(tt_(one_hot, order_key[:, :, 0:n], across(key_top[:, :], n), ALU.is_equal))

                dve.wait_ge(consts, 10)
                largest(logits[:, :, 0:G], G, 0, group[:, :, :])
                step(tt_(own[:, :, :, :], logits[:, :, G:].rearrange("p t (g j) -> p t g j", g=G),
                         group[:, :, :].unsqueeze(3).to_broadcast([P, T, G, J]), ALU.mult))
                step(nc.vector.tensor_reduce(el[:, :, :], own[:, :, :, :].rearrange("p t g j -> p t j g"), AX.X, ALU.add))
                step(tt_(low[:, :, 0:G], logits[:, :, 0:G], across(top[:, :, 0], G), ALU.subtract))
                largest(el[:, :, :], J, 1, first[:, :, :])
                step(stt_(second[:, :, :], first[:, :, :], -3.0e38, el[:, :, :], ALU.mult, ALU.add))
                step(nc.vector.tensor_reduce(top[:, :, 2], second[:, :, :], AX.X, ALU.max))
                step(tt_(is_top[:, :, :], second[:, :, :], across(top[:, :, 2], J), ALU.is_equal))
                step(tt_(low[:, :, G], top[:, :, 2], top[:, :, 1], ALU.subtract))
                step(tt_(is_top[:, :, :], is_top[:, :, :], first[:, :, :], ALU.subtract))
                assert step.n == 18, step.n
                step(stt_(order_key[:, :, :], is_top[:, :, :], float(J), iota[:, :].unsqueeze(1).to_broadcast([P, T, J]), ALU.mult, ALU.subtract))
                step(nc.vector.tensor_reduce(key_top[:, :], order_key[:, :, :], AX.X, ALU.max))
                step(tt_(second[:, :, :], order_key[:, :, :], across(key_top[:, :], J), ALU.is_equal))
                for k, one_hot in enumerate((first, second)):
                    step(tt_(chosen[:, :, k, :].rearrange("p t (g j) -> p t g j", g=G), group[:, :, :].unsqueeze(3).to_broadcast([P, T, G, J]),
                             one_hot[:, :, :].unsqueeze(2).to_broadcast([P, T, G, J]), ALU.mult))
                step(tt_(asum[:, :, :], chosen[:, :, 0, :], chosen[:, :, 1, :], ALU.add))
                for t in range(T):
                    step(tt_(before[:, t + 1, :], before[:, t, :], asum[:, t, :], ALU.add))
                dve.wait_ge(exped, 1)
                step(nc.vector.tensor_reduce(ssum[:, :, 0], ex[:, :, 0:G], AX.X, ALU.add))
                assert step.n == ROUTE_STEPS, step.n
                nc.vector.memset(keep["ids"][:, MAX_TILES:], 0).then_inc(idf_done, 1)
                dve.wait_ge(counted, 1)
                step(nc.vector.tensor_copy(cnt[:, :], ps_c[:, 0:E]))
                step(ts_(nt[:, :], cnt[:, :], float(P), 1.0, ALU.is_gt, ALU.add))
                for m in range(2, SEQ // P):
                    step(stt_(nt[:, :], cnt[:, :], float(m * P), nt[:, :], ALU.is_gt, ALU.add))
                step(nc.vector.tensor_tensor_scan(end[:, :], one[:, :], nt[:, :], 0.0, ALU.mult, ALU.add))
                step(tt_(pad[:, :], end[:, :], nt[:, :], ALU.subtract))
                step(ts_(pad[:, :], pad[:, :], float(P), None, ALU.mult))
                dve.wait_ge(counted, 2)
                step(tt_(prod[:, :, :].rearrange("p (t k) e -> p t k e", k=2), chosen[:, :, :, :],
                         ps_k[:, :, :].unsqueeze(2).to_broadcast([P, T, 2, E]), ALU.mult))
                step(nc.vector.tensor_reduce(rank[:, :], prod[:, :, :], AX.X, ALU.add))
                step(tt_(prod[:, :, :], chosen[:, :, :, :].rearrange("p t k e -> p (t k) e"), pad[:, :].unsqueeze(1).to_broadcast([P, 2 * TOK_TILES, E]), ALU.mult))
                step(nc.vector.tensor_reduce(slotf[:, :], prod[:, :, :], AX.X, ALU.add))
                step(tt_(slotf[:, :], slotf[:, :], rank[:, :], ALU.add))
                step(nc.vector.tensor_copy(keep["slot"][:, :, :].rearrange("p t k -> p (t k)"), slotf[:, :]))
                assert step.n == SLOT_STEPS, step.n
                step(stt_(ssum[:, :, 1], ex[:, :, G], 1.0, ssum[:, :, 0], ALU.add, ALU.mult))
                step(nc.vector.reciprocal(keep["gates"][:, :, 0], ssum[:, :, 1]))
                step(tt_(keep["gates"][:, :, 1], keep["gates"][:, :, 0], ex[:, :, G], ALU.mult))
                shp = [1, MAX_TILES, E - 1]
                step(tt_(te[:, :, :], end[0:1, 0:E - 1].unsqueeze(1).to_broadcast(shp), tio[:, :].unsqueeze(2).to_broadcast(shp), ALU.is_le))
                step(nc.vector.tensor_reduce(tef[:, :], te[:, :, :], AX.X, ALU.add))
                step(nc.vector.tensor_copy(keep["tile_expert"][:, 0, :], tef[:, :]))
                step(tt_(te[:, :, :], te[:, :, :], turn[:, 0:E - 1].unsqueeze(1).to_broadcast(shp), ALU.mult))
                step(nc.vector.tensor_reduce(tef[:, :], te[:, :, :], AX.X, ALU.add))
                step(nc.vector.tensor_copy(keep["tile_expert"][:, 1, :], tef[:, :]))
                nc.vector.memset(keep["tile_end"][:, 0:1], 0).then_inc(idf_done, 1)
                step(nc.vector.tensor_copy(keep["tile_end"][:, 1:E + 1], end[0:1, :]))
                step(ts_(spare[:, :], end[0:1, E - 1:E], -1.0, MAX_TILES + 1.0, ALU.mult, ALU.add))
                step(nc.vector.tensor_copy(keep["tile_end"][:, E + 1:E + 2], spare[:, :]))
                dve.wait_ge(ids_in, 16)
                nc.vector.tensor_copy(idf[:, :], ids[:, :]).then_inc(idf_done, 1)
                dve.wait_ge(turned, 1)
                nc.vector.tensor_copy(keep["ids"][:, 0:MAX_TILES], ps_i[:, 0:MAX_TILES]).then_inc(idf_done, 1)


def run_experts(nc, d, keep):
    with ExitStack() as cx:
        sb = lambda n, s, t=F32: cx.enter_context(nc.sbuf_tensor("e8_" + n, s, t))
        sem = lambda n: cx.enter_context(nc.semaphore("e8_" + n))
        ident, ids, order = keep["ident"], keep["ids"], keep["order"]
        FK = D_EXPERT // P
        PART = KT * D_EXPERT
        GATE, UP, DOWN = range(3)
        PARTS = (("expert_w_gate", KT), ("expert_w_up", KT), ("expert_w_down", FK))
        HALF = PART // 2
        W = 2 * PART
        ZEROS = 256
        with nc.sbuf_tensor("e8_in_raw", [P, W_SLOTS * W], F32) as in_raw:
            pass
        in_lo = sb("in_lo", [P, W_SLOTS * W], F32R)
        in_hi = sb("in_hi", [P, W_SLOTS * W], F32R)
        with nc.sbuf_tensor("e8_down_raw", [P, PART], F32) as down_raw:
            pass
        down_lo = sb("down_lo", [P, PART], F32R)
        down_hi = sb("down_hi", [P, PART], F32R)
        idc = sb("idc", [P, 1], U32)
        xg = sb("xg", [P, D_MODEL])
        xt_hi = sb("xt_hi", [P, KT, P], F32R)
        xt_lo = sb("xt_lo", [P, KT, P], F32R)
        s = sb("s", [P, D_EXPERT])
        a = sb("a", [P, D_EXPERT])
        at_hi = sb("at_hi", [P, FK, P], F32R)
        at_lo = sb("at_lo", [P, FK, P], F32R)
        y = sb("y", [P, D_MODEL])
        zero = sb("zero", [P, ZEROS])
        ps_t = cx.enter_context(nc.psum_tensor("e8_ps_t", [P, KT, P], F32))
        ps_g = cx.enter_context(nc.psum_tensor("e8_ps_g", [P, D_EXPERT], F32))
        ps_u = cx.enter_context(nc.psum_tensor("e8_ps_u", [P, D_EXPERT], F32))
        ps_a = cx.enter_context(nc.psum_tensor("e8_ps_a", [P, FK, P], F32))
        ps_y = cx.enter_context(nc.psum_tensor("e8_ps_y", [P, D_MODEL], F32))
        (in_hi_split, in_lo_split, down_hi_split, down_lo_split, down_in, idc_done, x_in, turned, x_hi, x_lo, g_made, u_made, silu_done, a_done, a_turned, a_hi, a_lo, y_made, y_out,
         y_sent, filled) = (sem(n) for n in (
            "in_hi_split", "in_lo_split", "down_hi_split", "down_lo_split", "down_in", "idc_done", "x_in", "turned", "x_hi", "x_lo", "g_made", "u_made", "silu_done", "a_done", "a_turned",
            "a_hi", "a_lo", "y_made", "y_out", "y_sent", "filled"))
        raw_in = [[sem(f"raw_in{j}{q}") for q in range(2)] for j in range(W_SLOTS)]
        end_of = lambda eng, e: eng.value_load(keep["tile_end"][0:1, bass.ds(e + 1, 1)], min_val=1, max_val=MAX_TILES - 1)
        tiles = lambda eng: end_of(eng, N_EXPERTS - 1)

        def experts(eng, tile):
            def rest(e):
                start = end_of(eng, e - 1) + 1 if not isinstance(e, int) or e else 1
                end = end_of(eng, e)
                with eng.If(start < end):
                    with eng.Fori(start, end) as t:
                        tile(t, None, None, None)

            def first(e, j, last=False):
                start = end_of(eng, e - 1)
                tile(start, e, None if last else e + 1, 1 - j)

            tile(0, 0, 1, 1)
            rest(0)
            with eng.Fori(0, N_EXPERTS // 2 - 1) as i:
                for j in (1, 0):
                    e = 2 * i + 2 - j
                    first(e, j)
                    rest(e)
            first(N_EXPERTS - 1, 1, last=True)
            rest(N_EXPERTS - 1)

        with nc.Block() as block:

            @block.sync
            def _(sp):
                def load(e, q, raw, at_, landed):
                    name, k = PARTS[q]
                    sp.dma_start(raw[:, at_:at_ + PART].rearrange("p (k n) -> p k n", k=k),
                                 d[name][0, bass.ds(e, 1), :, :].rearrange("a (k p) n -> p (a k) n", p=P)).then_inc(landed, 16)

                def next_loads(e, j):
                    end = end_of(sp, e - 2)
                    for q, used in ((GATE, g_made), (UP, u_made)):
                        sp.wait_ge(used, end)
                        sp.sem_inc(order, 1)
                        load(e, q, in_raw, j * W + q * PART, raw_in[j][q])
                    sp.wait_ge(y_made, end)
                    sp.sem_inc(order, 1)
                    load(e - 1, DOWN, down_raw, 0, down_in)

                for e in range(2):
                    for q in (GATE, UP):
                        load(e, q, in_raw, e * W + q * PART, raw_in[e][q])
                load(0, DOWN, down_raw, 0, down_in)
                used = tiles(sp)
                sp.wait_ge(idc_done, 1)
                with sp.Fori(used, MAX_TILES + 1) as t:
                    sp.dma_start(d["y_slots"][bass.ds(t * P, P), :].rearrange("p (a d) -> p a d", d=ZEROS),
                                 zero[:, :].unsqueeze(1).to_broadcast([P, D_MODEL // ZEROS, ZEROS])).then_inc(filled, 16)
                with sp.Fori(1, N_EXPERTS // 2) as i:
                    for j in range(2):
                        next_loads(2 * i + j, j)
                sp.wait_ge(y_made, end_of(sp, N_EXPERTS - 2))
                sp.sem_inc(order, 1)
                load(N_EXPERTS - 1, DOWN, down_raw, 0, down_in)
                spare = sp.value_load(keep["tile_end"][0:1, N_EXPERTS + 1:N_EXPERTS + 2], min_val=1, max_val=MAX_TILES)
                sp.wait_ge(filled, 16 * spare)
                sp.sem_inc(order, 1)

            @block.gpsimd
            def _(pool):
                nc.gpsimd.memset(zero[:, :], 0.0).then_inc(idc_done, 1)

                def gather(t):
                    if not isinstance(t, int) or t > 0:
                        pool.wait_ge(turned, t + 1)
                    pool.sem_inc(order, 1)
                    nc.gpsimd.tensor_copy(idc[:, :], ids[:, bass.ds(t, 1)]).then_inc(idc_done, 1)
                    pool.wait_ge(idc_done, t + 2)
                    pool.sem_inc(order, 1)
                    nc.gpsimd.indirect_dma_start(out=xg[:, :], out_offset=None, in_=d["h2"],
                                                 in_offset=bass.IndirectOffsetOnAxis(ap=idc[:, :], axis=0)).then_inc(x_in, 16)

                gather(0)
                gather(1)
                with pool.Fori(0, tiles(pool)) as t:
                    gather(t + 2)

            @block.tensor
            def _(pe):
                pe.sem_inc(turned, 1)

                def turn_x(t):
                    pe.wait_ge(x_in, 16 * t + 16)
                    pe.wait_ge(x_lo, t + 1)
                    for k in range(KT):
                        last = nc.tensor.transpose(ps_t[:, k, :], xg[:, k * P:(k + 1) * P], ident[:, :])
                    last.then_inc(turned, 1)

                def slot_of(t):
                    return pe.value_load(keep["tile_expert"][0:1, 1, bass.ds(t, 1)], min_val=0, max_val=W_SLOTS - 1)

                def expert_of(t):
                    return pe.value_load(keep["tile_expert"][0:1, 0, bass.ds(t, 1)], min_val=0, max_val=N_EXPERTS - 1)

                def gate_or_up(t, expert, slot, ps, q):
                    for k in range(KT):
                        if k % (KT // 2) == 0:
                            pe.wait_ge(in_lo_split, 4 * expert + (2 * q + 1 + k // (KT // 2)))
                        part = lambda w: w[:, bass.ds(slot * W + (q * PART + k * D_EXPERT), D_EXPERT)]
                        last = matmul3(nc, ps[:, :], xt_hi[:, k, :], xt_lo[:, k, :], part(in_hi), part(in_lo), k == 0, k == KT - 1)
                    return last

                def gate(t, expert, slot):
                    pe.wait_ge(x_lo, t + 2)
                    pe.wait_ge(silu_done, t + 1)
                    gate_or_up(t, expert, slot, ps_g, GATE).then_inc(g_made, 1)

                def up(t, expert, slot):
                    pe.wait_ge(a_done, t + 1)
                    gate_or_up(t, expert, slot, ps_u, UP).then_inc(u_made, 1)

                def turn_a(t):
                    pe.wait_ge(a_done, t + 2)
                    pe.wait_ge(a_lo, t + 1)
                    for k in range(FK):
                        last = nc.tensor.transpose(ps_a[:, k, :], a[:, k * P:(k + 1) * P], ident[:, :])
                    last.then_inc(a_turned, 1)

                def down(t, expert):
                    pe.wait_ge(a_lo, t + 2)
                    pe.wait_ge(y_out, t + 1)
                    for k in range(FK):
                        if k % (FK // 2) == 0:
                            pe.wait_ge(down_lo_split, 2 * expert + (1 + k // (FK // 2)))
                        for half in range(2):
                            cols = slice(half * 512, half * 512 + 512)
                            at_ = k * D_MODEL + half * 512
                            last = matmul3(nc, ps_y[:, cols], at_hi[:, k, :], at_lo[:, k, :], down_hi[:, at_:at_ + 512], down_lo[:, at_:at_ + 512], k == 0, k == FK - 1)
                    last.then_inc(y_made, 1)

                turn_x(0)
                gate(0, 0, 0)
                up(0, 0, 0)
                turn_x(1)
                with pe.Fori(0, tiles(pe)) as t:
                    expert, slot = expert_of(t + 1), slot_of(t + 1)
                    gate(t + 1, expert, slot)
                    turn_a(t)
                    up(t + 1, expert, slot)
                    turn_x(t + 2)
                    down(t, expert_of(t))

            @block.scalar
            def _(act):
                act.sem_inc(silu_done, 1)
                act.sem_inc(y_out, 1)
                act.sem_inc(y_sent, 16)

                def split(raw, hi, at_, landed, count, done):
                    act.wait_ge(landed, count)
                    for half in range(2):
                        cols = slice(at_ + half * HALF, at_ + (half + 1) * HALF)
                        nc.scalar.copy(hi[:, cols], raw[:, cols]).then_inc(done, 1)

                def split_in(e, j, q):
                    if e is not None:
                        split(in_raw, in_hi, j * W + q * PART, raw_in[j][q], 8 * e + (16 - 8 * j), in_hi_split)

                def split_down(e):
                    if e is not None:
                        split(down_raw, down_hi, 0, down_in, 16 * e + 16, down_hi_split)

                def take_x(t):
                    act.wait_ge(turned, t + 2)
                    if not isinstance(t, int):
                        act.wait_ge(u_made, t)
                    nc.scalar.copy(xt_hi[:, :, :], ps_t[:, :, :]).then_inc(x_hi, 1)

                def silu(t):
                    act.wait_ge(g_made, t + 1)
                    act.wait_ge(a_done, t + 1)
                    nc.scalar.activation(s[:, :], ps_g[:, :], ACT.Silu).then_inc(silu_done, 1)

                def take_y(t):
                    act.wait_ge(y_made, t + 1)
                    act.wait_ge(y_sent, 16 * t + 16)
                    nc.scalar.copy(y[:, :], ps_y[:, :]).then_inc(y_out, 1)

                def store_y(t):
                    act.wait_ge(y_out, t + 2)
                    act.dma_start(d["y_slots"][bass.ds(t * P, P), :], y[:, :]).then_inc(y_sent, 16)

                split_in(0, 0, GATE)
                take_x(0)
                split_in(0, 0, UP)
                silu(0)

                def tile(t, own, e, j):
                    take_x(t + 1)
                    split_in(e, j, GATE)
                    if not isinstance(t, int):
                        take_y(t - 1)
                        store_y(t - 1)
                    split_in(e, j, UP)
                    silu(t + 1)
                    act.wait_ge(a_turned, t + 1)
                    nc.scalar.copy(at_hi[:, :, :], ps_a[:, :, :]).then_inc(a_hi, 1)
                    split_down(own)

                experts(act, tile)
                last = tiles(act)
                take_y(last - 1)
                store_y(last - 1)
                act.wait_ge(y_sent, 16 * last + 16)
                act.sem_inc(order, 1)

            @block.vector
            def _(dve):
                tt_ = nc.vector.tensor_tensor
                dve.sem_inc(x_lo, 1)
                dve.sem_inc(a_done, 1)
                dve.sem_inc(a_lo, 1)

                def split(raw, hi, lo, at_, split_hi, count, done):
                    for half in range(2):
                        cols = slice(at_ + half * HALF, at_ + (half + 1) * HALF)
                        dve.wait_ge(split_hi, count + (half + 1))
                        tt_(lo[:, cols], raw[:, cols], hi[:, cols].bitcast(F32), ALU.subtract).then_inc(done, 1)

                def split_in(e, j, q):
                    if e is not None:
                        split(in_raw, in_hi, in_lo, j * W + q * PART, in_hi_split, 4 * e + 2 * q, in_lo_split)

                def split_down(e):
                    if e is not None:
                        split(down_raw, down_hi, down_lo, 0, down_hi_split, 2 * e, down_lo_split)

                def take_x(t):
                    dve.wait_ge(x_hi, t + 1)
                    tt_(xt_lo[:, :, :], ps_t[:, :, :], xt_hi[:, :, :].bitcast(F32), ALU.subtract).then_inc(x_lo, 1)

                def product(t):
                    dve.wait_ge(silu_done, t + 2)
                    dve.wait_ge(u_made, t + 1)
                    if not isinstance(t, int) or t > 0:
                        dve.wait_ge(a_turned, t)
                    tt_(a[:, :], s[:, :], ps_u[:, :], ALU.mult).then_inc(a_done, 1)

                split_in(0, 0, GATE)
                take_x(0)
                split_in(0, 0, UP)
                product(0)

                def tile(t, own, e, j):
                    take_x(t + 1)
                    split_in(e, j, GATE)
                    split_in(e, j, UP)
                    dve.wait_ge(a_hi, t + 1)
                    tt_(at_lo[:, :, :], ps_a[:, :, :], at_hi[:, :, :].bitcast(F32), ALU.subtract).then_inc(a_lo, 1)
                    split_down(own)
                    product(t + 1)

                experts(dve, tile)


def combine_and_norm(nc, d, keep):
    with ExitStack() as cx:
        sb = lambda n, s, t=F32: cx.enter_context(nc.sbuf_tensor("f9_" + n, s, t))
        sem = lambda n: cx.enter_context(nc.semaphore("f9_" + n))
        xt = sb("xt", [P, 2, D_MODEL])
        yg = sb("yg", [P, 2, 2, D_MODEL])
        o = sb("o", [P, 2, D_MODEL])
        sq = sb("sq", [P, 2, D_MODEL])
        gain = sb("gain", [P, D_MODEL])
        slc = sb("slc", [P, 2, 2], U32)
        gc = sb("gc", [P, 2, 2])
        sst = sb("sst", [P, 2, 3])
        cst = sb("cst", [P, 2])
        small_in, pool_steps, steps, combined, squared, rstd, done = (sem(n) for n in (
            "small_in", "pool_steps", "steps", "combined", "squared", "rstd", "done"))
        x_in = [sem("x_in0"), sem("x_in1")]
        y_in = [sem("y_in0"), sem("y_in1")]
        sent = [sem("sent0"), sem("sent1")]
        last_tile = TOK_TILES - 1
        turns = TOK_TILES // 2
        order = keep["order"]
        STEPS = 2
        with nc.Block() as block:

            @block.sync
            def _(sp):
                sp.dma_start(gain[:, :], d["norm_final"].unsqueeze(0).to_broadcast([P, D_MODEL])).then_inc(small_in, 16)
                with sp.Fori(0, turns) as i:
                    for b in range(2):
                        t = 2 * i + b
                        sp.wait_ge(done, t + 1)
                        sp.dma_start(xt[:, b, :], d["x2"][bass.ds(t * P, P), :]).then_inc(x_in[b], 16)

            @block.gpsimd
            def _(pool):
                pool.sem_inc(rstd, 4)
                nc.gpsimd.memset(cst[:, 0:1], -0.5).then_inc(pool_steps, 1)
                nc.gpsimd.memset(cst[:, 1:2], RMS_EPS * D_MODEL).then_inc(pool_steps, 1)

                def gather(t, b, turn):
                    pool.wait_ge(combined, t + 1)
                    pool.sem_inc(order, 1)
                    nc.gpsimd.tensor_copy(slc[:, b, :], keep["slot"][:, bass.ds(t, 1), :].rearrange("p a k -> p (a k)")).then_inc(pool_steps, 1)
                    pool.wait_ge(pool_steps, t + 3)
                    pool.sem_inc(order, 1)
                    for k in range(2):
                        nc.gpsimd.indirect_dma_start(out=yg[:, b, k, :], out_offset=None, in_=d["y_slots"],
                                                     in_offset=bass.IndirectOffsetOnAxis(ap=slc[:, b, k:k + 1], axis=0)).then_inc(y_in[b], 16)

                def scale(t, b):
                    pool.wait_ge(squared, t + 1)
                    nc.gpsimd.tensor_tensor(sst[:, b, 1:2], sst[:, b, 0:1], cst[:, 1:2], ALU.add).then_inc(rstd, 1)
                    pool.wait_ge(rstd, 2 * t + 5)
                    pool.wait_ge(done, t + 1)
                    nc.gpsimd.tensor_tensor(sst[:, b, 2:3], sst[:, b, 1:2], cst[:, 0:1], ALU.pow).then_inc(rstd, 1)

                gather(0, 0, 0)
                gather(1, 1, 0)
                with pool.Fori(0, turns - 1) as i:
                    for b in range(2):
                        scale(2 * i + b, b)
                        gather(2 * i + b + 2, b, i + 1)
                scale(last_tile - 1, 0)
                scale(last_tile, 1)

            @block.scalar
            def _(act):
                for q in sent:
                    act.sem_inc(q, 16)

                def square(t, b):
                    act.wait_ge(combined, t + 3)
                    act.wait_ge(rstd, 2 * t + 2)
                    nc.scalar.activation(sq[:, b, :], xt[:, b, :], ACT.Square, accum_out=sst[:, b, 0:1]).then_inc(squared, 1)

                def store(t, b):
                    act.wait_ge(done, t + 3)
                    act.dma_start(d["out"][0, bass.ds(t * P, P), :], o[:, b, :]).then_inc(sent[b], 16)

                square(0, 0)
                with act.Fori(0, turns - 1) as i:
                    for b in range(2):
                        square(2 * i + b + 1, 1 - b)
                        store(2 * i + b, b)
                square(last_tile, 1)
                store(last_tile - 1, 0)
                store(last_tile, 1)
                for q in sent:
                    act.wait_ge(q, 16 * (turns + 1))

            @block.vector
            def _(dve):
                stt_ = nc.vector.scalar_tensor_tensor
                dve.sem_inc(done, 2)
                dve.sem_inc(combined, 2)
                dve.wait_ge(small_in, 16)
                nc.vector.tensor_scalar(gain[:, :], gain[:, :], math.sqrt(D_MODEL), None, ALU.mult).then_inc(steps, 1)

                def head(t, b, turn):
                    step = Chain(dve, steps, STEPS * t + 1)
                    step(nc.vector.tensor_copy(gc[:, b, :], keep["gates"][:, bass.ds(t, 1), :].rearrange("p a k -> p (a k)")))
                    dve.wait_ge(x_in[b], 16 * turn + 16)
                    dve.wait_ge(y_in[b], 32 * turn + 32)
                    step(stt_(xt[:, b, :], yg[:, b, 0, :], gc[:, b, 0:1], xt[:, b, :], ALU.mult, ALU.add))
                    stt_(xt[:, b, :], yg[:, b, 1, :], gc[:, b, 1:2], xt[:, b, :], ALU.mult, ALU.add).then_inc(combined, 1)

                def tail(t, b, turn):
                    dve.wait_ge(rstd, 2 * t + 6)
                    dve.wait_ge(sent[b], 16 * turn + 16)
                    stt_(o[:, b, :], xt[:, b, :], sst[:, b, 2:3], gain[:, :], ALU.mult, ALU.mult).then_inc(done, 1)

                head(0, 0, 0)
                with dve.Fori(0, turns - 1) as i:
                    for b in range(2):
                        head(2 * i + b + 1, 1 - b, i + b)
                        tail(2 * i + b, b, i)
                head(last_tile, 1, turns - 1)
                tail(last_tile - 1, 0, turns - 1)
                tail(last_tile, 1, turns - 1)


def hybrid_block(nc, d):
    with ExitStack() as cx:
        sb = lambda n, s, t=F32: cx.enter_context(nc.sbuf_tensor(n, s, t))
        ident = sb("ident", [P, P])
        s5_constants(nc, d, ident)
        with ExitStack() as hold:
            h_hi = hold.enter_context(nc.sbuf_tensor("h_hi", [P, KT, SEQ], F32R))
            h_lo = hold.enter_context(nc.sbuf_tensor("h_lo", [P, KT, SEQ], F32R))
            norm_and_turn(nc, d, ident, h_hi, h_lo)
            s5_inputs(nc, d, h_hi, h_lo)
            s5_scan(nc, d, ident)
            rg_lru(nc, d, h_hi, h_lo)
        mix_branches(nc, d)
        keep = {
            "ident": ident,
            "order": cx.enter_context(nc.semaphore("order")),
            "gates": sb("gates", [P, TOK_TILES, 2]),
            "slot": sb("slot", [P, TOK_TILES, 2], U32),
            "ids": sb("ids", [P, MAX_TILES + 2], U32),
            "tile_expert": sb("tile_expert", [1, 2, MAX_TILES], I32),
            "tile_end": sb("tile_end", [1, N_EXPERTS + 2], I32),
        }
        with ExitStack() as hold:
            keep["logits"] = hold.enter_context(nc.sbuf_tensor("logits", [P, TOK_TILES, N_GROUPS + N_EXPERTS], F32))
            project_and_route(nc, d, keep)
            place_tokens(nc, d, keep)
        run_experts(nc, d, keep)
        combine_and_norm(nc, d, keep)


SCRATCH = {
    "s5_pack": ((CBS, P, PACK), F32),
    "h_t": ((2, D_MODEL, SEQ), F32),
    "u": ((CBS, P, CTS, CB_GROUPS * P), F32),
    "ys_t": ((2, S5_WIDTH, SEQ), F32),
    "yl_t": ((2, LRU_WIDTH, SEQ), F32),
    "mix_t": ((2, D_MODEL, SEQ), F32),
    "x2": ((SEQ, D_MODEL), F32),
    "h2": ((SEQ, D_MODEL), F32),
    "slot_tok": ((MAX_TILES * P, 1), I32),
    "y_slots": (((MAX_TILES + 1) * P, D_MODEL), F32),
}


def kernel(**inputs):
    import numpy as _np
    import concourse.bacc as _bacc
    from concourse import mybir as _mybir
    from concourse.bass_utils import run_bass_kernel_spmd as _run

    nc = _bacc.Bacc("TRN2", target_bir_lowering=False, num_devices=1)
    arrays, d = {}, {}
    for name in inputs:
        a = _np.ascontiguousarray(inputs[name])
        arrays[f"in_{name}_dram"] = a
        d[name] = nc.dram_tensor(f"in_{name}_dram", a.shape, _mybir.dt.from_np(a.dtype), kind="ExternalInput").ap()
    for name, (shape, dt) in SCRATCH.items():
        d[name] = nc.dram_tensor(name, shape, dt).ap()
    d["out"] = nc.dram_tensor("out_0_dram", (1, SEQ, D_MODEL), F32, kind="ExternalOutput").ap()
    hybrid_block(nc, d)
    r = _run(nc, [arrays], core_ids=[0])
    return r.results[0]["out_0_dram"]
```

```python
import math
from contextlib import ExitStack

import concourse.bass as bass
from concourse import mybir

F32 = mybir.dt.float32
F32R = mybir.dt.float32r
I32 = mybir.dt.int32
U32 = mybir.dt.uint32
ALU = mybir.AluOpType
ACT = mybir.ActivationFunctionType
AX = mybir.AxisListType

P = 128
D_MODEL = 1024
SEQ = 2048
KT = D_MODEL // P
TOK_TILES = SEQ // P
RMS_EPS = 1e-6
S5_WIDTH = D_MODEL // 2
S5_GROUP = 16
S5_GROUPS = S5_WIDTH // S5_GROUP
S5_STATE = 64
PAIRS = S5_GROUPS // 2
STEP = P // S5_GROUP
CHUNKS = SEQ // STEP
CTS = CHUNKS // P
CBS = S5_WIDTH // P
CB_PAIRS = PAIRS // CBS
CB_GROUPS = S5_GROUPS // CBS
LRU_WIDTH = D_MODEL
LRU_BLOCKS = LRU_WIDTH // P
CONV_WIDTH = 4
LRU_C = 8.0
N_GROUPS = 4
EXPERTS_PER_GROUP = 8
N_EXPERTS = N_GROUPS * EXPERTS_PER_GROUP
D_EXPERT = D_MODEL // 2
QUARTER = 512
QUARTERS = SEQ // QUARTER
O_LRU = S5_WIDTH
O_GATE = O_LRU + LRU_WIDTH
O_GA = O_GATE + LRU_WIDTH
O_GB = O_GA + D_MODEL
MAX_TILES = 2 * SEQ // P + N_EXPERTS
W_SLOTS = 2

PACK_W = 0
PACK_C = PACK_W + CB_PAIRS * 2 * P
PACK_T = PACK_C + CB_PAIRS * 2 * 2 * P
PACK_TAB = PACK_T + CB_GROUPS * P
PACK_DECAY = PACK_TAB + 2 * CB_PAIRS * CHUNKS
PACK = PACK_DECAY + CB_PAIRS


class Chain:

    def __init__(self, eng, sem, base=0):
        self.eng, self.sem, self.base, self.n = eng, sem, base, 0

    def __call__(self, ins):
        self.n += 1
        ins.then_inc(self.sem, 1)
        self.eng.wait_ge(self.sem, self.base + self.n)


def matmul3(nc, out, l_hi, l_lo, r_hi, r_lo, start, stop):
    nc.tensor.matmul(out, l_hi, r_hi, start=start, stop=False)
    nc.tensor.matmul(out, l_hi, r_lo, start=False, stop=False)
    return nc.tensor.matmul(out, l_lo, r_hi, start=False, stop=stop)


def columns(v, count):
    return v.rearrange("(c p) -> p c", p=P)


def s5_constants(nc, d, ident):
    with ExitStack() as cx:
        sb = lambda n, s, t=F32: cx.enter_context(nc.sbuf_tensor("c0_" + n, s, t))
        sem = lambda n: cx.enter_context(nc.semaphore("c0_" + n))
        lam = sb("lam", [P, 2, PAIRS])
        ldt = sb("ldt", [P, PAIRS])
        decay = sb("decay", [P, PAIRS])
        braw = sb("braw", [P, 2, PAIRS, S5_GROUP])
        craw = sb("craw", [P, 2, CBS, 2, S5_STATE])
        cl = sb("cl", [P, 2, PAIRS, S5_GROUP])
        sc = sb("sc", [P, 16, PAIRS])
        bb = sb("bb", [P, 2, PAIRS, S5_GROUP])
        pf = sb("pf", [P, 2, STEP + 1, PAIRS])
        pr = sb("pr", [P, 2, STEP, PAIRS])
        v = sb("v", [P, 2, PAIRS, STEP, S5_GROUP])
        t1 = sb("t1", [P, PAIRS * STEP * S5_GROUP + PAIRS * S5_GROUP])
        t2 = sb("t2", [P, PAIRS * STEP * S5_GROUP + PAIRS * S5_GROUP])
        crx = sb("crx", [P, PAIRS, 2, 2, STEP + 1, S5_GROUP])
        w = sb("w", [P, PAIRS, 2, P])
        kt = sb("kt", [S5_GROUP, S5_GROUPS, STEP, S5_GROUP])
        tt = sb("tt", [P, S5_GROUPS, P])
        tab = sb("tab", [P, 2, PAIRS, CHUNKS])
        ph = sb("ph", [P, 10, PAIRS])
        tab1 = sb("tab1", [P, PAIRS * CHUNKS // 2])
        tab2 = sb("tab2", [P, PAIRS * CHUNKS // 2])
        dcol = sb("dcol", [S5_GROUP, S5_GROUPS])
        dd = sb("dd", [S5_GROUP, S5_GROUPS, S5_GROUP])
        ps_c = cx.enter_context(nc.psum_tensor("c0_ps_c", [P, 2, 512], F32))
        ps_w = cx.enter_context(nc.psum_tensor("c0_ps_w", [P, 2, 512], F32))
        ps_k = cx.enter_context(nc.psum_tensor("c0_ps_k", [S5_GROUP, 2, 512], F32))
        loaded, exps, sins = sem("loaded"), sem("exps"), sem("sins")
        prepared, args_ready, chain = sem("prepared"), sem("args_ready"), sem("chain")
        c_turned, c_lanes, v_ready, w_turned, w_ready = (sem(n) for n in
            ("c_turned", "c_lanes", "v_ready", "w_turned", "w_ready"))
        k_rhs, k_made, k_ready, k_placed, stored, table_steps = (sem(n) for n in
            ("k_rhs", "k_made", "k_ready", "k_placed", "stored", "table_steps"))
        INPUTS = 16 * 11
        doublings = CHUNKS.bit_length() - 1
        TABLE_STEPS = 6 * (3 + 2 * doublings - 1) + 2
        (DT, ZR, ZI, ER, CO, SI, RA, RB, MR, MI, WR, WI, X1, X2, X3, X4) = range(16)

        with nc.Block() as block:

            @block.sync
            def _(sp):
                with nc.allow_non_contiguous_dma(reason="small parameters, one word a lane"):
                    for j, name in enumerate(("s5_lam_re", "s5_lam_im")):
                        sp.dma_start(lam[:, j, :], d[name][0].rearrange("(q r) p -> (r p) q", r=2)).then_inc(loaded, 16)
                    for r in range(2):
                        sp.dma_start(ldt[64 * r:64 * r + 64, :],
                                     d["s5_log_dt"][0].rearrange("(q r) -> r q", r=2)[r:r + 1, :].to_broadcast([64, PAIRS])
                                     ).then_inc(loaded, 16)
                    for j, name in enumerate(("s5_b_re", "s5_b_im")):
                        sp.dma_start(braw[:, j, :, :], d[name][0].rearrange("(q r) p c -> (r p) q c", r=2)).then_inc(loaded, 16)
                    for j, name in enumerate(("s5_c_re", "s5_c_im")):
                        for dup in range(2):
                            sp.dma_start(craw[:, j, :, dup, :],
                                         d[name][0].rearrange("(b g) c p -> (g c) b p", b=CBS)).then_inc(loaded, 16)
                    sp.dma_start(dcol[:, :], d["s5_d"][0].rearrange("(g c) -> c g", c=S5_GROUP)).then_inc(loaded, 16)
                def store(cols, part):
                    for b in range(CBS):
                        q = slice(b * CB_PAIRS, (b + 1) * CB_PAIRS)
                        part(d["s5_pack"][b][:, cols], q, b)

                def store_c(dst, q, b):
                    sp.dma_start(dst.rearrange("p (k m) -> p k m", m=P),
                                 crx[:, q, :, :, 1:, :].rearrange("p q j r t c -> p (q j r) (t c)")).then_inc(stored, 16)

                def store_w(dst, q, b):
                    sp.dma_start(dst, w[:, q, :, :].rearrange("p q j m -> p (q j m)")).then_inc(stored, 16)

                def store_decay(dst, q, b):
                    sp.dma_start(dst, decay[:, q]).then_inc(stored, 16)

                def store_tab(dst, q, b):
                    sp.dma_start(dst.rearrange("p (j m) -> p j m", j=2), tab[:, :, q, :].rearrange("p j q m -> p j (q m)")).then_inc(stored, 16)

                def store_t(dst, q, b):
                    sp.dma_start(dst, tt[:, b * CB_GROUPS:(b + 1) * CB_GROUPS, :].rearrange("p g m -> p (g m)")).then_inc(stored, 16)

                sp.wait_ge(exps, 3)
                store(slice(PACK_DECAY, PACK), store_decay)
                sp.wait_ge(k_rhs, 1)
                store(slice(PACK_C, PACK_T), store_c)
                sp.wait_ge(w_ready, 8)
                store(slice(PACK_W, PACK_C), store_w)
                sp.wait_ge(k_ready, 1)
                sp.wait_ge(prepared, 3)
                for s in range(STEP):
                    sp.dma_start(tt[s * S5_GROUP:(s + 1) * S5_GROUP, :, s * S5_GROUP:],
                                 kt[:, :, 0:STEP - s, :].rearrange("p g t c -> p g (t c)")).then_inc(k_placed, 16)
                sp.wait_ge(table_steps, TABLE_STEPS)
                store(slice(PACK_TAB, PACK_DECAY), store_tab)
                sp.wait_ge(k_placed, 16 * STEP)
                store(slice(PACK_T, PACK_TAB), store_t)
                sp.wait_ge(stored, 16 * 5 * CBS)

            @block.gpsimd
            def _(pool):
                nc.gpsimd.memset(ident[:, :], 0.0).then_inc(prepared, 1)
                pool.wait_ge(prepared, 1)
                nc.gpsimd.affine_select(out=ident[:, :], in_=ident[:, :], compare_op=ALU.not_equal, fill=1.0,
                                        base=0, pattern=[[-1, P]], channel_multiplier=1).then_inc(prepared, 1)
                nc.gpsimd.memset(tt[:, :, :], 0.0).then_inc(prepared, 1)
                nc.gpsimd.memset(crx[:, :, :, :, :, :], 0.0).then_inc(prepared, 1)
                step = Chain(pool, table_steps)
                tt_ = nc.gpsimd.tensor_tensor
                s = lambda i: ph[:, i, :]
                base, power, square, x, y = ([s(2 * i), s(2 * i + 1)] for i in range(5))

                def cmul(out, a, b, x, y):
                    step(tt_(x, a[0], b[0], ALU.mult))
                    step(tt_(y, a[1], b[1], ALU.mult))
                    step(tt_(out[0], x, y, ALU.subtract))
                    step(tt_(x, a[0], b[1], ALU.mult))
                    step(tt_(y, a[1], b[0], ALU.mult))
                    step(tt_(out[1], x, y, ALU.add))

                pool.wait_ge(sins, 2)
                cmul(base, (sc[:, CO, :], sc[:, SI, :]), (sc[:, CO, :], sc[:, SI, :]), x[0], x[1])
                cmul(square, base, base, x[0], x[1])
                cmul(power, square, square, x[0], x[1])
                step(nc.gpsimd.memset(tab[:, 0, :, 0:1], 1.0))
                step(nc.gpsimd.memset(tab[:, 1, :, 0:1], 0.0))
                m = 1
                while m < CHUNKS:
                    shp = [P, PAIRS, m]
                    x6, y6 = (t.rearrange("p (q m) -> p q m", m=m) for t in (tab1[:, 0:PAIRS * m], tab2[:, 0:PAIRS * m]))
                    phase = [v.unsqueeze(2).to_broadcast(shp) for v in power]
                    cmul([tab[:, j, :, m:2 * m] for j in range(2)], [tab[:, j, :, 0:m] for j in range(2)], phase, x6, y6)
                    if 2 * m < CHUNKS:
                        cmul(square, power, power, x[0], x[1])
                        power, square = square, power
                    m *= 2
                assert step.n == TABLE_STEPS, step.n

            @block.scalar
            def _(act):
                act.wait_ge(loaded, INPUTS - 32)
                act.wait_ge(loaded, INPUTS)
                nc.scalar.activation(sc[:, DT, :], ldt[:, :], ACT.Exp).then_inc(exps, 1)
                act.wait_ge(args_ready, 1)
                nc.scalar.activation(sc[:, ER, :], sc[:, ZR, :], ACT.Exp).then_inc(exps, 1)
                nc.scalar.activation(decay[:, :], sc[:, ZR, :], ACT.Exp, scale=float(STEP)).then_inc(exps, 1)
                nc.scalar.activation(sc[:, SI, :], sc[:, RA, :], ACT.Sin).then_inc(sins, 1)
                nc.scalar.activation(sc[:, CO, :], sc[:, RB, :], ACT.Sin).then_inc(sins, 1)
                act.wait_ge(c_turned, 1)
                for b in range(CBS):
                    for j in range(2):
                        src = ps_c[:, j, b * P:(b + 1) * P].rearrange("p (q r c) -> p q r c", r=2, c=S5_GROUP)
                        for r in range(2):
                            rows = slice(64 * r, 64 * r + 64)
                            nc.scalar.copy(cl[rows, j, b * CB_PAIRS:(b + 1) * CB_PAIRS, :], src[rows, :, r, :]).then_inc(c_lanes, 1)

            @block.tensor
            def _(pe):
                pe.wait_ge(prepared, 2)
                pe.wait_ge(loaded, INPUTS)
                for j in range(2):
                    for b in range(CBS):
                        last = nc.tensor.transpose(ps_c[:, j, b * P:(b + 1) * P],
                                                   craw[:, j, b, :, :].rearrange("p r s -> p (r s)"), ident[:, :])
                last.then_inc(c_turned, 1)
                pe.wait_ge(v_ready, 1)
                for i in range(PAIRS // 2):
                    if i >= 2:
                        pe.wait_ge(w_ready, i - 1)
                    for q in (2 * i, 2 * i + 1):
                        for j in range(2):
                            last = nc.tensor.transpose(ps_w[:, i % 2, ((q % 2) * 2 + j) * P:((q % 2) * 2 + j + 1) * P],
                                                       v[:, j, q, :, :].rearrange("p t c -> p (t c)"), ident[:, :])
                    last.then_inc(w_turned, 1)
                pe.wait_ge(k_rhs, 1)
                for i in range(PAIRS // 2):
                    if i >= 2:
                        pe.wait_ge(k_made, i - 1)
                    for q in (2 * i, 2 * i + 1):
                        for j in range(2):
                            last = nc.tensor.matmul(ps_k[:, i % 2, (q % 2) * 256:(q % 2) * 256 + 256], bb[:, j, q, :],
                                                    crx[:, q, j, :, 0:STEP, :],
                                                    start=(j == 0), stop=(j == 1))
                    last.then_inc(w_turned, 1)

            @block.vector
            def _(dve):
                step = Chain(dve, chain)
                tt_ = nc.vector.tensor_tensor
                ts_ = nc.vector.tensor_scalar

                def cmul(o_re, o_im, a_re, a_im, b_re, b_im, x, y):
                    step(tt_(x, a_re, b_re, ALU.mult))
                    step(tt_(y, a_im, b_im, ALU.mult))
                    step(tt_(o_re, x, y, ALU.subtract))
                    step(tt_(x, a_re, b_im, ALU.mult))
                    step(tt_(y, a_im, b_re, ALU.mult))
                    step(tt_(o_im, x, y, ALU.add))

                s = lambda i: sc[:, i, :]
                dve.wait_ge(loaded, INPUTS)
                dve.wait_ge(exps, 1)
                step(tt_(s(ZR), lam[:, 0, :], s(DT), ALU.mult))
                step(tt_(s(ZI), lam[:, 1, :], s(DT), ALU.mult))
                magic, inv = 1.5 * 2.0 ** 23, 1.0 / (2 * math.pi)
                c1, c2 = 6.28125, 0.0019350051879882812
                c3 = 2 * math.pi - c1 - c2
                for out, turn in ((RA, 0.0), (RB, 0.25)):
                    step(ts_(s(X1), s(ZI), inv, turn, ALU.mult, ALU.add))
                    step(ts_(s(X2), s(X1), magic, None, ALU.add))
                    step(ts_(s(X1), s(X2), magic, None, ALU.subtract))
                    for n, part in enumerate((c1, c2, c3)):
                        step(nc.vector.scalar_tensor_tensor(s(X2), s(X1), -part, s(ZI) if n == 0 else s(X2), ALU.mult, ALU.add))
                    step(ts_(s(X2), s(X2), turn * 2 * math.pi, 3.1415925, ALU.add, ALU.min))
                    step(ts_(s(out), s(X2), -3.1415925, None, ALU.max))
                nc.vector.tensor_copy(s(X3), s(ZI)).then_inc(args_ready, 1)
                dve.wait_ge(exps, 3)
                dve.wait_ge(sins, 2)
                step(nc.vector.memset(pf[:, 0, 0, :], 1.0))
                step(nc.vector.memset(pf[:, 1, 0, :], 0.0))
                step(tt_(pf[:, 0, 1, :], s(ER), s(CO), ALU.mult))
                step(tt_(pf[:, 1, 1, :], s(ER), s(SI), ALU.mult))
                for n in range(2, STEP + 1):
                    h, k = n // 2, n - n // 2
                    cmul(pf[:, 0, n, :], pf[:, 1, n, :], pf[:, 0, h, :], pf[:, 1, h, :], pf[:, 0, k, :], pf[:, 1, k, :], s(X1), s(X2))
                for n in range(STEP):
                    step(nc.vector.tensor_copy(pr[:, :, n, :], pf[:, :, STEP - 1 - n, :]))
                step(tt_(s(X1), lam[:, 0, :], lam[:, 0, :], ALU.mult))
                step(tt_(s(X2), lam[:, 1, :], lam[:, 1, :], ALU.mult))
                step(tt_(s(X3), s(X1), s(X2), ALU.add))
                step(nc.vector.reciprocal(s(X4), s(X3)))
                step(tt_(s(MR), lam[:, 0, :], s(X4), ALU.mult))
                step(tt_(s(X3), lam[:, 1, :], s(X4), ALU.mult))
                step(ts_(s(MI), s(X3), -1.0, None, ALU.mult))
                step(ts_(s(X4), pf[:, 0, 1, :], -1.0, None, ALU.add))
                cmul(s(WR), s(WI), s(X4), pf[:, 1, 1, :], s(MR), s(MI), s(X1), s(X2))
                wide = lambda a, shape: a.unsqueeze(len(shape) - 1).to_broadcast(shape)
                small = [P, PAIRS, S5_GROUP]
                x3 = t1[:, 0:PAIRS * S5_GROUP].rearrange("p (q c) -> p q c", q=PAIRS)
                y3 = t2[:, 0:PAIRS * S5_GROUP].rearrange("p (q c) -> p q c", q=PAIRS)
                cmul(bb[:, 0], bb[:, 1], wide(s(WR), small), wide(s(WI), small), braw[:, 0], braw[:, 1], x3, y3)
                big = [P, STEP, PAIRS, S5_GROUP]
                vt = lambda j: v[:, j].rearrange("p q t c -> p t q c")
                bw = lambda j: bb[:, j].unsqueeze(1).to_broadcast(big)
                x4 = t1[:, 0:PAIRS * P].rearrange("p (t q c) -> p t q c", t=STEP, q=PAIRS)
                y4 = t2[:, 0:PAIRS * P].rearrange("p (t q c) -> p t q c", t=STEP, q=PAIRS)
                cmul(vt(0), vt(1), wide(pr[:, 0], big), wide(pr[:, 1], big), bw(0), bw(1), x4, y4)
                nc.vector.tensor_copy(s(X1), s(X2)).then_inc(v_ready, 1)
                dve.wait_ge(c_lanes, 4 * CBS)
                dve.wait_ge(prepared, 4)
                for r in range(2):
                    rows = slice(64 * r, 64 * r + 64)
                    shp = [64, STEP + 1, PAIRS, S5_GROUP]
                    x5 = t1[rows, :].rearrange("p (t q c) -> p t q c", t=STEP + 1, q=PAIRS)
                    y5 = t2[rows, :].rearrange("p (t q c) -> p t q c", t=STEP + 1, q=PAIRS)
                    o = lambda j: crx[rows, :, j, r].rearrange("p q t c -> p t q c")
                    pw = lambda j: pf[rows, j].unsqueeze(3).to_broadcast(shp)
                    cc = lambda j: cl[rows, j].unsqueeze(1).to_broadcast(shp)
                    step(tt_(x5, pw(0), cc(0), ALU.mult))
                    step(tt_(y5, pw(1), cc(1), ALU.mult))
                    step(tt_(o(0), x5, y5, ALU.subtract))
                    step(tt_(x5, pw(0), cc(1), ALU.mult))
                    step(tt_(y5, pw(1), cc(0), ALU.mult))
                    step(tt_(x5, x5, y5, ALU.add))
                    step(ts_(o(1), x5, -1.0, None, ALU.mult))
                nc.vector.tensor_copy(s(X1), s(X2)).then_inc(k_rhs, 1)
                for i in range(PAIRS // 2):
                    dve.wait_ge(w_turned, i + 1)
                    nc.vector.tensor_copy(w[:, 2 * i:2 * i + 2, :, :].rearrange("p q j m -> p (q j m)"), ps_w[:, i % 2, :]).then_inc(w_ready, 1)
                for i in range(PAIRS // 2):
                    dve.wait_ge(w_turned, PAIRS // 2 + i + 1)
                    nc.vector.tensor_copy(kt[:, 4 * i:4 * i + 4, :, :].rearrange("p g t c -> p (g t c)"),
                                          ps_k[:, i % 2, :]).then_inc(k_made, 1)
                dve.wait_ge(k_made, PAIRS // 2)
                dshape = [S5_GROUP, S5_GROUPS, S5_GROUP]
                step(tt_(dd[:, :, :], dcol[:, :].unsqueeze(2).to_broadcast(dshape),
                         ident[0:S5_GROUP, 0:S5_GROUP].unsqueeze(1).to_broadcast(dshape), ALU.mult))
                tt_(kt[:, :, 0, :], kt[:, :, 0, :], dd[:, :, :], ALU.add).then_inc(k_ready, 1)


def norm_and_turn(nc, d, ident, h_hi, h_lo):
    with ExitStack() as cx:
        sb = lambda n, s, t=F32: cx.enter_context(nc.sbuf_tensor("n1_" + n, s, t))
        sem = lambda n: cx.enter_context(nc.semaphore("n1_" + n))
        xin = sb("xin", [P, 2, D_MODEL])
        xn = sb("xn", [P, 2, D_MODEL])
        hs = sb("hs", [P, 2, KT, P])
        sq = sb("sq", [P, 2, D_MODEL])
        ss = sb("ss", [P, 2])
        ms = sb("ms", [P, 2])
        rs = sb("rs", [P, 2])
        gain = sb("gain", [P, KT])
        half = sb("half", [P, 2])
        pst = cx.enter_context(nc.psum_tensor("n1_pst", [P, 2, KT, P], F32))
        gain_in, squared, mean, rstd, normed, turned, gained, high, split = (sem(n) for n in
            ("gain_in", "squared", "mean", "rstd", "normed", "turned", "gained", "high", "split"))
        x_in = [sem("x_in0"), sem("x_in1")]
        last = TOK_TILES - 1
        with nc.Block() as block:

            @block.sync
            def _(sp):
                with nc.allow_non_contiguous_dma(reason="one gain a partition"):
                    sp.dma_start(gain[:, :], columns(d["norm_mix"][0], KT)).then_inc(gain_in, 16)
                with sp.Fori(0, TOK_TILES // 2) as i:
                    for b in range(2):
                        sp.wait_ge(normed, 2 * i + b + 1)
                        sp.dma_start(xin[:, b, :], d["x"][0, bass.ds((2 * i + b) * P, P), :]).then_inc(x_in[b], 16)

            @block.scalar
            def _(act):
                act.sem_inc(high, 2)

                def square(t, b, turn):
                    act.wait_ge(x_in[b], 16 * (turn + 1))
                    act.wait_ge(rstd, t + 1)
                    nc.scalar.activation(sq[:, b, :], xin[:, b, :], ACT.Square, accum_out=ss[:, b:b + 1]).then_inc(squared, 1)

                def take_high(t, b):
                    act.wait_ge(gained, t + 3)
                    nc.scalar.copy(h_hi[:, :, bass.ds(t * P, P)], hs[:, b, :, :]).then_inc(high, 1)

                square(0, 0, 0)
                with act.Fori(0, TOK_TILES // 2 - 1) as i:
                    for b in range(2):
                        square(2 * i + b + 1, 1 - b, i + b)
                        take_high(2 * i + b, b)
                square(last, 1, TOK_TILES // 2 - 1)
                take_high(last - 1, 0)
                take_high(last, 1)

            @block.gpsimd
            def _(pool):
                pool.sem_inc(rstd, 2)
                nc.gpsimd.memset(half[:, 0:1], -0.5).then_inc(mean, 1)
                nc.gpsimd.memset(half[:, 1:2], RMS_EPS * D_MODEL).then_inc(mean, 1)
                pool.wait_ge(mean, 2)
                with pool.Fori(0, TOK_TILES // 2) as i:
                    for b in range(2):
                        t = 2 * i + b
                        pool.wait_ge(squared, t + 1)
                        nc.gpsimd.tensor_tensor(ms[:, b:b + 1], ss[:, b:b + 1], half[:, 1:2], ALU.add).then_inc(mean, 1)
                        pool.wait_ge(mean, t + 3)
                        pool.wait_ge(normed, t + 1)
                        nc.gpsimd.tensor_tensor(rs[:, b:b + 1], ms[:, b:b + 1], half[:, 0:1], ALU.pow).then_inc(rstd, 1)

            @block.tensor
            def _(pe):
                pe.sem_inc(turned, 2)
                with pe.Fori(0, TOK_TILES // 2) as i:
                    for b in range(2):
                        t = 2 * i + b
                        pe.wait_ge(normed, t + 3)
                        pe.wait_ge(gained, t + 1)
                        for k in range(KT):
                            done = nc.tensor.transpose(pst[:, b, k, :], xn[:, b, k * P:(k + 1) * P], ident[:, :])
                        done.then_inc(turned, 1)

            @block.vector
            def _(dve):
                dve.sem_inc(normed, 2)
                dve.sem_inc(gained, 2)
                dve.sem_inc(split, 2)
                dve.wait_ge(gain_in, 16)

                def norm(t, b):
                    dve.wait_ge(rstd, t + 3)
                    dve.wait_ge(turned, t + 1)
                    nc.vector.tensor_scalar(xn[:, b, :], xin[:, b, :], rs[:, b:b + 1], math.sqrt(D_MODEL), ALU.mult, ALU.mult).then_inc(normed, 1)

                def take(t, b):
                    dve.wait_ge(turned, t + 3)
                    dve.wait_ge(split, t + 1)
                    nc.vector.tensor_tensor(hs[:, b, :, :], pst[:, b, :, :],
                                            gain[:, :].unsqueeze(2).to_broadcast([P, KT, P]), ALU.mult).then_inc(gained, 1)

                def split_low(t, b):
                    dve.wait_ge(high, t + 3)
                    nc.vector.tensor_tensor(h_lo[:, :, bass.ds(t * P, P)], hs[:, b, :, :],
                                            h_hi[:, :, bass.ds(t * P, P)].bitcast(F32), ALU.subtract).then_inc(split, 1)

                norm(0, 0)
                norm(1, 1)
                take(0, 0)
                with dve.Fori(0, TOK_TILES // 2 - 1) as i:
                    for b in range(2):
                        t = 2 * i + b
                        norm(t + 2, b)
                        take(t + 1, 1 - b)
                        split_low(t, b)
                take(last, 1)
                split_low(last - 1, 0)
                split_low(last, 1)


def s5_inputs(nc, d, h_hi, h_lo):
    with ExitStack() as cx:
        sb = lambda n, s, t=F32: cx.enter_context(nc.sbuf_tensor("u2_" + n, s, t))
        sem = lambda n: cx.enter_context(nc.semaphore("u2_" + n))
        raw = sb("raw", [P, 2, S5_WIDTH])
        w_hi = sb("w_hi", [P, KT, S5_WIDTH], F32R)
        w_lo = sb("w_lo", [P, KT, S5_WIDTH], F32R)
        u = sb("u", [P, CTS, S5_GROUPS, STEP, S5_GROUP])
        ps = cx.enter_context(nc.psum_tensor("u2_ps", [P, 4, S5_WIDTH], F32))
        w_split, made, taken, stored, high, h_sent = (sem(n) for n in ("w_split", "made", "taken", "stored", "high", "h_sent"))
        w_in = [sem("w_in0"), sem("w_in1")]
        hv = [h[:, :, :].rearrange("p k (a m t) -> p k a t m", a=CTS, t=STEP) for h in (h_hi, h_lo)]
        with nc.Block() as block:

            @block.sync
            def _(sp):
                for k in range(KT):
                    if k >= 2:
                        sp.wait_ge(w_split, k - 1)
                    sp.dma_start(raw[:, k % 2, :], d["w_in"][0, k * P:(k + 1) * P, 0:S5_WIDTH]).then_inc(w_in[k % 2], 16)
                for a, h in ((0, h_hi), (1, h_lo)):
                    for k in range(KT):
                        sp.dma_start(d["h_t"][a, k * P:(k + 1) * P, :], h[:, k, :].bitcast(F32)).then_inc(h_sent, 16)
                for a in range(CTS):
                    sp.wait_ge(taken, STEP * (a + 1))
                    for b in range(CBS):
                        sp.dma_start(d["u"][b, :, a, :], u[:, a, b * CB_GROUPS:(b + 1) * CB_GROUPS, :, :].rearrange("p g t c -> p (g t c)")
                                     ).then_inc(stored, 16)
                sp.wait_ge(stored, 16 * CTS * CBS)
                sp.wait_ge(h_sent, 16 * 2 * KT)

            @block.vector
            def _(dve):
                for k in range(KT):
                    dve.wait_ge(w_in[k % 2], 16 * (k // 2 + 1))
                    nc.vector.tensor_copy(w_hi[:, k, :], raw[:, k % 2, :]).then_inc(high, 1)
                    dve.wait_ge(high, k + 1)
                    nc.vector.tensor_tensor(w_lo[:, k, :], raw[:, k % 2, :], w_hi[:, k, :].bitcast(F32), ALU.subtract).then_inc(w_split, 1)

            @block.tensor
            def _(pe):
                n = 0
                for a in range(CTS):
                    for t in range(STEP):
                        if n >= 4:
                            pe.wait_ge(taken, n - 3)
                        for k in range(KT):
                            if n == 0:
                                pe.wait_ge(w_split, k + 1)
                            last = matmul3(nc, ps[:, n % 4, :], hv[0][:, k, a, t, :], hv[1][:, k, a, t, :],
                                           w_hi[:, k, :], w_lo[:, k, :], k == 0, k == KT - 1)
                        last.then_inc(made, 1)
                        n += 1

            @block.scalar
            def _(act):
                for n in range(CTS * STEP):
                    act.wait_ge(made, n + 1)
                    nc.scalar.copy(u[:, n // STEP, :, n % STEP, :], ps[:, n % 4, :].rearrange("p (g c) -> p g c", c=S5_GROUP)).then_inc(taken, 1)


def s5_scan(nc, d, ident, first_h):
    with ExitStack() as cx:
        sb = lambda n, s, t=F32: cx.enter_context(nc.sbuf_tensor("s3_" + n, s, t))
        sem = lambda n: cx.enter_context(nc.semaphore("s3_" + n))
        pack = sb("pack", [P, 2, PACK])
        uy = sb("uy", [P, 2, CTS, CB_GROUPS * P])
        ut = sb("ut", [P, 2, CB_GROUPS, CHUNKS])
        state = sb("state", [P, 2, 2, CB_PAIRS, CHUNKS])
        scanned = sb("scanned", [P, 2, CB_PAIRS, CHUNKS])
        t1 = sb("t1", [P, CB_PAIRS, CHUNKS])
        t2 = sb("t2", [P, CB_PAIRS, CHUNKS])
        out_hi = sb("out_hi", [P, CTS, P, STEP], F32R)
        out_lo = sb("out_lo", [P, CTS, P, STEP], F32R)
        ps_t = cx.enter_context(nc.psum_tensor("s3_ps_t", [P, 2, 4, P], F32))
        ps_x = cx.enter_context(nc.psum_tensor("s3_ps_x", [P, CB_PAIRS, 2, CHUNKS], F32))
        ps_y = cx.enter_context(nc.psum_tensor("s3_ps_y", [P, 2, 512], F32))
        (u_turned, y_turned, ut_ready, x_made, dve_steps, y_made, y_ready, high, low) = (sem(n) for n in
            ("u_turned", "y_turned", "ut_ready", "x_made", "dve_steps", "y_made", "y_ready", "high", "low"))
        loaded = [sem("loaded0"), sem("loaded1")]
        sent = [sem("sent0"), sem("sent1")]
        w = [pack[:, b, PACK_W:PACK_C].rearrange("p (q j m) -> p q j m", q=CB_PAIRS, j=2) for b in range(2)]
        cm = [pack[:, b, PACK_C:PACK_T].rearrange("p (q j m) -> p q j m", q=CB_PAIRS, j=2) for b in range(2)]
        tm = [pack[:, b, PACK_T:PACK_TAB].rearrange("p (g m) -> p g m", g=CB_GROUPS) for b in range(2)]
        tab = [pack[:, b, PACK_TAB:PACK_DECAY].rearrange("p (j q m) -> p j q m", j=2, q=CB_PAIRS) for b in range(2)]
        decay = [pack[:, b, PACK_DECAY:PACK] for b in range(2)]
        BACK_STEPS = 6
        DVE_STEPS = BACK_STEPS + 2 * CB_PAIRS + 6
        last_block = CBS - 1

        def blocks(eng, head, tail):
            head(0, 0, 0)
            with eng.Fori(0, CBS // 2 - 1) as i:
                for b in range(2):
                    head(2 * i + b + 1, 1 - b, i + b)
                    tail(2 * i + b, b)
            head(last_block, 1, CBS // 2 - 1)
            tail(last_block - 1, 0)
            tail(last_block, 1)

        with nc.Block() as block:

            @block.sync
            def _(sp):
                for q in sent:
                    sp.sem_inc(q, 32)

                def load(i, b):
                    sp.dma_start(uy[:, b], d["u"][bass.ds(i, 1), :, :, :].rearrange("a p t n -> (a p) t n")).then_inc(loaded[b], 16)
                    sp.dma_start(pack[:, b], d["s5_pack"][bass.ds(i, 1), :, :].rearrange("a p n -> (a p) n")).then_inc(loaded[b], 16)

                def store(i):
                    for a in range(CTS):
                        sp.wait_ge(low, 4 * i + 2 * a + 6)
                        for j, o in enumerate((out_hi, out_lo)):
                            sp.dma_start(d["ys_t"][j, bass.ds(i * P, P), a * P * STEP:(a + 1) * P * STEP],
                                         o[:, a].rearrange("p m t -> p (m t)").bitcast(F32)).then_inc(sent[a], 16)

                load(0, 0)
                load(1, 1)
                h, first_h_in = first_h
                for a in range(2):
                    sp.dma_start(h[:, 0, a].bitcast(F32), d["h_t"][a, :, 0:QUARTER].rearrange("(k p) t -> p k t", p=P)).then_inc(first_h_in, 16)
                with sp.Fori(0, CBS // 2 - 1) as i:
                    for b in range(2):
                        store(2 * i + b)
                        load(2 * i + b + 2, b)
                store(last_block - 1)
                store(last_block)
                for q in sent:
                    sp.wait_ge(q, 32 + 32 * CBS)

            @block.tensor
            def _(pe):

                def head(i, b, turn):
                    pe.wait_ge(loaded[b], 32 * (turn + 1))
                    if not isinstance(i, int) or i > 0:
                        pe.wait_ge(low, 4 * i)
                    for j in range(4):
                        if j >= 2:
                            pe.wait_ge(ut_ready, 4 * i + j - 1)
                        for g in range(2):
                            for a in range(CTS):
                                last = nc.tensor.transpose(ps_t[:, j % 2, 2 * g + a, :],
                                                           uy[:, b, a, (2 * j + g) * P:(2 * j + g + 1) * P], ident[:, :])
                        last.then_inc(u_turned, 1)
                    if not isinstance(i, int) or i > 0:
                        pe.wait_ge(dve_steps, DVE_STEPS * (i - 1) + 2 + BACK_STEPS)
                    for q in range(CB_PAIRS):
                        pe.wait_ge(ut_ready, 4 * i + q + 1)
                        for j in range(2):
                            for r in range(2):
                                last = nc.tensor.matmul(ps_x[64 * r:64 * r + 64, q, j, :], w[b][:, q, j, 64 * r:64 * r + 64],
                                                        ut[:, b, 2 * q + r, :], start=True, stop=True)
                    last.then_inc(x_made, 1)

                def tail(i, b):
                    pe.wait_ge(dve_steps, DVE_STEPS * (i + 1) + 2)
                    for a in range(CTS):
                        for h in range(2):
                            n = 2 * a + h
                            if n >= 2:
                                pe.wait_ge(y_ready, 4 * i + n - 1)
                            for q in (2 * h, 2 * h + 1):
                                o = ps_y[:, h, (q % 2) * 256:(q % 2) * 256 + 256]
                                for j in range(2):
                                    nc.tensor.matmul(o, state[:, b, j, q, a * P:(a + 1) * P], cm[b][:, q, j, :], start=(j == 0), stop=False)
                                for r in range(2):
                                    last = nc.tensor.matmul(o[:, r * P:(r + 1) * P], ut[:, b, 2 * q + r, a * P:(a + 1) * P],
                                                            tm[b][:, 2 * q + r, :], start=False, stop=(r == 1))
                            last.then_inc(y_made, 1)
                    pe.wait_ge(low, 4 * i + 4)
                    for a in range(CTS):
                        pe.wait_ge(y_ready, 4 * i + 2 * a + 2)
                        for h in range(2):
                            n = 2 * a + h
                            if n >= 2:
                                pe.wait_ge(low, 4 * i + n + 3)
                            for t in range(4):
                                last = nc.tensor.transpose(ps_t[:, n % 2, t, :],
                                                           uy[:, b, a, (4 * h + t) * P:(4 * h + t + 1) * P],
                                                           ident[:, :])
                            last.then_inc(y_turned, 1)

                blocks(pe, head, tail)

            @block.scalar
            def _(act):

                def head(i, b, turn):
                    for j in range(4):
                        act.wait_ge(u_turned, 4 * i + j + 1)
                        nc.scalar.copy(ut[:, b, 2 * j:2 * j + 2, :], ps_t[:, j % 2, :, :].rearrange("p (g a) m -> p g (a m)", g=2)).then_inc(ut_ready, 1)

                def tail(i, b):
                    for a in range(CTS):
                        for h in range(2):
                            act.wait_ge(y_made, 4 * i + 2 * a + h + 1)
                            nc.scalar.activation(uy[:, b, a, :].rearrange("p (t g c) -> p g t c", t=STEP, g=CB_GROUPS)[:, 4 * h:4 * h + 4],
                                                 ps_y[:, h, :].rearrange("p (g t c) -> p g t c", g=4, t=STEP), ACT.Gelu_apprx_tanh).then_inc(y_ready, 1)
                    for a in range(CTS):
                        for h in range(2):
                            n = 2 * a + h
                            act.wait_ge(y_turned, 4 * i + n + 1)
                            if h == 0:
                                act.wait_ge(sent[a], 32 * i + 32)
                            nc.scalar.copy(out_hi[:, a, :, 4 * h:4 * h + 4].rearrange("p m t -> p t m"), ps_t[:, n % 2, :, :]).then_inc(high, 1)

                blocks(act, head, tail)

            @block.vector
            def _(dve):
                tt_ = nc.vector.tensor_tensor
                dve.sem_inc(low, 4)
                zero = Chain(dve, dve_steps)
                for j in range(2):
                    zero(nc.vector.memset(scanned[:, j, :, 0:1], 0.0))
                n1 = CHUNKS - 1

                def scan(i, b, turn):
                    step = Chain(dve, dve_steps, base=DVE_STEPS * i + 2)
                    dve.wait_ge(loaded[b], 32 * (turn + 1))
                    dve.wait_ge(x_made, i + 1)
                    re, im = (ps_x[:, :, j, 0:n1] for j in range(2))
                    co, si = (tab[b][:, j, :, 1:CHUNKS] for j in range(2))
                    x, y = t1[:, :, 0:n1], t2[:, :, 0:n1]
                    step(tt_(x, co, re, ALU.mult))
                    step(tt_(y, si, im, ALU.mult))
                    step(tt_(state[:, b, 0, :, 1:], x, y, ALU.add))
                    step(tt_(x, co, im, ALU.mult))
                    step(tt_(y, si, re, ALU.mult))
                    step(tt_(state[:, b, 1, :, 1:], x, y, ALU.subtract))
                    for j in range(2):
                        for q in range(CB_PAIRS):
                            step(nc.vector.tensor_tensor_scan(scanned[:, j, q, 1:], decay[b][:, q:q + 1].to_broadcast([P, n1]),
                                                              state[:, b, j, q, 1:], 0.0, ALU.mult, ALU.add))

                def turn_forward(i, b):
                    step = Chain(dve, dve_steps, base=DVE_STEPS * (i + 1) + 2 - 6)
                    re, im = (scanned[:, j, :, :] for j in range(2))
                    co, si = (tab[b][:, j, :, :] for j in range(2))
                    x, y = t1[:, :, :], t2[:, :, :]
                    step(tt_(x, co, re, ALU.mult))
                    step(tt_(y, si, im, ALU.mult))
                    step(tt_(state[:, b, 0], x, y, ALU.subtract))
                    step(tt_(x, co, im, ALU.mult))
                    step(tt_(y, si, re, ALU.mult))
                    step(tt_(state[:, b, 1], x, y, ALU.add))

                def split(i):
                    for n in range(4):
                        dve.wait_ge(high, 4 * i + n + 1)
                        a, h = n // 2, n % 2
                        tt_(out_lo[:, a, :, 4 * h:4 * h + 4].rearrange("p m t -> p t m"), ps_t[:, n % 2, :, :],
                            out_hi[:, a, :, 4 * h:4 * h + 4].rearrange("p m t -> p t m").bitcast(F32), ALU.subtract).then_inc(low, 1)

                scan(0, 0, 0)
                turn_forward(0, 0)
                with dve.Fori(0, CBS // 2 - 1) as i:
                    for b in range(2):
                        scan(2 * i + b + 1, 1 - b, i + b)
                        split(2 * i + b)
                        turn_forward(2 * i + b + 1, 1 - b)
                scan(last_block, 1, CBS // 2 - 1)
                split(last_block - 1)
                turn_forward(last_block, 1)
                split(last_block)


def lru_units(eng, head, tail):
    per, turns = 2 * QUARTERS, LRU_BLOCKS // 2
    head(0, 0)
    with eng.Fori(0, turns - 1) as i:
        for u in range(per):
            head(*((i, u + 1) if u + 1 < per else (i + 1, 0)))
            tail(i, u)
    for u in range(per):
        if u + 1 < per:
            head(turns - 1, u + 1)
        tail(turns - 1, u)


def rg_lru(nc, d, h_hi, h_lo):
    with ExitStack() as cx:
        sb = lambda n, s, t=F32: cx.enter_context(nc.sbuf_tensor("r4_" + n, s, t))
        sem = lambda n: cx.enter_context(nc.semaphore("r4_" + n))
        Q = QUARTER
        HALO = CONV_WIDTH - 1
        raw = sb("raw", [P, 2, KT, P])
        w_hi = sb("w_hi", [P, 2, 2, KT, P], F32R)
        w_lo = sb("w_lo", [P, 2, 2, KT, P], F32R)
        graw = sb("graw", [P, 2, P])
        g_hi = sb("g_hi", [P, 2, 2, P], F32R)
        g_lo = sb("g_lo", [P, 2, 2, P], F32R)
        NPAR = CONV_WIDTH + 5
        C_BIAS, C_BR, C_BI, C_LAM, C_LOG = range(CONV_WIDTH, NPAR)
        par = sb("par", [P, NPAR, LRU_BLOCKS])
        pslot = sb("pslot", [P, 2, NPAR])
        pt = sb("pt", [P, 5, LRU_BLOCKS])
        xl = sb("xl", [P, 2, HALO + Q])
        xc = sb("xc", [P, 2, Q])
        xc_hi = sb("xc_hi", [P, Q], F32R)
        xc_lo = sb("xc_lo", [P, Q], F32R)
        rg = sb("rg", [P, Q])
        ig = sb("ig", [P, Q])
        decay = sb("decay", [P, Q])
        root = sb("root", [P, Q])
        hh = sb("hh", [P, 2, Q])
        gy = sb("gy", [P, 2, Q])
        y_hi = sb("y_hi", [P, Q], F32R)
        y_lo = sb("y_lo", [P, Q], F32R)
        psum = lambda n: cx.enter_context(nc.psum_tensor("r4_" + n, [P, 2, Q], F32))
        ps_x, ps_g, ps_r, ps_i = psum("ps_x"), psum("ps_g"), psum("ps_r"), psum("ps_i")
        (par_in, raw_in, w_split, w_steps, lam_steps, lam_exp, in_made, ri_made, xl_taken, sig_done, tanh_done,
         root_done, gelu_done, conv_done, xc_split, head_steps, tail_steps, bx_done, y_split, m2_done, y_sent, zeroed, scanned) = (sem(n) for n in (
            "par_in", "raw_in", "w_split", "w_steps", "lam_steps", "lam_exp", "in_made", "ri_made", "xl_taken", "sig_done",
            "tanh_done", "root_done", "gelu_done", "conv_done", "xc_split", "head_steps", "tail_steps", "bx_done", "y_split", "m2_done", "y_sent", "zeroed", "scanned"))
        LOADS = 16 * 6
        W_STEPS = 7
        HEAD_STEPS = 5
        TAIL_STEPS = 3
        PARAMS = ("conv_b", "lru_b_r", "lru_b_i", "lru_lambda")
        unit = lambda i, u: 2 * QUARTERS * i + u
        block_of = lambda i, u: 2 * i + u // QUARTERS

        with nc.Block() as block:

            @block.sync
            def _(sp):
                sp.sem_inc(y_sent, 32)
                sp.wait_ge(zeroed, 1)

                def load(c):
                    sp.wait_ge(w_split, 4 * c + 4)
                    for j, o in enumerate((O_LRU, O_GATE)):
                        sp.dma_start(raw[:, j, :, :], d["w_in"][0, :, bass.ds(c * P + o, P)].rearrange("(k p) n -> p k n", p=P)).then_inc(raw_in, 16)
                    for j, name in enumerate(("lru_w_r", "lru_w_i")):
                        for r in range(2):
                            rows = slice(64 * r, 64 * r + 64)
                            sp.dma_start(graw[rows, j, rows], d[name][0, bass.ds(2 * c + r, 1), :, :].rearrange("a i j -> (a i) j")).then_inc(raw_in, 16)

                def store(i, u):
                    n = unit(i, u)
                    sp.wait_ge(y_split, n + 3)
                    for j, y in enumerate((y_hi, y_lo)):
                        sp.dma_start(d["yl_t"][j, bass.ds(block_of(i, u) * P, P), (u % QUARTERS) * Q:(u % QUARTERS + 1) * Q],
                                     y[:, :].bitcast(F32)).then_inc(y_sent, 16)

                load(0)
                with nc.allow_non_contiguous_dma(reason="one parameter a partition"):
                    for k in range(CONV_WIDTH):
                        sp.dma_start(par[:, k, :], columns(d["conv_w"][0, k], LRU_BLOCKS)).then_inc(par_in, 16)
                    for k, name in enumerate(PARAMS):
                        sp.dma_start(par[:, CONV_WIDTH + k, :], columns(d[name][0], LRU_BLOCKS)).then_inc(par_in, 16)
                load(1)
                with sp.Fori(0, LRU_BLOCKS // 2 - 1) as i:
                    for u in range(2 * QUARTERS):
                        if u % QUARTERS == QUARTERS - 1:
                            load(2 * i + u // QUARTERS + 2)
                        store(i, u)
                for u in range(2 * QUARTERS):
                    store(LRU_BLOCKS // 2 - 1, u)
                sp.wait_ge(y_sent, 32 * (1 + QUARTERS * LRU_BLOCKS))

            @block.tensor
            def _(pe):
                pe.sem_inc(ri_made, 1)

                def head(i, u):
                    n, c, p, b = unit(i, u), block_of(i, u), u % 2, u // QUARTERS
                    if u % QUARTERS == 0:
                        pe.wait_ge(w_split, 4 * c + 8)
                    toks = slice((u % QUARTERS) * Q, (u % QUARTERS + 1) * Q)
                    for j, (ps, free) in enumerate(((ps_x, xl_taken), (ps_g, gelu_done))):
                        pe.wait_ge(free, n + 1)
                        for k in range(KT):
                            last = matmul3(nc, ps[:, p, :], w_hi[:, b, j, k, :], w_lo[:, b, j, k, :],
                                           h_hi[:, k, toks], h_lo[:, k, toks], k == 0, k == KT - 1)
                        last.then_inc(in_made, 1)

                def tail(i, u):
                    n, p, b = unit(i, u), u % 2, u // QUARTERS
                    pe.wait_ge(xc_split, n + 1)
                    pe.wait_ge(sig_done, n + 1)
                    for j, ps in enumerate((ps_r, ps_i)):
                        last = matmul3(nc, ps[:, p, :], g_hi[:, b, j, :], g_lo[:, b, j, :], xc_hi[:, :], xc_lo[:, :], True, True)
                    last.then_inc(ri_made, 1)

                lru_units(pe, head, tail)

            @block.scalar
            def _(act):
                act.sem_inc(xl_taken, 2)
                act.sem_inc(gelu_done, 2)
                act.sem_inc(sig_done, 2)
                act.wait_ge(lam_steps, 1)
                nc.scalar.activation(pt[:, 1, :], pt[:, 0, :], ACT.Exp, scale=-1.0).then_inc(lam_exp, 1)

                def head(i, u):
                    n, p = unit(i, u), u % 2
                    act.wait_ge(in_made, 2 * n + 1)
                    act.wait_ge(conv_done, n + 3)
                    nc.scalar.copy(xl[:, p, HALO:], ps_x[:, p, :]).then_inc(xl_taken, 1)
                    act.wait_ge(in_made, 2 * n + 2)
                    act.wait_ge(y_split, n + 1)
                    nc.scalar.activation(gy[:, p, :], ps_g[:, p, :], ACT.Gelu_apprx_tanh).then_inc(gelu_done, 1)

                def tail(i, u):
                    n, p, b = unit(i, u), u % 2, u // QUARTERS
                    act.wait_ge(ri_made, n + 2)
                    act.wait_ge(bx_done, n + 1)
                    nc.scalar.activation(rg[:, :], ps_r[:, p, :], ACT.Sigmoid, bias=pslot[:, b, C_BR:C_BR + 1]).then_inc(tanh_done, 1)
                    nc.scalar.activation(ig[:, :], ps_i[:, p, :], ACT.Sigmoid, bias=pslot[:, b, C_BI:C_BI + 1]).then_inc(sig_done, 1)
                    act.wait_ge(tanh_done, 2 * n + 1)
                    act.wait_ge(scanned, n + 1)
                    nc.scalar.activation(decay[:, :], rg[:, :], ACT.Exp, scale=pslot[:, b, C_LOG:C_LOG + 1]).then_inc(root_done, 1)
                    nc.scalar.activation(root[:, :], rg[:, :], ACT.Tanh, scale=pslot[:, b, C_LAM:C_LAM + 1]).then_inc(tanh_done, 1)
                    act.wait_ge(tanh_done, 2 * n + 2)
                    nc.scalar.activation(root[:, :], root[:, :], ACT.Sqrt, scale=-1.0).then_inc(root_done, 1)

                lru_units(act, head, tail)

            @block.gpsimd
            def _(pool):
                nc.gpsimd.memset(graw[:, :, :], 0.0).then_inc(zeroed, 1)

                def head(i, u):
                    pass

                def tail(i, u):
                    n, p = unit(i, u), u % 2
                    pool.wait_ge(conv_done, n + 4)
                    pool.wait_ge(sig_done, n + 3)
                    nc.gpsimd.tensor_tensor(ig[:, :], ig[:, :], xc[:, p, :], ALU.mult).then_inc(m2_done, 1)

                lru_units(pool, head, tail)

            @block.vector
            def _(dve):
                ts_, tt_, stt_ = nc.vector.tensor_scalar, nc.vector.tensor_tensor, nc.vector.scalar_tensor_tensor
                dve.sem_inc(w_split, 4)
                dve.sem_inc(conv_done, 3)
                dve.sem_inc(bx_done, 1)
                dve.sem_inc(scanned, 1)
                dve.sem_inc(y_split, 2)
                def split_weights(c, b, part):
                    if part == 0:
                        dve.wait_ge(raw_in, LOADS * (c + 1))
                    step = Chain(dve, w_steps, W_STEPS * c + part)
                    ks = slice(2 * part, 2 * part + 2)
                    step(nc.vector.tensor_copy(w_hi[:, b, :, ks, :], raw[:, :, ks, :]))
                    if part == QUARTERS - 1:
                        step(nc.vector.tensor_copy(g_hi[:, b, :, :], graw[:, :, :]))
                        step(tt_(g_lo[:, b, :, :], graw[:, :, :], g_hi[:, b, :, :].bitcast(F32), ALU.subtract))
                        step(nc.vector.tensor_copy(pslot[:, b, :].unsqueeze(2), par[:, :, bass.ds(c, 1)]))
                    tt_(w_lo[:, b, :, ks, :], raw[:, :, ks, :], w_hi[:, b, :, ks, :].bitcast(F32), ALU.subtract).then_inc(w_split, 1)

                for part in range(QUARTERS - 1):
                    split_weights(0, 0, part)
                dve.wait_ge(par_in, 16 * (CONV_WIDTH + len(PARAMS)))
                lam = par[:, C_LAM, :]
                step = Chain(dve, lam_steps)
                step(stt_(pt[:, 0, :], lam, -1.0, lam, ALU.mult, ALU.max))
                dve.wait_ge(lam_exp, 1)
                step(ts_(pt[:, 2, :], pt[:, 1, :], 2.0, None, ALU.add))
                step(nc.vector.reciprocal(pt[:, 3, :], pt[:, 2, :]))
                step(tt_(pt[:, 1, :], pt[:, 1, :], pt[:, 3, :], ALU.mult))
                step(tt_(pt[:, 2, :], pt[:, 1, :], pt[:, 1, :], ALU.mult))
                step(ts_(pt[:, 3, :], pt[:, 2, :], 1.0 / 15, 1.0 / 13, ALU.mult, ALU.add))
                for m in (11, 9, 7, 5, 3, 1):
                    step(tt_(pt[:, 4, :], pt[:, 3, :], pt[:, 2, :], ALU.mult))
                    step(ts_(pt[:, 3, :], pt[:, 4, :], 1.0 / m, None, ALU.add))
                step(tt_(pt[:, 4, :], pt[:, 3, :], pt[:, 1, :], ALU.mult))
                step(ts_(pt[:, 3, :], lam, -1.0, 0.0, ALU.mult, ALU.max))
                step(stt_(pt[:, 2, :], pt[:, 4, :], 2.0, pt[:, 3, :], ALU.mult, ALU.add))
                step(ts_(par[:, C_LOG, :], pt[:, 2, :], -LRU_C, None, ALU.mult))
                step(ts_(lam, pt[:, 2, :], -LRU_C / 2, None, ALU.mult))
                split_weights(0, 0, QUARTERS - 1)
                dve.wait_ge(w_split, 8)

                def head(i, u):
                    n, c, p, b, t = unit(i, u), block_of(i, u), u % 2, u // QUARTERS, u % QUARTERS
                    step = Chain(dve, head_steps, HEAD_STEPS * n)
                    tap = lambda k: pslot[:, b, k:k + 1]
                    dve.wait_ge(xl_taken, n + 3)
                    if t == 0:
                        step(nc.vector.memset(xl[:, p, 0:HALO], 0.0))
                    else:
                        step(nc.vector.tensor_copy(xl[:, p, 0:HALO], xl[:, 1 - p, Q:Q + HALO]))
                    step(ts_(xc[:, p, :], xl[:, p, 0:Q], tap(0), tap(C_BIAS), ALU.mult, ALU.add))
                    for k in (1, 2):
                        step(stt_(xc[:, p, :], xl[:, p, k:k + Q], tap(k), xc[:, p, :], ALU.mult, ALU.add))
                    stt_(xc[:, p, :], xl[:, p, HALO:], tap(HALO), xc[:, p, :], ALU.mult, ALU.add).then_inc(conv_done, 1)
                    dve.wait_ge(conv_done, n + 4)
                    dve.wait_ge(ri_made, n + 1)
                    step(nc.vector.tensor_copy(xc_hi[:, :], xc[:, p, :]))
                    tt_(xc_lo[:, :], xc[:, p, :], xc_hi[:, :].bitcast(F32), ALU.subtract).then_inc(xc_split, 1)
                    if not (isinstance(c, int) and c == LRU_BLOCKS - 1):
                        for part in ((0,), (1,), (2, 3), ())[t]:
                            split_weights(c + 1, 1 - b, part)

                def tail(i, u):
                    n, p, t = unit(i, u), u % 2, u % QUARTERS
                    step = Chain(dve, tail_steps, TAIL_STEPS * n)
                    dve.wait_ge(root_done, 2 * n + 2)
                    step(stt_(root[:, :], decay[:, :], 1.0, root[:, :], ALU.add, ALU.mult))
                    dve.wait_ge(m2_done, n + 1)
                    tt_(root[:, :], root[:, :], ig[:, :], ALU.mult).then_inc(bx_done, 1)
                    dve.wait_ge(bx_done, n + 2)
                    nc.vector.tensor_tensor_scan(hh[:, p, :], decay[:, :], root[:, :], 0.0 if t == 0 else hh[:, 1 - p, Q - 1:Q],
                                                 ALU.mult, ALU.add).then_inc(scanned, 1)
                    dve.wait_ge(scanned, n + 2)
                    dve.wait_ge(gelu_done, n + 3)
                    step(tt_(gy[:, p, :], gy[:, p, :], hh[:, p, :], ALU.mult))
                    dve.wait_ge(y_sent, 32 * n + 32)
                    step(nc.vector.tensor_copy(y_hi[:, :], gy[:, p, :]))
                    tt_(y_lo[:, :], gy[:, p, :], y_hi[:, :].bitcast(F32), ALU.subtract).then_inc(y_split, 1)

                lru_units(dve, head, tail)


def mix_branches(nc, d, order, first_h):
    DB = D_MODEL // P
    KS = S5_WIDTH // P
    Q = QUARTER
    UNITS = QUARTERS * DB
    with ExitStack() as cx:
        sb = lambda n, s, t=F32: cx.enter_context(nc.sbuf_tensor("m5_" + n, s, t))
        sem = lambda n: cx.enter_context(nc.semaphore("m5_" + n))
        ys = sb("ys", [P, 2, KS, Q], F32R)
        yl = sb("yl", [P, 2, KT, Q], F32R)
        raw = sb("raw", [P, 2, KT, P])
        w_hi = sb("w_hi", [P, 2, 4, KT, P], F32R)
        w_lo = sb("w_lo", [P, 2, 4, KT, P], F32R)
        ga = sb("ga", [P, Q])
        gb = sb("gb", [P, Q])
        gz = sb("gz", [P, Q])
        m_hi = sb("m_hi", [P, Q], F32R)
        m_lo = sb("m_lo", [P, Q], F32R)
        ps = {n: cx.enter_context(nc.psum_tensor("m5_ps_" + n, [P, Q], F32)) for n in ("ga", "gb", "z1", "z2", "yb")}
        (ys_in, yl_in, w_split, high, gates_made, made_z, made_yb, sig, steps, mixed, sent) = (sem(n) for n in (
            "ys_in", "yl_in", "w_split", "high", "gates_made", "made_z", "made_yb", "sig", "steps", "mixed", "sent"))
        raw_in = [sem("raw_in0"), sem("raw_in1")]
        h, first_h_in = first_h
        h_in = [sem("h_in0"), sem("h_in1")]
        PIECES = 4
        GA, GB, Z, YB = range(PIECES)
        STEPS = 5

        def units(eng, body, enter=lambda tq: None):
            for tq in range(QUARTERS):
                enter(tq)
                with eng.Fori(0, DB // 2) as i:
                    for b in range(2):
                        body(DB * tq + 2 * i + b, tq, 2 * i + b, b)

        with nc.Block() as block:

            @block.sync
            def _(sp):
                def piece(n, blk, p, turn):
                    sp.wait_ge(w_split, PIECES * n + p + 1)
                    sp.sem_inc(order, 1)
                    cols = lambda o: bass.ds(blk * P + o, P)
                    if p == Z:
                        for j in range(2):
                            sp.dma_start(raw[:, p % 2, j * KS:(j + 1) * KS, :],
                                         d["w_s5_out"][0, :, cols(j * D_MODEL)].rearrange("(k p) n -> p k n", p=P)).then_inc(raw_in[p % 2], 16)
                    else:
                        src = d["w_lru_out"][0, :, cols(0)] if p == YB else d["w_in"][0, :, cols(O_GA if p == GA else O_GB)]
                        sp.dma_start(raw[:, p % 2, :, :], src.rearrange("(k p) n -> p k n", p=P)).then_inc(raw_in[p % 2], 16)

                def body(n, tq, blk, b):
                    for p in range(PIECES):
                        piece(n, blk, p, n)

                units(sp, body)

            @block.gpsimd
            def _(pool):
                def take(dst, src, sem_):
                    pool.dma_start(dst.bitcast(F32), src.rearrange("(k p) t -> p k t", p=P)).then_inc(sem_, 16)

                for tq in range(QUARTERS):
                    toks = slice(tq * Q, (tq + 1) * Q)
                    if tq >= 1:
                        pool.wait_ge(made_z, DB * tq)
                    for a in range(2):
                        take(ys[:, a], d["ys_t"][a, :, toks], ys_in)
                    if tq >= 1:
                        pool.wait_ge(made_yb, DB * tq)
                    else:
                        pool.wait_ge(w_split, PIECES + 2)
                    for a in range(2):
                        take(yl[:, a], d["yl_t"][a, :, toks], yl_in)
                    if tq + 1 < QUARTERS:
                        pool.wait_ge(yl_in, 32 * (tq + 1))
                        toks = slice((tq + 1) * Q, (tq + 2) * Q)
                        for a in range(2):
                            take(h[:, (tq + 1) % 2, a], d["h_t"][a, :, toks], h_in[(tq + 1) % 2])

            @block.tensor
            def _(pe):
                def group(out, b, p, k0, count, act):
                    for k in range(count):
                        last = matmul3(nc, out[:, :], w_hi[:, b, p, k0 + k, :], w_lo[:, b, p, k0 + k, :],
                                       act[:, 0, k, :], act[:, 1, k, :], k == 0, k == count - 1)
                    return last

                def enter(tq):
                    if tq == 0:
                        pe.wait_ge(first_h_in, 32)
                    else:
                        pe.wait_ge(h_in[tq % 2], 32 * ((tq + 1) // 2))

                def body(n, tq, blk, b):
                    split = lambda p: pe.wait_ge(w_split, PIECES * n + p + 3)
                    split(GA)
                    pe.wait_ge(sig, 3 * n + 3)
                    group(ps["ga"], b, GA, 0, KT, h[:, tq % 2]).then_inc(gates_made, 1)
                    split(GB)
                    group(ps["gb"], b, GB, 0, KT, h[:, tq % 2]).then_inc(gates_made, 1)
                    split(Z)
                    pe.wait_ge(ys_in, 32 * (tq + 1))
                    pe.wait_ge(mixed, n + 1)
                    group(ps["z2"], b, Z, KS, KS, ys)
                    group(ps["z1"], b, Z, 0, KS, ys).then_inc(made_z, 1)
                    split(YB)
                    pe.wait_ge(yl_in, 32 * (tq + 1))
                    group(ps["yb"], b, YB, 0, KT, yl).then_inc(made_yb, 1)

                units(pe, body, enter)

            @block.scalar
            def _(act):
                act.sem_inc(sig, 3)

                def body(n, tq, blk, b):
                    act.wait_ge(gates_made, 2 * n + 1)
                    act.wait_ge(mixed, n + 1)
                    nc.scalar.activation(ga[:, :], ps["ga"][:, :], ACT.Sigmoid).then_inc(sig, 1)
                    act.wait_ge(gates_made, 2 * n + 2)
                    nc.scalar.activation(gb[:, :], ps["gb"][:, :], ACT.Sigmoid).then_inc(sig, 1)
                    act.wait_ge(made_z, n + 1)
                    nc.scalar.activation(gz[:, :], ps["z2"][:, :], ACT.Sigmoid).then_inc(sig, 1)
                    act.wait_ge(mixed, n + 2)
                    for a, m in enumerate((m_hi, m_lo)):
                        act.dma_start(d["mix_t"][a, bass.ds(blk * P, P), tq * Q:(tq + 1) * Q], m[:, :].bitcast(F32)).then_inc(sent, 16)

                units(act, body)
                act.wait_ge(sent, 32 * UNITS + 32)

            @block.vector
            def _(dve):
                tt_ = nc.vector.tensor_tensor
                dve.sem_inc(mixed, 1)
                dve.sem_inc(w_split, 2)
                dve.sem_inc(sent, 32)

                def split(n, b, turn):
                    for p in range(PIECES):
                        dve.wait_ge(raw_in[p % 2], (48 * turn + (16, 16, 48, 32)[p]) if p % 2 == 0 else 32 * turn + (0, 16, 0, 32)[p])
                        nc.vector.tensor_copy(w_hi[:, b, p], raw[:, p % 2]).then_inc(high, 1)
                        dve.wait_ge(high, PIECES * n + p + 1)
                        tt_(w_lo[:, b, p], raw[:, p % 2], w_hi[:, b, p].bitcast(F32), ALU.subtract).then_inc(w_split, 1)

                def mix(n):
                    step = Chain(dve, steps, STEPS * n)
                    dve.wait_ge(sig, 3 * n + 6)
                    step(tt_(gz[:, :], gz[:, :], ps["z1"][:, :], ALU.mult))
                    step(tt_(ga[:, :], ga[:, :], gz[:, :], ALU.mult))
                    dve.wait_ge(made_yb, n + 1)
                    step(tt_(gb[:, :], gb[:, :], ps["yb"][:, :], ALU.mult))
                    step(tt_(ga[:, :], ga[:, :], gb[:, :], ALU.add))
                    dve.wait_ge(sent, 32 * n + 32)
                    step(nc.vector.tensor_copy(m_hi[:, :], ga[:, :]))
                    tt_(m_lo[:, :], ga[:, :], m_hi[:, :].bitcast(F32), ALU.subtract).then_inc(mixed, 1)

                split(0, 0, 0)
                with dve.Fori(0, UNITS // 2 - 1) as i:
                    for b in range(2):
                        split(2 * i + b + 1, 1 - b, 2 * i + b + 1)
                        mix(2 * i + b)
                split(UNITS - 1, 1, UNITS - 1)
                mix(UNITS - 2)
                mix(UNITS - 1)


def project_and_route(nc, d, keep):
    with ExitStack() as cx:
        sb = lambda n, s, t=F32: cx.enter_context(nc.sbuf_tensor("p6_" + n, s, t))
        sem = lambda n: cx.enter_context(nc.semaphore("p6_" + n))
        NR = N_GROUPS + N_EXPERTS
        ident = keep["ident"]
        raw = sb("raw", [P, KT, D_MODEL])
        w_hi = sb("w_hi", [P, KT, D_MODEL], F32R)
        w_lo = sb("w_lo", [P, KT, D_MODEL], F32R)
        mix = sb("mix", [P, 2, 2, KT, P], F32R)
        xt = sb("xt", [P, 2, D_MODEL])
        h2 = sb("h2", [P, 2, D_MODEL])
        sq = sb("sq", [P, 2, D_MODEL])
        gain = sb("gain", [P, D_MODEL])
        ht = sb("ht", [P, KT, P])
        wr = sb("wr", [P, KT, NR])
        br = sb("br", [P, NR])
        sst = sb("sst", [P, 2, 3])
        cst = sb("cst", [P, 2])
        ps_o = cx.enter_context(nc.psum_tensor("p6_ps_o", [P, 2, D_MODEL], F32))
        ps_t = cx.enter_context(nc.psum_tensor("p6_ps_t", [P, KT, P], F32))
        ps_l = cx.enter_context(nc.psum_tensor("p6_ps_l", [P, 512], F32))
        (w_split, high, small_in, pool_steps, made, x2_done, squared, rstd, normed, turned, ht_done, logits, taken) = (
            sem(n) for n in ("w_split", "high", "small_in", "pool_steps", "made", "x2_done", "squared", "rstd", "normed",
                             "turned", "ht_done", "logits", "taken"))
        x2_sent = [sem("x2_sent0"), sem("x2_sent1")]
        h2_sent = [sem("h2_sent0"), sem("h2_sent1")]
        w_in = [sem("w_in0"), sem("w_in1")]
        order = keep["order"]
        t_in = [sem("t_in0"), sem("t_in1")]
        last_tile = TOK_TILES - 1

        def tiles(eng, first, step):
            first(0, 0, 0)
            with eng.Fori(0, TOK_TILES // 2 - 1) as i:
                for b in (1, 0):
                    step(2 * i + 2 - b, b, i + 1 - b)
            step(last_tile, 1, TOK_TILES // 2 - 1)

        with nc.Block() as block:

            @block.sync
            def _(sp):
                for half in range(2):
                    ks = slice(half * KT // 2, (half + 1) * KT // 2)
                    sp.dma_start(raw[:, ks, :], d["w_o"][0].rearrange("(k p) n -> p k n", p=P)[:, ks, :]).then_inc(w_in[half], 16)
                sp.dma_start(gain[:, :], d["norm_ffn"][0:1, :].to_broadcast([P, D_MODEL])).then_inc(small_in, 16)
                with nc.allow_non_contiguous_dma(reason="the router's narrow weights"):
                    sp.dma_start(wr[:, :, 0:N_GROUPS], d["router_group_w"][0].rearrange("(k p) n -> p k n", p=P)).then_inc(small_in, 16)
                    sp.dma_start(wr[:, :, N_GROUPS:], d["router_expert_w"][0].rearrange("(k p) n -> p k n", p=P)).then_inc(small_in, 16)
                sp.dma_start(br[:, 0:N_GROUPS], d["router_group_b"][0:1, :].to_broadcast([P, N_GROUPS])).then_inc(small_in, 16)
                sp.dma_start(br[:, N_GROUPS:], d["router_expert_b"][0:1, :].to_broadcast([P, N_EXPERTS])).then_inc(small_in, 16)
                with sp.Fori(0, TOK_TILES // 2) as i:
                    for b in range(2):
                        t = 2 * i + b
                        sp.wait_ge(made, t + 1)
                        sp.sem_inc(order, 1)
                        for a in range(2):
                            sp.dma_start(mix[:, b, a].bitcast(F32), d["mix_t"][a, :, bass.ds(t * P, P)].rearrange("(k p) t -> p k t", p=P)).then_inc(t_in[b], 16)
                        sp.wait_ge(normed, t + 1)
                        sp.sem_inc(order, 1)
                        sp.wait_ge(x2_sent[b], 16 * i + 16)
                        sp.dma_start(xt[:, b, :], d["x"][0, bass.ds(t * P, P), :]).then_inc(t_in[b], 16)

            @block.tensor
            def _(pe):
                pe.sem_inc(made, 2)
                pe.sem_inc(turned, 1)
                pe.sem_inc(logits, 1)
                pe.wait_ge(small_in, 16 * 5)

                def head(t, b, turn):
                    pe.wait_ge(t_in[b], 48 * (turn + 1))
                    pe.wait_ge(x2_done, t + 1)
                    for half in range(2):
                        for k in range(KT):
                            if isinstance(t, int) and t == 0 and half == 0:
                                pe.wait_ge(w_split, k + 1)
                            cols = slice(half * 512, half * 512 + 512)
                            last = matmul3(nc, ps_o[:, b, cols], mix[:, b, 0, k, :], mix[:, b, 1, k, :], w_hi[:, k, cols], w_lo[:, k, cols],
                                           k == 0, k == KT - 1)
                    last.then_inc(made, 1)

                def turn_h(t, b):
                    pe.wait_ge(normed, t + 3)
                    pe.wait_ge(ht_done, t + 1)
                    for k in range(KT):
                        last = nc.tensor.transpose(ps_t[:, k, :], h2[:, b, k * P:(k + 1) * P], ident[:, :])
                    last.then_inc(turned, 1)

                def route(t):
                    pe.wait_ge(ht_done, t + 2)
                    pe.wait_ge(taken, t + 1)
                    for k in range(KT):
                        last = nc.tensor.matmul(ps_l[:, 0:NR], ht[:, k, :], wr[:, k, :], start=(k == 0), stop=(k == KT - 1))
                    last.then_inc(logits, 1)

                head(0, 0, 0)
                head(1, 1, 0)
                turn_h(0, 0)
                with pe.Fori(0, TOK_TILES // 2 - 1) as i:
                    for b in (1, 0):
                        t = 2 * i + 2 - b
                        head(t + 1, 1 - b, i + 1)
                        route(t - 1)
                        turn_h(t, b)
                route(last_tile - 1)
                turn_h(last_tile, 1)
                route(last_tile)

            @block.scalar
            def _(act):
                for s in x2_sent + h2_sent:
                    act.sem_inc(s, 16)
                act.sem_inc(ht_done, 1)
                for k in range(KT):
                    act.wait_ge(w_in[2 * k // KT], 16)
                    nc.scalar.copy(w_hi[:, k, :], raw[:, k, :]).then_inc(high, 1)
                act.wait_ge(small_in, 16 * 5)

                def square(t, b, turn):
                    act.wait_ge(x2_done, t + 3)
                    act.dma_start(d["x2"][bass.ds(t * P, P), :], xt[:, b, :]).then_inc(x2_sent[b], 16)
                    act.wait_ge(rstd, t + 1)
                    nc.scalar.activation(sq[:, b, :], xt[:, b, :], ACT.Square, accum_out=sst[:, b, 0:1]).then_inc(squared, 1)

                def store_h(t, b):
                    act.wait_ge(normed, t + 3)
                    act.dma_start(d["h2"][bass.ds(t * P, P), :], h2[:, b, :]).then_inc(h2_sent[b], 16)

                def take_turned(t):
                    act.wait_ge(turned, t + 2)
                    act.wait_ge(logits, t + 1)
                    nc.scalar.copy(ht[:, :, :], ps_t[:, :, :]).then_inc(ht_done, 1)

                def first(t, b, turn):
                    square(t, b, turn)
                    store_h(t, b)

                def step(t, b, turn):
                    square(t, b, turn)
                    take_turned(t - 1)
                    store_h(t, b)

                tiles(act, first, step)
                take_turned(last_tile)
                for s in x2_sent + h2_sent:
                    act.wait_ge(s, 16 * (TOK_TILES // 2 + 1))

            @block.gpsimd
            def _(pool):
                pool.sem_inc(rstd, 2)
                nc.gpsimd.memset(cst[:, 0:1], -0.5).then_inc(pool_steps, 1)
                nc.gpsimd.memset(cst[:, 1:2], RMS_EPS * D_MODEL).then_inc(pool_steps, 1)
                pool.wait_ge(pool_steps, 2)

                def head(t, b, turn):
                    pool.wait_ge(squared, t + 1)
                    nc.gpsimd.tensor_tensor(sst[:, b, 1:2], sst[:, b, 0:1], cst[:, 1:2], ALU.add).then_inc(pool_steps, 1)
                    pool.wait_ge(pool_steps, t + 3)
                    pool.wait_ge(normed, t + 1)
                    nc.gpsimd.tensor_tensor(sst[:, b, 2:3], sst[:, b, 1:2], cst[:, 0:1], ALU.pow).then_inc(rstd, 1)

                tiles(pool, head, head)

            @block.vector
            def _(dve):
                tt_, stt_ = nc.vector.tensor_tensor, nc.vector.scalar_tensor_tensor
                dve.sem_inc(x2_done, 2)
                dve.sem_inc(normed, 2)
                dve.sem_inc(taken, 1)
                for k in range(KT):
                    dve.wait_ge(high, k + 1)
                    tt_(w_lo[:, k, :], raw[:, k, :], w_hi[:, k, :].bitcast(F32), ALU.subtract).then_inc(w_split, 1)
                dve.wait_ge(small_in, 16 * 5)
                nc.vector.tensor_scalar(gain[:, :], gain[:, :], math.sqrt(D_MODEL), None, ALU.mult).then_inc(high, 1)
                dve.wait_ge(high, KT + 1)

                def head(t, b, turn):
                    dve.wait_ge(made, t + 3)
                    tt_(xt[:, b, :], ps_o[:, b, :], xt[:, b, :], ALU.add).then_inc(x2_done, 1)

                    dve.wait_ge(rstd, t + 3)
                    dve.wait_ge(turned, t + 1)
                    dve.wait_ge(h2_sent[b], 16 * turn + 16)
                    stt_(h2[:, b, :], xt[:, b, :], sst[:, b, 2:3], gain[:, :], ALU.mult, ALU.mult).then_inc(normed, 1)

                def take(t):
                    dve.wait_ge(logits, t + 2)
                    tt_(keep["logits"][:, bass.ds(t, 1), :].rearrange("p a n -> p (a n)"), ps_l[:, 0:NR], br[:, :], ALU.add).then_inc(taken, 1)

                head(0, 0, 0)
                head(1, 1, 0)
                with dve.Fori(1, TOK_TILES // 2) as i:
                    for b in range(2):
                        head(2 * i + b, b, i)
                        take(2 * i + b - 2)
                take(last_tile - 1)
                take(last_tile)


def place_tokens(nc, d, keep, weights):
    with ExitStack() as cx:
        sb = lambda n, s, t=F32: cx.enter_context(nc.sbuf_tensor("q7_" + n, s, t))
        sem = lambda n: cx.enter_context(nc.semaphore("q7_" + n))
        E = N_EXPERTS
        G, J, T = N_GROUPS, EXPERTS_PER_GROUP, TOK_TILES
        ROUTE_STEPS = 25 + T
        SLOT_STEPS = ROUTE_STEPS + 2 + SEQ // P + 7
        top = sb("top", [P, T, 3])
        is_top = sb("is_top", [P, T, J])
        group = sb("group", [P, T, G])
        first = sb("first", [P, T, J])
        chosen = sb("chosen", [P, T, 2, E])
        second = sb("second", [P, T, J])
        order_key = sb("order_key", [P, T, J])
        key_top = sb("key_top", [P, T])
        own = sb("own", [P, T, G, J])
        el = sb("el", [P, T, J])
        low = sb("low", [P, T, G + 1])
        ex = sb("ex", [P, T, G + 1])
        ssum = sb("ssum", [P, T, 2])
        iota = sb("iota", [P, J])
        tri = sb("tri", [P, P])
        asum = sb("asum", [P, T, E])
        before = sb("before", [P, T + 1, E])
        rank = sb("rank", [P, T * 2])
        ones = sb("ones", [P, P])
        cnt = sb("cnt", [P, E])
        nt = sb("nt", [P, E])
        end = sb("end", [P, E])
        pad = sb("pad", [P, E])
        one = sb("one", [P, E])
        prod = sb("prod", [P, TOK_TILES * 2, E])
        slotf = sb("slotf", [P, TOK_TILES * 2])
        te = sb("te", [1, MAX_TILES, E - 1])
        turn = sb("turn", [1, E])
        tef = sb("tef", [1, MAX_TILES])
        tio = sb("tio", [1, MAX_TILES])
        tok = sb("tok", [P, TOK_TILES], I32)
        zero = sb("zero", [MAX_TILES, P], I32)
        ids = sb("ids", [MAX_TILES, P], I32)
        idf = sb("idf", [MAX_TILES, P])
        spare = sb("spare", [1, 1])
        ps_c = cx.enter_context(nc.psum_tensor("q7_ps_c", [P, 512], F32))
        ps_k = cx.enter_context(nc.psum_tensor("q7_ps_k", [P, T, E], F32))
        ps_i = cx.enter_context(nc.psum_tensor("q7_ps_i", [P, 512], F32))
        consts, exped, counted, steps, ids_moved, scattered, idf_done, turned = (sem(n) for n in (
            "consts", "exped", "counted", "steps", "ids_moved", "scattered", "idf_done", "turned"))
        with nc.Block() as block:

            @block.gpsimd
            def _(pool):
                nc.gpsimd.memset(ones[:, :], 1.0).then_inc(consts, 1)
                nc.gpsimd.memset(one[:, :], 1.0).then_inc(consts, 1)
                nc.gpsimd.memset(zero[:, :], 0).then_inc(consts, 1)
                nc.gpsimd.iota(tio[:, :], pattern=[[1, MAX_TILES]], base=0, channel_multiplier=0,
                               allow_small_or_imprecise_dtypes=True).then_inc(consts, 1)
                nc.gpsimd.iota(tok[:, :], pattern=[[P, TOK_TILES]], base=0, channel_multiplier=1).then_inc(consts, 1)
                nc.gpsimd.memset(turn[:, :], 1.0).then_inc(consts, 1)
                nc.gpsimd.iota(iota[:, :], pattern=[[1, J]], base=0, channel_multiplier=0,
                               allow_small_or_imprecise_dtypes=True).then_inc(consts, 1)
                nc.gpsimd.memset(before[:, 0, :], 0.0).then_inc(consts, 1)
                pool.wait_ge(consts, 8)
                nc.gpsimd.memset(turn[:, W_SLOTS - 1::W_SLOTS], 1.0 - W_SLOTS).then_inc(consts, 1)
                nc.gpsimd.affine_select(out=tri[:, :], in_=ones[:, :], compare_op=ALU.is_gt, fill=0.0,
                                        base=0, pattern=[[1, P]], channel_multiplier=-1).then_inc(consts, 1)
                pool.wait_ge(consts, 10)
                pool.wait_ge(ids_moved, 16)
                pool.wait_ge(steps, SLOT_STEPS)
                for t in range(TOK_TILES):
                    for k in range(2):
                        nc.gpsimd.indirect_dma_start(out=d["slot_tok"], out_offset=bass.IndirectOffsetOnAxis(ap=keep["slot"][:, t, k:k + 1], axis=0),
                                                     in_=tok[:, t:t + 1], in_offset=None).then_inc(scattered, 16)

            @block.sync
            def _(sp):
                weights.load_first(sp, d)
                sp.wait_ge(consts, 10)
                sp.dma_start(d["slot_tok"].rearrange("(t p) o -> t (p o)", p=P), zero[:, :]).then_inc(ids_moved, 16)
                sp.wait_ge(scattered, 16 * 2 * TOK_TILES)
                sp.dma_start(ids[:, :], d["slot_tok"].rearrange("(t p) o -> t (p o)", p=P)).then_inc(ids_moved, 16)

            @block.tensor
            def _(pe):
                pe.wait_ge(consts, 10)
                pe.wait_ge(steps, ROUTE_STEPS)
                nc.tensor.matmul(ps_c[:, 0:E], ones[:, :], before[:, T, :], start=True, stop=True).then_inc(counted, 1)
                nc.tensor.matmul(ps_k[:, :, :], tri[:, :], asum[:, :, :], start=True, stop=False)
                nc.tensor.matmul(ps_k[:, :, :], ones[:, :], before[:, 0:T, :], start=False, stop=True).then_inc(counted, 1)
                pe.wait_ge(idf_done, 3)
                nc.tensor.transpose(ps_i[:, 0:MAX_TILES], idf[:, :], keep["ident"][0:MAX_TILES, 0:MAX_TILES]).then_inc(turned, 1)

            @block.scalar
            def _(act):
                act.wait_ge(steps, 18)
                nc.scalar.activation(ex[:, :, :], low[:, :, :], ACT.Exp).then_inc(exped, 1)

            @block.vector
            def _(dve):
                ts_, tt_, stt_ = nc.vector.tensor_scalar, nc.vector.tensor_tensor, nc.vector.scalar_tensor_tensor
                step = Chain(dve, steps)
                logits = keep["logits"]
                across = lambda v, n: v.unsqueeze(2).to_broadcast([P, T, n])

                def largest(values, n, slot, one_hot):
                    step(nc.vector.tensor_reduce(top[:, :, slot], values, AX.X, ALU.max))
                    step(tt_(is_top[:, :, 0:n], values, across(top[:, :, slot], n), ALU.is_equal))
                    step(stt_(order_key[:, :, 0:n], is_top[:, :, 0:n], float(J), iota[:, 0:n].unsqueeze(1).to_broadcast([P, T, n]), ALU.mult, ALU.subtract))
                    step(nc.vector.tensor_reduce(key_top[:, :], order_key[:, :, 0:n], AX.X, ALU.max))
                    step(tt_(one_hot, order_key[:, :, 0:n], across(key_top[:, :], n), ALU.is_equal))

                dve.wait_ge(consts, 10)
                largest(logits[:, :, 0:G], G, 0, group[:, :, :])
                step(tt_(own[:, :, :, :], logits[:, :, G:].rearrange("p t (g j) -> p t g j", g=G),
                         group[:, :, :].unsqueeze(3).to_broadcast([P, T, G, J]), ALU.mult))
                step(nc.vector.tensor_reduce(el[:, :, :], own[:, :, :, :].rearrange("p t g j -> p t j g"), AX.X, ALU.add))
                step(tt_(low[:, :, 0:G], logits[:, :, 0:G], across(top[:, :, 0], G), ALU.subtract))
                largest(el[:, :, :], J, 1, first[:, :, :])
                step(stt_(second[:, :, :], first[:, :, :], -3.0e38, el[:, :, :], ALU.mult, ALU.add))
                step(nc.vector.tensor_reduce(top[:, :, 2], second[:, :, :], AX.X, ALU.max))
                step(tt_(is_top[:, :, :], second[:, :, :], across(top[:, :, 2], J), ALU.is_equal))
                step(tt_(low[:, :, G], top[:, :, 2], top[:, :, 1], ALU.subtract))
                step(tt_(is_top[:, :, :], is_top[:, :, :], first[:, :, :], ALU.subtract))
                assert step.n == 18, step.n
                step(stt_(order_key[:, :, :], is_top[:, :, :], float(J), iota[:, :].unsqueeze(1).to_broadcast([P, T, J]), ALU.mult, ALU.subtract))
                step(nc.vector.tensor_reduce(key_top[:, :], order_key[:, :, :], AX.X, ALU.max))
                step(tt_(second[:, :, :], order_key[:, :, :], across(key_top[:, :], J), ALU.is_equal))
                for k, one_hot in enumerate((first, second)):
                    step(tt_(chosen[:, :, k, :].rearrange("p t (g j) -> p t g j", g=G), group[:, :, :].unsqueeze(3).to_broadcast([P, T, G, J]),
                             one_hot[:, :, :].unsqueeze(2).to_broadcast([P, T, G, J]), ALU.mult))
                step(tt_(asum[:, :, :], chosen[:, :, 0, :], chosen[:, :, 1, :], ALU.add))
                for t in range(T):
                    step(tt_(before[:, t + 1, :], before[:, t, :], asum[:, t, :], ALU.add))
                dve.wait_ge(exped, 1)
                step(nc.vector.tensor_reduce(ssum[:, :, 0], ex[:, :, 0:G], AX.X, ALU.add))
                assert step.n == ROUTE_STEPS, step.n
                nc.vector.memset(keep["ids"][:, MAX_TILES:], 0).then_inc(idf_done, 1)
                dve.wait_ge(counted, 1)
                step(nc.vector.tensor_copy(cnt[:, :], ps_c[:, 0:E]))
                step(ts_(nt[:, :], cnt[:, :], float(P), 1.0, ALU.is_gt, ALU.add))
                for m in range(2, SEQ // P):
                    step(stt_(nt[:, :], cnt[:, :], float(m * P), nt[:, :], ALU.is_gt, ALU.add))
                step(nc.vector.tensor_tensor_scan(end[:, :], one[:, :], nt[:, :], 0.0, ALU.mult, ALU.add))
                step(tt_(pad[:, :], end[:, :], nt[:, :], ALU.subtract))
                step(ts_(pad[:, :], pad[:, :], float(P), None, ALU.mult))
                dve.wait_ge(counted, 2)
                step(tt_(prod[:, :, :].rearrange("p (t k) e -> p t k e", k=2), chosen[:, :, :, :],
                         ps_k[:, :, :].unsqueeze(2).to_broadcast([P, T, 2, E]), ALU.mult))
                step(nc.vector.tensor_reduce(rank[:, :], prod[:, :, :], AX.X, ALU.add))
                step(tt_(prod[:, :, :], chosen[:, :, :, :].rearrange("p t k e -> p (t k) e"), pad[:, :].unsqueeze(1).to_broadcast([P, 2 * TOK_TILES, E]), ALU.mult))
                step(nc.vector.tensor_reduce(slotf[:, :], prod[:, :, :], AX.X, ALU.add))
                step(tt_(slotf[:, :], slotf[:, :], rank[:, :], ALU.add))
                step(nc.vector.tensor_copy(keep["slot"][:, :, :].rearrange("p t k -> p (t k)"), slotf[:, :]))
                assert step.n == SLOT_STEPS, step.n
                step(stt_(ssum[:, :, 1], ex[:, :, G], 1.0, ssum[:, :, 0], ALU.add, ALU.mult))
                step(nc.vector.reciprocal(keep["gates"][:, :, 0], ssum[:, :, 1]))
                step(tt_(keep["gates"][:, :, 1], keep["gates"][:, :, 0], ex[:, :, G], ALU.mult))
                shp = [1, MAX_TILES, E - 1]
                step(tt_(te[:, :, :], end[0:1, 0:E - 1].unsqueeze(1).to_broadcast(shp), tio[:, :].unsqueeze(2).to_broadcast(shp), ALU.is_le))
                step(nc.vector.tensor_reduce(tef[:, :], te[:, :, :], AX.X, ALU.add))
                step(nc.vector.tensor_copy(keep["tile_expert"][:, 0, :], tef[:, :]))
                step(tt_(te[:, :, :], te[:, :, :], turn[:, 0:E - 1].unsqueeze(1).to_broadcast(shp), ALU.mult))
                step(nc.vector.tensor_reduce(tef[:, :], te[:, :, :], AX.X, ALU.add))
                step(nc.vector.tensor_copy(keep["tile_expert"][:, 1, :], tef[:, :]))
                nc.vector.memset(keep["tile_end"][:, 0:1], 0).then_inc(idf_done, 1)
                step(nc.vector.tensor_copy(keep["tile_end"][:, 1:E + 1], end[0:1, :]))
                step(ts_(spare[:, :], end[0:1, E - 1:E], -1.0, MAX_TILES + 1.0, ALU.mult, ALU.add))
                step(nc.vector.tensor_copy(keep["tile_end"][:, E + 1:E + 2], spare[:, :]))
                dve.wait_ge(ids_moved, 32)
                nc.vector.tensor_copy(idf[:, :], ids[:, :]).then_inc(idf_done, 1)
                dve.wait_ge(turned, 1)
                nc.vector.tensor_copy(keep["ids"][:, 0:MAX_TILES], ps_i[:, 0:MAX_TILES]).then_inc(idf_done, 1)


PART = KT * D_EXPERT
W_EXPERT = 2 * PART
GATE, UP, DOWN = range(3)
EXPERT_PARTS = (("expert_w_gate", KT), ("expert_w_up", KT), ("expert_w_down", D_EXPERT // P))


class ExpertWeights:

    def __init__(self, nc, cx):
        sb = lambda n, size, t: cx.enter_context(nc.sbuf_tensor("w8_" + n, [P, size], t))
        sem = lambda n: cx.enter_context(nc.semaphore("w8_" + n))
        with nc.sbuf_tensor("w8_in_raw", [P, W_SLOTS * W_EXPERT], F32) as in_raw:
            pass
        in_lo, in_hi = (sb(n, W_SLOTS * W_EXPERT, F32R) for n in ("in_lo", "in_hi"))
        with nc.sbuf_tensor("w8_down_raw", [P, PART], F32) as down_raw:
            pass
        down_lo, down_hi = (sb(n, PART, F32R) for n in ("down_lo", "down_hi"))
        self.tensors = in_raw, in_lo, in_hi, down_raw, down_lo, down_hi
        self.in_landed = [[sem(f"in_landed{j}{q}") for q in range(2)] for j in range(W_SLOTS)]
        self.down_landed = sem("down_landed")

    def load(self, sp, d, e, q, raw, at_, landed):
        name, k = EXPERT_PARTS[q]
        sp.dma_start(raw[:, at_:at_ + PART].rearrange("p (k n) -> p k n", k=k),
                     d[name][0, bass.ds(e, 1), :, :].rearrange("a (k p) n -> p (a k) n", p=P)).then_inc(landed, 16)

    def load_first(self, sp, d):
        in_raw, down_raw = self.tensors[0], self.tensors[3]
        for e in range(W_SLOTS):
            for q in (GATE, UP):
                self.load(sp, d, e, q, in_raw, e * W_EXPERT + q * PART, self.in_landed[e][q])
        self.load(sp, d, 0, DOWN, down_raw, 0, self.down_landed)


def run_experts(nc, d, keep, weights):
    with ExitStack() as cx:
        sb = lambda n, s, t=F32: cx.enter_context(nc.sbuf_tensor("e8_" + n, s, t))
        sem = lambda n: cx.enter_context(nc.semaphore("e8_" + n))
        ident, ids, order = keep["ident"], keep["ids"], keep["order"]
        FK, W, HALF = D_EXPERT // P, W_EXPERT, PART // 2
        ZEROS = 256
        in_raw, in_lo, in_hi, down_raw, down_lo, down_hi = weights.tensors
        raw_in, down_in = weights.in_landed, weights.down_landed
        idc = sb("idc", [P, 1], U32)
        xg = sb("xg", [P, D_MODEL])
        xt_hi = sb("xt_hi", [P, KT, P], F32R)
        xt_lo = sb("xt_lo", [P, KT, P], F32R)
        s = sb("s", [P, D_EXPERT])
        a = sb("a", [P, D_EXPERT])
        at_hi = sb("at_hi", [P, FK, P], F32R)
        at_lo = sb("at_lo", [P, FK, P], F32R)
        y = sb("y", [P, D_MODEL])
        zero = sb("zero", [P, ZEROS])
        ps_t = cx.enter_context(nc.psum_tensor("e8_ps_t", [P, KT, P], F32))
        ps_g = cx.enter_context(nc.psum_tensor("e8_ps_g", [P, D_EXPERT], F32))
        ps_u = cx.enter_context(nc.psum_tensor("e8_ps_u", [P, D_EXPERT], F32))
        ps_a = cx.enter_context(nc.psum_tensor("e8_ps_a", [P, FK, P], F32))
        ps_y = cx.enter_context(nc.psum_tensor("e8_ps_y", [P, D_MODEL], F32))
        (in_hi_split, in_lo_split, down_hi_split, down_lo_split, idc_done, x_in, turned, x_hi, x_lo, g_made, u_made, silu_done, a_done, a_turned, a_hi, a_lo, y_made, y_out,
         y_sent, filled) = (sem(n) for n in (
            "in_hi_split", "in_lo_split", "down_hi_split", "down_lo_split", "idc_done", "x_in", "turned", "x_hi", "x_lo", "g_made", "u_made", "silu_done", "a_done", "a_turned",
            "a_hi", "a_lo", "y_made", "y_out", "y_sent", "filled"))
        end_of = lambda eng, e: eng.value_load(keep["tile_end"][0:1, bass.ds(e + 1, 1)], min_val=1, max_val=MAX_TILES - 1)
        tiles = lambda eng: end_of(eng, N_EXPERTS - 1)

        def experts(eng, tile):
            def rest(e):
                start = end_of(eng, e - 1) + 1 if not isinstance(e, int) or e else 1
                end = end_of(eng, e)
                with eng.If(start < end):
                    with eng.Fori(start, end) as t:
                        tile(t, None, None, None)

            def first(e, j, last=False):
                start = end_of(eng, e - 1)
                tile(start, e, None if last else e + 1, 1 - j)

            tile(0, 0, 1, 1)
            rest(0)
            with eng.Fori(0, N_EXPERTS // 2 - 1) as i:
                for j in (1, 0):
                    e = 2 * i + 2 - j
                    first(e, j)
                    rest(e)
            first(N_EXPERTS - 1, 1, last=True)
            rest(N_EXPERTS - 1)

        with nc.Block() as block:

            @block.sync
            def _(sp):
                load = lambda *what: weights.load(sp, d, *what)

                def next_loads(e, j):
                    end = end_of(sp, e - 2)
                    for q, used in ((GATE, g_made), (UP, u_made)):
                        sp.wait_ge(used, end)
                        sp.sem_inc(order, 1)
                        load(e, q, in_raw, j * W + q * PART, raw_in[j][q])
                    sp.wait_ge(y_made, end)
                    sp.sem_inc(order, 1)
                    load(e - 1, DOWN, down_raw, 0, down_in)

                for e in (2, 3):
                    next_loads(e, e % 2)
                used = tiles(sp)
                sp.wait_ge(idc_done, 1)
                with sp.Fori(used, MAX_TILES + 1) as t:
                    sp.dma_start(d["y_slots"][bass.ds(t * P, P), :].rearrange("p (a d) -> p a d", d=ZEROS),
                                 zero[:, :].unsqueeze(1).to_broadcast([P, D_MODEL // ZEROS, ZEROS])).then_inc(filled, 16)
                with sp.Fori(2, N_EXPERTS // 2) as i:
                    for j in range(2):
                        next_loads(2 * i + j, j)
                sp.wait_ge(y_made, end_of(sp, N_EXPERTS - 2))
                sp.sem_inc(order, 1)
                load(N_EXPERTS - 1, DOWN, down_raw, 0, down_in)
                spare = sp.value_load(keep["tile_end"][0:1, N_EXPERTS + 1:N_EXPERTS + 2], min_val=1, max_val=MAX_TILES)
                sp.wait_ge(filled, 16 * spare)
                sp.sem_inc(order, 1)

            @block.gpsimd
            def _(pool):
                nc.gpsimd.memset(zero[:, :], 0.0).then_inc(idc_done, 1)

                def gather(t):
                    if not isinstance(t, int) or t > 0:
                        pool.wait_ge(turned, t + 1)
                    pool.sem_inc(order, 1)
                    nc.gpsimd.tensor_copy(idc[:, :], ids[:, bass.ds(t, 1)]).then_inc(idc_done, 1)
                    pool.wait_ge(idc_done, t + 2)
                    pool.sem_inc(order, 1)
                    nc.gpsimd.indirect_dma_start(out=xg[:, :], out_offset=None, in_=d["h2"],
                                                 in_offset=bass.IndirectOffsetOnAxis(ap=idc[:, :], axis=0)).then_inc(x_in, 16)

                gather(0)
                gather(1)
                with pool.Fori(0, tiles(pool)) as t:
                    gather(t + 2)

            @block.tensor
            def _(pe):
                pe.sem_inc(turned, 1)

                def turn_x(t):
                    pe.wait_ge(x_in, 16 * t + 16)
                    pe.wait_ge(x_lo, t + 1)
                    for k in range(KT):
                        last = nc.tensor.transpose(ps_t[:, k, :], xg[:, k * P:(k + 1) * P], ident[:, :])
                    last.then_inc(turned, 1)

                def slot_of(t):
                    return pe.value_load(keep["tile_expert"][0:1, 1, bass.ds(t, 1)], min_val=0, max_val=W_SLOTS - 1)

                def expert_of(t):
                    return pe.value_load(keep["tile_expert"][0:1, 0, bass.ds(t, 1)], min_val=0, max_val=N_EXPERTS - 1)

                def gate_or_up(t, expert, slot, ps, q):
                    for k in range(KT):
                        if k % (KT // 2) == 0:
                            pe.wait_ge(in_lo_split, 4 * expert + (2 * q + 1 + k // (KT // 2)))
                        part = lambda w: w[:, bass.ds(slot * W + (q * PART + k * D_EXPERT), D_EXPERT)]
                        last = matmul3(nc, ps[:, :], xt_hi[:, k, :], xt_lo[:, k, :], part(in_hi), part(in_lo), k == 0, k == KT - 1)
                    return last

                def gate(t, expert, slot):
                    pe.wait_ge(x_lo, t + 2)
                    pe.wait_ge(silu_done, t + 1)
                    gate_or_up(t, expert, slot, ps_g, GATE).then_inc(g_made, 1)

                def up(t, expert, slot):
                    pe.wait_ge(a_done, t + 1)
                    gate_or_up(t, expert, slot, ps_u, UP).then_inc(u_made, 1)

                def turn_a(t):
                    pe.wait_ge(a_done, t + 2)
                    pe.wait_ge(a_lo, t + 1)
                    for k in range(FK):
                        last = nc.tensor.transpose(ps_a[:, k, :], a[:, k * P:(k + 1) * P], ident[:, :])
                    last.then_inc(a_turned, 1)

                def down(t, expert):
                    pe.wait_ge(a_lo, t + 2)
                    pe.wait_ge(y_out, t + 1)
                    for k in range(FK):
                        if k % (FK // 2) == 0:
                            pe.wait_ge(down_lo_split, 2 * expert + (1 + k // (FK // 2)))
                        for half in range(2):
                            cols = slice(half * 512, half * 512 + 512)
                            at_ = k * D_MODEL + half * 512
                            last = matmul3(nc, ps_y[:, cols], at_hi[:, k, :], at_lo[:, k, :], down_hi[:, at_:at_ + 512], down_lo[:, at_:at_ + 512], k == 0, k == FK - 1)
                    last.then_inc(y_made, 1)

                turn_x(0)
                gate(0, 0, 0)
                up(0, 0, 0)
                turn_x(1)
                with pe.Fori(0, tiles(pe)) as t:
                    expert, slot = expert_of(t + 1), slot_of(t + 1)
                    gate(t + 1, expert, slot)
                    turn_a(t)
                    up(t + 1, expert, slot)
                    turn_x(t + 2)
                    down(t, expert_of(t))

            @block.scalar
            def _(act):
                act.sem_inc(silu_done, 1)
                act.sem_inc(y_out, 1)
                act.sem_inc(y_sent, 16)

                def split(raw, hi, at_, landed, count, done):
                    act.wait_ge(landed, count)
                    for half in range(2):
                        cols = slice(at_ + half * HALF, at_ + (half + 1) * HALF)
                        nc.scalar.copy(hi[:, cols], raw[:, cols]).then_inc(done, 1)

                def split_in(e, j, q):
                    if e is not None:
                        split(in_raw, in_hi, j * W + q * PART, raw_in[j][q], 8 * e + (16 - 8 * j), in_hi_split)

                def split_down(e):
                    if e is not None:
                        split(down_raw, down_hi, 0, down_in, 16 * e + 16, down_hi_split)

                def take_x(t):
                    act.wait_ge(turned, t + 2)
                    if not isinstance(t, int):
                        act.wait_ge(u_made, t)
                    nc.scalar.copy(xt_hi[:, :, :], ps_t[:, :, :]).then_inc(x_hi, 1)

                def silu(t):
                    act.wait_ge(g_made, t + 1)
                    act.wait_ge(a_done, t + 1)
                    nc.scalar.activation(s[:, :], ps_g[:, :], ACT.Silu).then_inc(silu_done, 1)

                def take_y(t):
                    act.wait_ge(y_made, t + 1)
                    act.wait_ge(y_sent, 16 * t + 16)
                    nc.scalar.copy(y[:, :], ps_y[:, :]).then_inc(y_out, 1)

                def store_y(t):
                    act.wait_ge(y_out, t + 2)
                    act.dma_start(d["y_slots"][bass.ds(t * P, P), :], y[:, :]).then_inc(y_sent, 16)

                split_in(0, 0, GATE)
                take_x(0)
                split_in(0, 0, UP)
                silu(0)

                def tile(t, own, e, j):
                    take_x(t + 1)
                    split_in(e, j, GATE)
                    if not isinstance(t, int):
                        take_y(t - 1)
                        store_y(t - 1)
                    split_in(e, j, UP)
                    silu(t + 1)
                    act.wait_ge(a_turned, t + 1)
                    nc.scalar.copy(at_hi[:, :, :], ps_a[:, :, :]).then_inc(a_hi, 1)
                    split_down(own)

                experts(act, tile)
                last = tiles(act)
                take_y(last - 1)
                store_y(last - 1)
                act.wait_ge(y_sent, 16 * last + 16)
                act.sem_inc(order, 1)

            @block.vector
            def _(dve):
                tt_ = nc.vector.tensor_tensor
                dve.sem_inc(x_lo, 1)
                dve.sem_inc(a_done, 1)
                dve.sem_inc(a_lo, 1)

                def split(raw, hi, lo, at_, split_hi, count, done):
                    for half in range(2):
                        cols = slice(at_ + half * HALF, at_ + (half + 1) * HALF)
                        dve.wait_ge(split_hi, count + (half + 1))
                        tt_(lo[:, cols], raw[:, cols], hi[:, cols].bitcast(F32), ALU.subtract).then_inc(done, 1)

                def split_in(e, j, q):
                    if e is not None:
                        split(in_raw, in_hi, in_lo, j * W + q * PART, in_hi_split, 4 * e + 2 * q, in_lo_split)

                def split_down(e):
                    if e is not None:
                        split(down_raw, down_hi, down_lo, 0, down_hi_split, 2 * e, down_lo_split)

                def take_x(t):
                    dve.wait_ge(x_hi, t + 1)
                    tt_(xt_lo[:, :, :], ps_t[:, :, :], xt_hi[:, :, :].bitcast(F32), ALU.subtract).then_inc(x_lo, 1)

                def product(t):
                    dve.wait_ge(silu_done, t + 2)
                    dve.wait_ge(u_made, t + 1)
                    if not isinstance(t, int) or t > 0:
                        dve.wait_ge(a_turned, t)
                    tt_(a[:, :], s[:, :], ps_u[:, :], ALU.mult).then_inc(a_done, 1)

                split_in(0, 0, GATE)
                take_x(0)
                split_in(0, 0, UP)
                product(0)

                def tile(t, own, e, j):
                    take_x(t + 1)
                    split_in(e, j, GATE)
                    split_in(e, j, UP)
                    dve.wait_ge(a_hi, t + 1)
                    tt_(at_lo[:, :, :], ps_a[:, :, :], at_hi[:, :, :].bitcast(F32), ALU.subtract).then_inc(a_lo, 1)
                    split_down(own)
                    product(t + 1)

                experts(dve, tile)


def combine_and_norm(nc, d, keep):
    with ExitStack() as cx:
        sb = lambda n, s, t=F32: cx.enter_context(nc.sbuf_tensor("f9_" + n, s, t))
        sem = lambda n: cx.enter_context(nc.semaphore("f9_" + n))
        xt = sb("xt", [P, 2, D_MODEL])
        yg = sb("yg", [P, 2, 2, D_MODEL])
        o = sb("o", [P, 2, D_MODEL])
        sq = sb("sq", [P, 2, D_MODEL])
        gain = sb("gain", [P, D_MODEL])
        slc = sb("slc", [P, 2, 2], U32)
        gc = sb("gc", [P, 2, 2])
        sst = sb("sst", [P, 2, 3])
        cst = sb("cst", [P, 2])
        small_in, pool_steps, steps, combined, squared, rstd, done = (sem(n) for n in (
            "small_in", "pool_steps", "steps", "combined", "squared", "rstd", "done"))
        x_in = [sem("x_in0"), sem("x_in1")]
        y_in = [sem("y_in0"), sem("y_in1")]
        sent = [sem("sent0"), sem("sent1")]
        last_tile = TOK_TILES - 1
        turns = TOK_TILES // 2
        order = keep["order"]
        STEPS = 2
        with nc.Block() as block:

            @block.sync
            def _(sp):
                sp.dma_start(gain[:, :], d["norm_final"].unsqueeze(0).to_broadcast([P, D_MODEL])).then_inc(small_in, 16)
                with sp.Fori(0, turns) as i:
                    for b in range(2):
                        t = 2 * i + b
                        sp.wait_ge(done, t + 1)
                        sp.dma_start(xt[:, b, :], d["x2"][bass.ds(t * P, P), :]).then_inc(x_in[b], 16)

            @block.gpsimd
            def _(pool):
                pool.sem_inc(rstd, 4)
                nc.gpsimd.memset(cst[:, 0:1], -0.5).then_inc(pool_steps, 1)
                nc.gpsimd.memset(cst[:, 1:2], RMS_EPS * D_MODEL).then_inc(pool_steps, 1)

                def gather(t, b, turn):
                    pool.wait_ge(combined, t + 1)
                    pool.sem_inc(order, 1)
                    nc.gpsimd.tensor_copy(slc[:, b, :], keep["slot"][:, bass.ds(t, 1), :].rearrange("p a k -> p (a k)")).then_inc(pool_steps, 1)
                    pool.wait_ge(pool_steps, t + 3)
                    pool.sem_inc(order, 1)
                    for k in range(2):
                        nc.gpsimd.indirect_dma_start(out=yg[:, b, k, :], out_offset=None, in_=d["y_slots"],
                                                     in_offset=bass.IndirectOffsetOnAxis(ap=slc[:, b, k:k + 1], axis=0)).then_inc(y_in[b], 16)

                def scale(t, b):
                    pool.wait_ge(squared, t + 1)
                    nc.gpsimd.tensor_tensor(sst[:, b, 1:2], sst[:, b, 0:1], cst[:, 1:2], ALU.add).then_inc(rstd, 1)
                    pool.wait_ge(rstd, 2 * t + 5)
                    pool.wait_ge(done, t + 1)
                    nc.gpsimd.tensor_tensor(sst[:, b, 2:3], sst[:, b, 1:2], cst[:, 0:1], ALU.pow).then_inc(rstd, 1)

                gather(0, 0, 0)
                gather(1, 1, 0)
                with pool.Fori(0, turns - 1) as i:
                    for b in range(2):
                        gather(2 * i + b + 2, b, i + 1)
                        scale(2 * i + b, b)
                scale(last_tile - 1, 0)
                scale(last_tile, 1)

            @block.scalar
            def _(act):
                for q in sent:
                    act.sem_inc(q, 16)

                def square(t, b):
                    act.wait_ge(combined, t + 3)
                    act.wait_ge(rstd, 2 * t + 2)
                    nc.scalar.activation(sq[:, b, :], xt[:, b, :], ACT.Square, accum_out=sst[:, b, 0:1]).then_inc(squared, 1)

                def store(t, b):
                    act.wait_ge(done, t + 3)
                    act.dma_start(d["out"][0, bass.ds(t * P, P), :], o[:, b, :]).then_inc(sent[b], 16)

                with act.Fori(0, turns) as i:
                    for b in range(2):
                        square(2 * i + b, b)
                        store(2 * i + b, b)
                for q in sent:
                    act.wait_ge(q, 16 * (turns + 1))

            @block.vector
            def _(dve):
                stt_ = nc.vector.scalar_tensor_tensor
                dve.sem_inc(done, 2)
                dve.sem_inc(combined, 2)
                dve.wait_ge(small_in, 16)
                nc.vector.tensor_scalar(gain[:, :], gain[:, :], math.sqrt(D_MODEL), None, ALU.mult).then_inc(steps, 1)

                def head(t, b, turn):
                    step = Chain(dve, steps, STEPS * t + 1)
                    step(nc.vector.tensor_copy(gc[:, b, :], keep["gates"][:, bass.ds(t, 1), :].rearrange("p a k -> p (a k)")))
                    dve.wait_ge(x_in[b], 16 * turn + 16)
                    dve.wait_ge(y_in[b], 32 * turn + 32)
                    step(stt_(xt[:, b, :], yg[:, b, 0, :], gc[:, b, 0:1], xt[:, b, :], ALU.mult, ALU.add))
                    stt_(xt[:, b, :], yg[:, b, 1, :], gc[:, b, 1:2], xt[:, b, :], ALU.mult, ALU.add).then_inc(combined, 1)

                def tail(t, b, turn):
                    dve.wait_ge(rstd, 2 * t + 6)
                    dve.wait_ge(sent[b], 16 * turn + 16)
                    stt_(o[:, b, :], xt[:, b, :], sst[:, b, 2:3], gain[:, :], ALU.mult, ALU.mult).then_inc(done, 1)

                with dve.Fori(0, turns) as i:
                    for b in range(2):
                        head(2 * i + b, b, i)
                        tail(2 * i + b, b, i)


def hybrid_block(nc, d):
    with ExitStack() as cx:
        sb = lambda n, s, t=F32: cx.enter_context(nc.sbuf_tensor(n, s, t))
        ident = sb("ident", [P, P])
        order = cx.enter_context(nc.semaphore("order"))
        s5_constants(nc, d, ident)
        with ExitStack() as hold:
            h_hi = hold.enter_context(nc.sbuf_tensor("h_hi", [P, KT, SEQ], F32R))
            h_lo = hold.enter_context(nc.sbuf_tensor("h_lo", [P, KT, SEQ], F32R))
            norm_and_turn(nc, d, ident, h_hi, h_lo)
            s5_inputs(nc, d, h_hi, h_lo)
            rg_lru(nc, d, h_hi, h_lo)
        with ExitStack() as hold:
            first_h = (hold.enter_context(nc.sbuf_tensor("first_h", [P, 2, 2, KT, QUARTER], F32R)),
                       hold.enter_context(nc.semaphore("first_h_in")))
            s5_scan(nc, d, ident, first_h)
            mix_branches(nc, d, order, first_h)
        keep = {
            "ident": ident,
            "order": order,
            "gates": sb("gates", [P, TOK_TILES, 2]),
            "slot": sb("slot", [P, TOK_TILES, 2], U32),
            "ids": sb("ids", [P, MAX_TILES + 2], U32),
            "tile_expert": sb("tile_expert", [1, 2, MAX_TILES], I32),
            "tile_end": sb("tile_end", [1, N_EXPERTS + 2], I32),
        }
        keep["logits"] = sb("logits", [P, TOK_TILES, N_GROUPS + N_EXPERTS])
        project_and_route(nc, d, keep)
        with ExitStack() as hold:
            weights = ExpertWeights(nc, hold)
            place_tokens(nc, d, keep, weights)
            run_experts(nc, d, keep, weights)
        combine_and_norm(nc, d, keep)


SCRATCH = {
    "s5_pack": ((CBS, P, PACK), F32),
    "h_t": ((2, D_MODEL, SEQ), F32),
    "u": ((CBS, P, CTS, CB_GROUPS * P), F32),
    "ys_t": ((2, S5_WIDTH, SEQ), F32),
    "yl_t": ((2, LRU_WIDTH, SEQ), F32),
    "mix_t": ((2, D_MODEL, SEQ), F32),
    "x2": ((SEQ, D_MODEL), F32),
    "h2": ((SEQ, D_MODEL), F32),
    "slot_tok": ((MAX_TILES * P, 1), I32),
    "y_slots": (((MAX_TILES + 1) * P, D_MODEL), F32),
}


def kernel(**inputs):
    import numpy as _np
    import concourse.bacc as _bacc
    from concourse import mybir as _mybir
    from concourse.bass_utils import run_bass_kernel_spmd as _run

    nc = _bacc.Bacc("TRN2", target_bir_lowering=False, num_devices=1)
    arrays, d = {}, {}
    for name in inputs:
        a = _np.ascontiguousarray(inputs[name])
        arrays[f"in_{name}_dram"] = a
        d[name] = nc.dram_tensor(f"in_{name}_dram", a.shape, _mybir.dt.from_np(a.dtype), kind="ExternalInput").ap()
    for name, (shape, dt) in SCRATCH.items():
        d[name] = nc.dram_tensor(name, shape, dt).ap()
    d["out"] = nc.dram_tensor("out_0_dram", (1, SEQ, D_MODEL), F32, kind="ExternalOutput").ap()
    hybrid_block(nc, d)
    r = _run(nc, [arrays], core_ids=[0])
    return r.results[0]["out_0_dram"]
```
